# Optimizing a Trainium2 kernel written in Bass

```python
import jax, jax.numpy as jnp
from jax import lax
import numpy as np

D_MODEL = 1024
BATCH = 1
SEQ = 512
DEPTH = 1

N_META = 16
CHUNK = 64
N_PAD = CHUNK - N_META
GLA_HEADS = 4
GLA_DK = 128
GLA_DV = 256
GLA_KEY = GLA_HEADS * GLA_DK
GLA_VAL = GLA_HEADS * GLA_DV
GATE_RANK = 16
GATE_TAU = 16.0
SSM_WIDTH = D_MODEL
SSM_GROUP = 16
SSM_GROUPS = SSM_WIDTH // SSM_GROUP
SSM_STATE = 64
D_FF = 4 * D_MODEL
EPS = 1e-6

Q_END = GLA_KEY
K_END = Q_END + GLA_KEY
V_END = K_END + GLA_VAL
R_END = V_END + GLA_VAL
A_END = R_END + GATE_RANK
U_END = A_END + SSM_WIDTH
G1_END = U_END + D_MODEL
IN_WIDTH = G1_END + D_MODEL


def rmsnorm(x, g):
    xf = x.astype(jnp.float32)
    ms = jnp.mean(xf * xf, axis=-1, keepdims=True)
    return (xf * lax.rsqrt(ms + EPS) * g.astype(jnp.float32)).astype(x.dtype)

def gla_chunked(q, k, v, log_a):
    bsz, p, h, dk = q.shape
    dv = v.shape[-1]
    nc = p // CHUNK

    def to_chunks(t):
        return t.reshape(bsz, nc, CHUNK, h, t.shape[-1]).transpose(1, 0, 3, 2, 4)

    qc, kc, vc = to_chunks(q), to_chunks(k), to_chunks(v)
    b = jnp.cumsum(to_chunks(log_a).astype(jnp.float32), axis=3)
    b_ref = b[:, :, :, CHUNK // 2:CHUNK // 2 + 1, :]
    q_in = qc * jnp.exp(b - b_ref)
    k_in = kc * jnp.exp(b_ref - b)
    mask = jnp.tril(jnp.ones((CHUNK, CHUNK), dtype=bool))
    scores = jnp.where(mask, jnp.einsum('nbhid,nbhjd->nbhij', q_in, k_in), 0.0)
    o_intra = jnp.einsum('nbhij,nbhjv->nbhiv', scores, vc.astype(jnp.float32))

    b_last = b[:, :, :, -1:, :]
    q_inter = qc * jnp.exp(b)
    k_state = kc * jnp.exp(b_last - b)
    decay_chunk = jnp.exp(b_last[:, :, :, 0, :])

    def step(state, inp):
        qi, ks, vv, dc = inp
        o = jnp.einsum('bhid,bhdv->bhiv', qi, state)
        new_state = dc[..., None] * state + jnp.einsum('bhjd,bhjv->bhdv', ks, vv.astype(jnp.float32))
        return new_state, o

    s0 = jnp.zeros((bsz, h, dk, dv), jnp.float32)
    _, o_inter = lax.scan(step, s0, (q_inter, k_state, vc, decay_chunk))
    o = (o_intra + o_inter).transpose(1, 0, 3, 2, 4).reshape(bsz, p, h, dv)
    return o.astype(v.dtype)

def _complex_combine(e1, e2):
    a1r, a1i, b1r, b1i = e1
    a2r, a2i, b2r, b2i = e2
    return (a2r * a1r - a2i * a1i,
            a2r * a1i + a2i * a1r,
            a2r * b1r - a2i * b1i + b2r,
            a2r * b1i + a2i * b1r + b2i)

def s5_ssm(u, a_re, a_im, log_step, b_re, b_im, c_re, c_im, d_skip):
    bsz, p, _ = u.shape
    g, n, hg = SSM_GROUPS, SSM_STATE, SSM_GROUP
    ar = a_re.astype(jnp.float32)
    ai = a_im.astype(jnp.float32)
    dt = jnp.exp(log_step.astype(jnp.float32))[:, None]
    mag = jnp.exp(ar * dt)
    lam_re, lam_im = mag * jnp.cos(ai * dt), mag * jnp.sin(ai * dt)
    zr, zi = lam_re - 1.0, lam_im
    den = ar * ar + ai * ai
    fr = (zr * ar + zi * ai) / den
    fi = (zi * ar - zr * ai) / den
    br, bi = b_re.astype(jnp.float32), b_im.astype(jnp.float32)
    bb_re = fr[..., None] * br - fi[..., None] * bi
    bb_im = fr[..., None] * bi + fi[..., None] * br
    cr, ci = c_re.astype(jnp.float32), c_im.astype(jnp.float32)

    nc = p // CHUNK
    uc = u.reshape(bsz, nc, CHUNK, g, hg).transpose(1, 0, 2, 3, 4)
    lam_b_re = jnp.broadcast_to(lam_re, (bsz, CHUNK, g, n))
    lam_b_im = jnp.broadcast_to(lam_im, (bsz, CHUNK, g, n))

    def step(carry, u_blk):
        h_re, h_im = carry
        uf = u_blk.astype(jnp.float32)
        bu_re = jnp.einsum('bcgh,gnh->bcgn', uf, bb_re)
        bu_im = jnp.einsum('bcgh,gnh->bcgn', uf, bb_im)
        acc_re, acc_im, x_re, x_im = lax.associative_scan(
            _complex_combine, (lam_b_re, lam_b_im, bu_re, bu_im), axis=1)
        s_re = x_re + acc_re * h_re[:, None] - acc_im * h_im[:, None]
        s_im = x_im + acc_re * h_im[:, None] + acc_im * h_re[:, None]
        y = jnp.einsum('bcgn,ghn->bcgh', s_re, cr) - jnp.einsum('bcgn,ghn->bcgh', s_im, ci)
        return (s_re[:, -1], s_im[:, -1]), y

    carry0 = (jnp.zeros((bsz, g, n), jnp.float32), jnp.zeros((bsz, g, n), jnp.float32))
    _, y = lax.scan(step, carry0, uc)
    y = y.transpose(1, 0, 2, 3, 4).reshape(bsz, p, g * hg)
    return (y + d_skip.astype(jnp.float32) * u.astype(jnp.float32)).astype(u.dtype)

def first_inputs(seed: int = 0) -> dict:
    key = jax.random.key(seed)
    ks = jax.random.split(key, 24)
    nrm = lambda k, shape, s: jax.random.normal(k, shape, jnp.float32) * s
    gain = lambda k, shape: 1.0 + 0.05 * jax.random.normal(k, shape, jnp.float32)
    L = DEPTH
    x = jax.random.normal(ks[0], (BATCH, SEQ, D_MODEL), jnp.float32)
    meta_tokens = nrm(ks[1], (N_META, D_MODEL), 1.0)
    g_mix_pre = gain(ks[2], (L, D_MODEL))
    w_in = nrm(ks[3], (L, D_MODEL, IN_WIDTH), D_MODEL ** -0.5)
    w_gate_up = nrm(ks[4], (L, GATE_RANK, GLA_KEY), GATE_RANK ** -0.5)
    b_gate = 1.0 + 0.5 * jax.random.normal(ks[5], (L, GLA_KEY), jnp.float32)
    gla_norm_g = gain(ks[6], (L, GLA_HEADS, GLA_DV))
    w_o_gla = nrm(ks[7], (L, GLA_VAL, D_MODEL), GLA_VAL ** -0.5)
    n_idx = jnp.arange(SSM_STATE, dtype=jnp.float32)
    a_re = -0.5 + 0.01 * jax.random.normal(ks[8], (L, SSM_GROUPS, SSM_STATE), jnp.float32)
    a_im = jnp.broadcast_to(jnp.pi * n_idx, (L, SSM_GROUPS, SSM_STATE)) + 0.0
    log_step = jax.random.uniform(ks[9], (L, SSM_GROUPS), jnp.float32,
                                  minval=float(np.log(1e-3)), maxval=float(np.log(1e-1)))
    b_re = nrm(ks[10], (L, SSM_GROUPS, SSM_STATE, SSM_GROUP), (2 * SSM_GROUP) ** -0.5)
    b_im = nrm(ks[11], (L, SSM_GROUPS, SSM_STATE, SSM_GROUP), (2 * SSM_GROUP) ** -0.5)
    c_re = nrm(ks[12], (L, SSM_GROUPS, SSM_GROUP, SSM_STATE), (2 * SSM_STATE) ** -0.5)
    c_im = nrm(ks[13], (L, SSM_GROUPS, SSM_GROUP, SSM_STATE), (2 * SSM_STATE) ** -0.5)
    d_skip = nrm(ks[14], (L, SSM_WIDTH), 1.0)
    w_glu = nrm(ks[15], (L, SSM_WIDTH, 2 * D_MODEL), SSM_WIDTH ** -0.5)
    b_glu = nrm(ks[16], (L, 2 * D_MODEL), 0.02)
    w_out = nrm(ks[17], (L, D_MODEL, D_MODEL), D_MODEL ** -0.5)
    g_mix_post = gain(ks[18], (L, D_MODEL))
    g_ffn_pre = gain(ks[19], (L, D_MODEL))
    w_ff1 = nrm(ks[20], (L, D_MODEL, D_FF), D_MODEL ** -0.5)
    w_ff2 = nrm(ks[21], (L, D_FF, D_MODEL), D_FF ** -0.5)
    g_ffn_post = gain(ks[22], (L, D_MODEL))
    return {"x": x, "meta_tokens": meta_tokens, "g_mix_pre": g_mix_pre, "w_in": w_in,
            "w_gate_up": w_gate_up, "b_gate": b_gate, "gla_norm_g": gla_norm_g, "w_o_gla": w_o_gla,
            "a_re": a_re, "a_im": a_im, "log_step": log_step, "b_re": b_re, "b_im": b_im,
            "c_re": c_re, "c_im": c_im, "d_skip": d_skip, "w_glu": w_glu, "b_glu": b_glu,
            "w_out": w_out, "g_mix_post": g_mix_post, "g_ffn_pre": g_ffn_pre, "w_ff1": w_ff1,
            "w_ff2": w_ff2, "g_ffn_post": g_ffn_post}

def first_block(x, meta_tokens, g_mix_pre, w_in, w_gate_up, b_gate, gla_norm_g, w_o_gla,
              a_re, a_im, log_step, b_re, b_im, c_re, c_im, d_skip, w_glu, b_glu,
              w_out, g_mix_post, g_ffn_pre, w_ff1, w_ff2, g_ffn_post):
    bsz, seq, dm = x.shape
    meta = jnp.broadcast_to(meta_tokens.astype(x.dtype)[None], (bsz, N_META, dm))
    h = jnp.concatenate([meta, x], axis=1)
    p = N_PAD + N_META + seq

    def pad(t):
        return jnp.pad(t, ((0, 0), (N_PAD, 0), (0, 0)))

    def heads(t, d):
        return t.reshape(bsz, p, GLA_HEADS, d)

    for l in range(DEPTH):
        xn = rmsnorm(h, g_mix_pre[l])
        proj = xn @ w_in[l]
        q = proj[..., :Q_END]
        k = proj[..., Q_END:K_END]
        v = proj[..., K_END:V_END]
        r = proj[..., V_END:R_END]
        a_low = proj[..., R_END:A_END]
        u = proj[..., A_END:U_END]
        z_gla = proj[..., U_END:G1_END]
        z_ssm = proj[..., G1_END:]

        log_a = jax.nn.log_sigmoid((a_low @ w_gate_up[l] + b_gate[l]).astype(jnp.float32)) / GATE_TAU
        o = gla_chunked(heads(pad(q), GLA_DK) * (GLA_DK ** -0.5), heads(pad(k), GLA_DK),
                        heads(pad(v), GLA_DV), heads(pad(log_a), GLA_DK))[:, N_PAD:]
        o = rmsnorm(o, gla_norm_g[l]).reshape(bsz, N_META + seq, GLA_VAL) * jax.nn.silu(r)
        y_gla = o @ w_o_gla[l]

        y_s = s5_ssm(pad(u), a_re[l], a_im[l], log_step[l], b_re[l], b_im[l],
                     c_re[l], c_im[l], d_skip[l])[:, N_PAD:]
        g_s = jax.nn.gelu(y_s)
        glu = g_s @ w_glu[l] + b_glu[l]
        y_ssm = glu[..., :D_MODEL] * jax.nn.sigmoid(glu[..., D_MODEL:])

        mixed = jax.nn.sigmoid(z_gla) * y_gla + jax.nn.sigmoid(z_ssm) * y_ssm
        h = h + rmsnorm(mixed @ w_out[l], g_mix_post[l])

        hn = rmsnorm(h, g_ffn_pre[l])
        f = jnp.square(jax.nn.relu(hn @ w_ff1[l])) @ w_ff2[l]
        h = h + rmsnorm(f, g_ffn_post[l])

    return h[:, N_META:]


N_HEADS = 8
QK_NOPE_DIM = 64
QK_ROPE_DIM = 32
V_HEAD_DIM = 64
Q_LORA_RANK = 384
KV_LORA_RANK = 256
ROPE_BASE = 10000.0
Q_BLOCK = 128
QK_DIM = QK_NOPE_DIM + QK_ROPE_DIM
ATTN_WIDTH = N_HEADS * V_HEAD_DIM
CONV_CHANNELS = 512
CONV_KERNEL = 31
N_GROUPS = 4
EXPERTS_PER_GROUP = 8
TOP_K_IN_GROUP = 2
D_EXPERT = 128
SPLIT_POINTS = tuple(int(v) for v in np.cumsum([Q_LORA_RANK, KV_LORA_RANK, QK_ROPE_DIM, 2 * CONV_CHANNELS]))
IN_COLS = Q_LORA_RANK + KV_LORA_RANK + QK_ROPE_DIM + 2 * CONV_CHANNELS + 2 * D_MODEL


def rmsnorm_2(x, g):
    xf = x.astype(jnp.float32)
    y = xf * lax.rsqrt(jnp.mean(xf * xf, axis=-1, keepdims=True) + EPS)
    return (y * g.astype(jnp.float32)).astype(x.dtype)

def layernorm(x, g, b):
    xf = x.astype(jnp.float32)
    mu = jnp.mean(xf, axis=-1, keepdims=True)
    var = jnp.mean(jnp.square(xf - mu), axis=-1, keepdims=True)
    y = (xf - mu) * lax.rsqrt(var + EPS)
    return (y * g.astype(jnp.float32) + b.astype(jnp.float32)).astype(x.dtype)

def rope_tables(positions):
    inv_freq = ROPE_BASE ** (-jnp.arange(0, QK_ROPE_DIM, 2, dtype=jnp.float32) / QK_ROPE_DIM)
    ang = positions.astype(jnp.float32)[..., None] * inv_freq
    return jnp.cos(ang), jnp.sin(ang)

def apply_rope(x, cos, sin):
    xf = x.astype(jnp.float32)
    x1, x2 = jnp.split(xf, 2, axis=-1)
    return jnp.concatenate([x1 * cos - x2 * sin, x2 * cos + x1 * sin], axis=-1).astype(x.dtype)

def causal_block_attention(q, k, v, positions):
    B, H, S, _ = q.shape
    nb = S // Q_BLOCK
    scale = QK_DIM ** -0.5
    qb = q.reshape(B, H, nb, Q_BLOCK, QK_DIM).transpose(2, 0, 1, 3, 4)
    pb = positions.reshape(B, nb, Q_BLOCK).transpose(1, 0, 2)
    neg = jnp.finfo(jnp.float32).min

    def one_block(args):
        q_blk, p_blk = args
        s = jnp.einsum('bhqd,bhkd->bhqk', q_blk, k, preferred_element_type=jnp.float32) * scale
        mask = positions[:, None, None, :] <= p_blk[:, None, :, None]
        p = jax.nn.softmax(jnp.where(mask, s, neg), axis=-1)
        return jnp.einsum('bhqk,bhkd->bhqd', p.astype(v.dtype), v)

    out = lax.map(one_block, (qb, pb))
    return out.transpose(1, 0, 3, 2, 4).reshape(B, S, H * V_HEAD_DIM)

def causal_depthwise_conv(u, w, b):
    y = lax.conv_general_dilated(
        u, w[:, None, :].astype(u.dtype), window_strides=(1,),
        padding=[(CONV_KERNEL - 1, 0)], dimension_numbers=('NWC', 'WIO', 'NWC'),
        feature_group_count=u.shape[-1])
    return y + b

def hierarchical_moe(h, rg_w, rg_b, re_w, re_b, e_gate, e_up, e_down):
    B, S, D = h.shape
    t = h.reshape(-1, D)
    g_prob = jax.nn.softmax((t @ rg_w + rg_b).astype(jnp.float32), axis=-1)
    g_val, g_idx = lax.top_k(g_prob, 1)
    e_logits = (t @ re_w + re_b).astype(jnp.float32).reshape(-1, N_GROUPS, EXPERTS_PER_GROUP)
    e_sel = jnp.take_along_axis(e_logits, g_idx[:, :, None], axis=1)[:, 0]
    e_val, e_idx = lax.top_k(jax.nn.softmax(e_sel, axis=-1), TOP_K_IN_GROUP)
    e_val = e_val / jnp.sum(e_val, axis=-1, keepdims=True)
    w_group = jnp.sum(jax.nn.one_hot(e_idx, EXPERTS_PER_GROUP, dtype=jnp.float32) * e_val[..., None], axis=1)
    combine = (jax.nn.one_hot(g_idx[:, 0], N_GROUPS, dtype=jnp.float32)[:, :, None]
               * (g_val * w_group)[:, None, :]).astype(h.dtype)
    out = jnp.zeros_like(t)
    for gi in range(N_GROUPS):
        a = jnp.einsum('td,edf->tef', t, e_gate[gi])
        u = jnp.einsum('td,edf->tef', t, e_up[gi])
        hid = jax.nn.silu(a) * u * combine[:, gi, :, None]
        out = out + jnp.einsum('tef,efd->td', hid, e_down[gi])
    return out.reshape(B, S, D)

def second_inputs(seed: int = 0) -> dict:
    key = jax.random.key(seed)
    ks = iter(jax.random.split(key, 32))
    L, D = DEPTH, D_MODEL

    def nrm(shape, scale):
        return jax.random.normal(next(ks), shape, jnp.float32) * scale

    x = nrm((BATCH, SEQ, D), 1.0)
    c = nrm((BATCH, D), 1.0)
    offsets = jax.random.randint(next(ks), (BATCH, 1), 0, 1024, dtype=jnp.int32)
    positions = offsets + jnp.arange(SEQ, dtype=jnp.int32)[None, :]
    G, E, F = N_GROUPS, EXPERTS_PER_GROUP, D_EXPERT
    return {
        "x": x, "c": c, "positions": positions,
        "ada_w": nrm((L, D, 6 * D), 0.5 * D ** -0.5),
        "ada_b": nrm((L, 6 * D), 0.02),
        "norm1_g": 1.0 + nrm((L, D), 0.02),
        "norm2_g": 1.0 + nrm((L, D), 0.02),
        "w_in": nrm((L, D, IN_COLS), D ** -0.5),
        "q_norm_g": 1.0 + nrm((L, Q_LORA_RANK), 0.02),
        "w_uq": nrm((L, Q_LORA_RANK, N_HEADS * QK_DIM), Q_LORA_RANK ** -0.5),
        "kv_norm_g": 1.0 + nrm((L, KV_LORA_RANK), 0.02),
        "w_ukv": nrm((L, KV_LORA_RANK, N_HEADS * (QK_NOPE_DIM + V_HEAD_DIM)), KV_LORA_RANK ** -0.5),
        "w_o_attn": nrm((L, ATTN_WIDTH, D), ATTN_WIDTH ** -0.5),
        "conv_w": nrm((L, CONV_KERNEL, CONV_CHANNELS), CONV_KERNEL ** -0.5),
        "conv_b": nrm((L, CONV_CHANNELS), 0.02),
        "conv_ln_g": 1.0 + nrm((L, CONV_CHANNELS), 0.02),
        "conv_ln_b": nrm((L, CONV_CHANNELS), 0.02),
        "w_conv_out": nrm((L, CONV_CHANNELS, D), CONV_CHANNELS ** -0.5),
        "w_out": nrm((L, D, D), D ** -0.5),
        "router_group_w": nrm((L, D, G), D ** -0.5),
        "router_group_b": nrm((L, G), 0.01),
        "router_expert_w": nrm((L, D, G * E), D ** -0.5),
        "router_expert_b": nrm((L, G * E), 0.01),
        "expert_w_gate": nrm((L, G, E, D, F), D ** -0.5),
        "expert_w_up": nrm((L, G, E, D, F), D ** -0.5),
        "expert_w_down": nrm((L, G, E, F, D), F ** -0.5),
        "final_norm_g": 1.0 + nrm((D,), 0.02),
    }

def second_block(x, c, positions, ada_w, ada_b, norm1_g, norm2_g, w_in, q_norm_g, w_uq,
              kv_norm_g, w_ukv, w_o_attn, conv_w, conv_b, conv_ln_g, conv_ln_b,
              w_conv_out, w_out, router_group_w, router_group_b, router_expert_w,
              router_expert_b, expert_w_gate, expert_w_up, expert_w_down, final_norm_g):
    B, S, D = x.shape
    cos, sin = rope_tables(positions)
    c_act = jax.nn.silu(c)
    for l in range(DEPTH):
        ada = c_act @ ada_w[l] + ada_b[l]
        sh1, sc1, gt1, sh2, sc2, gt2 = [a[:, None, :] for a in jnp.split(ada, 6, axis=-1)]

        h = rmsnorm_2(x, norm1_g[l]) * (1.0 + sc1) + sh1
        z = h @ w_in[l]
        q_lat, kv_lat, k_rope, conv_in, gate_logits = jnp.split(z, SPLIT_POINTS, axis=-1)

        q = (rmsnorm_2(q_lat, q_norm_g[l]) @ w_uq[l]).reshape(B, S, N_HEADS, QK_DIM)
        q_nope, q_pe = jnp.split(q, [QK_NOPE_DIM], axis=-1)
        q_pe = apply_rope(q_pe, cos[:, :, None, :], sin[:, :, None, :])
        kv = (rmsnorm_2(kv_lat, kv_norm_g[l]) @ w_ukv[l]).reshape(B, S, N_HEADS, QK_NOPE_DIM + V_HEAD_DIM)
        k_nope, v = jnp.split(kv, [QK_NOPE_DIM], axis=-1)
        k_pe = jnp.broadcast_to(apply_rope(k_rope, cos, sin)[:, :, None, :], (B, S, N_HEADS, QK_ROPE_DIM))
        qh = jnp.concatenate([q_nope, q_pe], axis=-1).transpose(0, 2, 1, 3)
        kh = jnp.concatenate([k_nope, k_pe], axis=-1).transpose(0, 2, 1, 3)
        attn = causal_block_attention(qh, kh, v.transpose(0, 2, 1, 3), positions)
        y_attn = attn @ w_o_attn[l]

        glu_a, glu_b = jnp.split(conv_in, 2, axis=-1)
        u = glu_a * jax.nn.sigmoid(glu_b)
        u = causal_depthwise_conv(u, conv_w[l], conv_b[l])
        u = jax.nn.silu(layernorm(u, conv_ln_g[l], conv_ln_b[l]))
        y_conv = u @ w_conv_out[l]

        g_attn, g_conv = jnp.split(jax.nn.sigmoid(gate_logits), 2, axis=-1)
        y = (g_attn * y_attn + g_conv * y_conv) @ w_out[l]
        x = x + gt1 * y

        h = rmsnorm_2(x, norm2_g[l]) * (1.0 + sc2) + sh2
        x = x + gt2 * hierarchical_moe(h, router_group_w[l], router_group_b[l], router_expert_w[l],
                                       router_expert_b[l], expert_w_gate[l], expert_w_up[l],
                                       expert_w_down[l])
    return rmsnorm_2(x, final_norm_g)


def setup_inputs(seed=0):
    out = dict(first_inputs(seed))
    for name, value in second_inputs(seed + 1).items():
        if name != "x":
            out[name + "_2"] = value
    return out


def reference(
    x, meta_tokens, g_mix_pre, w_in, w_gate_up, b_gate, gla_norm_g, w_o_gla, a_re, a_im,
    log_step, b_re, b_im, c_re, c_im, d_skip, w_glu, b_glu, w_out, g_mix_post, g_ffn_pre, w_ff1,
    w_ff2, g_ffn_post, c_2, positions_2, ada_w_2, ada_b_2, norm1_g_2, norm2_g_2, w_in_2,
    q_norm_g_2, w_uq_2, kv_norm_g_2, w_ukv_2, w_o_attn_2, conv_w_2, conv_b_2, conv_ln_g_2,
    conv_ln_b_2, w_conv_out_2, w_out_2, router_group_w_2, router_group_b_2, router_expert_w_2,
    router_expert_b_2, expert_w_gate_2, expert_w_up_2, expert_w_down_2, final_norm_g_2,
):
    x = first_block(
        x, meta_tokens, g_mix_pre, w_in, w_gate_up, b_gate, gla_norm_g, w_o_gla, a_re, a_im,
        log_step, b_re, b_im, c_re, c_im, d_skip, w_glu, b_glu, w_out, g_mix_post, g_ffn_pre,
        w_ff1, w_ff2, g_ffn_post,
    )
    return second_block(
        x, c_2, positions_2, ada_w_2, ada_b_2, norm1_g_2, norm2_g_2, w_in_2, q_norm_g_2, w_uq_2,
        kv_norm_g_2, w_ukv_2, w_o_attn_2, conv_w_2, conv_b_2, conv_ln_g_2, conv_ln_b_2,
        w_conv_out_2, w_out_2, router_group_w_2, router_group_b_2, router_expert_w_2,
        router_expert_b_2, expert_w_gate_2, expert_w_up_2, expert_w_down_2, final_norm_g_2,
    )


_drawn_inputs = setup_inputs


def setup_inputs(seed=0):
    import zlib

    import numpy as np

    out = dict(_drawn_inputs(seed))
    spreads = {}
    factors = {'a_re': 8.0,
     'b_re': 3.301,
     'b_im': 3.365,
     'c_re': 3.314,
     'c_im': 3.359,
     'b_glu': 4.515,
     'ada_b_2': 5.447,
     'norm1_g_2': 8.0,
     'norm2_g_2': 8.0,
     'q_norm_g_2': 8.0,
     'w_uq_2': 4.716,
     'kv_norm_g_2': 8.0,
     'conv_b_2': 8.0,
     'conv_ln_g_2': 8.0,
     'conv_ln_b_2': 8.0,
     'router_group_b_2': 8.0,
     'router_expert_b_2': 8.0,
     'final_norm_g_2': 2.754}
    for name, (base, spread) in spreads.items():
        noise = np.random.default_rng([zlib.crc32(name.encode()), seed]).standard_normal(out[name].shape)
        drawn = base * np.exp(spread * noise) if base else spread * noise
        out[name] = __import__('jax').numpy.asarray(drawn.astype(out[name].dtype))
    for name, factor in factors.items():
        out[name] = (out[name] * factor).astype(out[name].dtype)
    return out
```

```python
from contextlib import ExitStack
import math

import numpy as np
import concourse.bass as bass
from concourse import mybir

F32 = mybir.dt.float32
I32 = mybir.dt.int32
ALU = mybir.AluOpType
ACT = mybir.ActivationFunctionType
AX = mybir.AxisListType.X
EPS = 1e-6
NT = 528
RING = 5
MAGIC = 12582912.0
C1, C2, C3 = 6.28125, 0.0019350051879882812, 3.0199159819e-07
PI_IN = 3.1415925
BIG = -3.0e38

VEC = [("g_mix_pre", 8), ("b_gate", 4), ("gla_norm_g", 8), ("d_skip", 8), ("b_glu", 16), ("g_mix_post", 8),
       ("g_ffn_pre", 8), ("g_ffn_post", 8), ("c_2", 8), ("ada_b_2", 48), ("norm1_g_2", 8), ("norm2_g_2", 8),
       ("q_norm_g_2", 3), ("kv_norm_g_2", 2), ("conv_b_2", 4), ("conv_ln_g_2", 4), ("conv_ln_b_2", 4),
       ("final_norm_g_2", 8), ("conv_w_2", 124), ("a_re", 32), ("a_im", 32), ("log_step", 32), ("rb", 36)]
VOFF, _o = {}, 0
for _n, _c in VEC:
    VOFF[_n] = (_o, _c)
    _o += _c
NVEC = _o
CST = [("ident", 128), ("ones", 128), ("tril", 128), ("reset", NT), ("freq", 1), ("sign", 1), ("rev4", 4), ("rev8", 8)]
COFF, _o = {}, 0
for _n, _c in CST:
    COFF[_n] = (_o, _c)
    _o += _c
NCST = _o
PLAN = ([("u", i) for i in range(4)] + [("k", i) for i in range(2)] + [("v", i) for i in range(4)]
        + [("q", i) for i in range(2)] + [("r", i) for i in range(4)])
for _j in range(4):
    PLAN += [("zg", _j), ("og", _j)]
for _j in range(4):
    PLAN += [("zs", _j), ("glua", _j), ("glub", _j)]
PLAN += [("wo", i) for i in range(4)] + [("f1", i) for i in range(16)] + [("ada", i) for i in range(24)]
PLAN += [("f2", i) for i in range(16)]
PLAN += [("lat", i) for i in range(3)] + [("cin", i) for i in range(4)] + [("kv", 0)]
for _j in range(4):
    PLAN += [("ga", _j)] + ([("oa", _j // 2)] if _j % 2 == 0 else [])
for _j in range(4):
    PLAN += [("gc", _j)] + ([("oc", _j // 2)] if _j % 2 == 0 else [])
PLAN += [("wo2", i) for i in range(4)] + [("ex", i) for i in range(32)] + [("dn", i) for i in range(16)]
NU = len(PLAN)


def program(nc, W, vecs, cst, xT, wal, wgu, wuq, bc, rw, sel, posr, posc, out):
    ctx = ExitStack()
    with ctx:
        def sbt(name, shape, dt=F32):
            return ctx.enter_context(nc.sbuf_tensor(name, shape, dt))

        ENG = ["pe", "act", "dve", "pool", "sp"]
        sem = {e: ctx.enter_context(nc.semaphore("s_" + e)) for e in ENG}
        s_ring = [ctx.enter_context(nc.semaphore(f"s_ring{i}")) for i in range(RING)]
        s_out = ctx.enter_context(nc.semaphore("s_out"))
        n_ld = [0]
        queue = {e: [] for e in ENG}
        count = {e: 0 for e in ENG}

        def flat(w):
            if w is None:
                return []
            if isinstance(w, tuple):
                return [w]
            return [t for x in w for t in flat(x)]

        def emit(e, fn, w=None, inc=True):
            queue[e].append((flat(w), fn, inc))
            if inc:
                count[e] += 1
            return (sem[e], count[e])

        def now(e):
            return (sem[e], count[e])

        def step(e, fn, w=None):
            return emit(e, fn, [now(e), flat(w)])

        def act(o, i, f, w=None, **kw):
            return step("act", lambda g: g.activation(o, i, f, **kw), w)

        def tt(o, a, b, op, w=None, e="dve"):
            return step(e, lambda g: g.tensor_tensor(o, a, b, op), w)

        def ts(o, a, s1, s2, op0, op1=None, w=None, e="dve"):
            if op1 is None:
                return step(e, lambda g: g.tensor_scalar(o, a, s1, None, op0), w)
            return step(e, lambda g: g.tensor_scalar(o, a, s1, s2, op0, op1), w)

        def stt(o, a, s, b, op0, op1, w=None):
            return step("dve", lambda g: g.scalar_tensor_tensor(out=o, in0=a, scalar=s, in1=b, op0=op0, op1=op1), w)

        def cp(o, i, w=None, e="dve"):
            if e == "act":
                return act(o, i, ACT.Copy, w)
            return step(e, lambda g: g.tensor_copy(o, i), w)

        def red(o, i, op, w=None):
            return step("dve", lambda g: g.tensor_reduce(o, i, AX, op), w)

        def recip(o, i, w=None):
            return step("dve", lambda g: g.reciprocal(o, i), w)

        def zero(o, w=None, e="pool"):
            return step(e, lambda g: g.memset(o, 0.0), w)

        MUL, ADD, SUB, MAX = ALU.mult, ALU.add, ALU.subtract, ALU.max

        def mm(group, w=None):
            w = flat(w)
            for n, (o, l, r, st, sp) in enumerate(group):
                t = emit("pe", lambda g, o=o, l=l, r=r, st=st, sp=sp: g.matmul(
                    o, l, r, start=st, stop=sp, skip_group_check=True), w if n == 0 else None, n == len(group) - 1)
            return t

        def tr(group, w=None):
            w = flat(w)
            for n, (o, i, idt) in enumerate(group):
                t = emit("pe", lambda g, o=o, i=i, idt=idt: g.transpose(o, i, idt), w if n == 0 else None,
                         n == len(group) - 1)
            return t

        banks = [ctx.enter_context(nc.psum_tensor(f"bank{i}", [128, 512], F32)) for i in range(8)]
        bfree = [None] * 8
        bnext = [0]

        def take():
            i = next(j % 8 for j in range(bnext[0], bnext[0] + 8) if bfree[j % 8] != "held")
            bnext[0] = i + 1
            f, bfree[i] = bfree[i], "held"
            return i, banks[i][:, :], f

        def give(i, t):
            bfree[i] = flat(t)

        ringt = sbt("ring", [128, RING, 2048])
        upos = [0]

        def load_unit(n, w):
            s = n % RING
            emit("sp", lambda g: g.dma_start(ringt[:, s, :], W[n]).then_inc(s_ring[s], 16), w, False)

        def unit(name, i):
            n = upos[0]
            assert PLAN[n] == (name, i), (PLAN[n], name, i)
            upos[0] += 1
            return n, ringt[:, n % RING, :], (s_ring[n % RING], 16 * (n // RING + 1))

        def release(n, t):
            if n + RING < NU:
                load_unit(n + RING, t)

        HT = sbt("h", [128, 8, NT])
        vt = sbt("vecs", [128, NVEC])
        ct = sbt("cst", [128, NCST])
        adat = sbt("adat", [128, 48])
        small = sbt("small", [128, 64])
        ARENA = 36600
        arena = sbt("arena", [128, ARENA])
        top = [0]

        def al(*dims):
            n = int(np.prod(dims))
            a = arena[:, top[0]:top[0] + n]
            top[0] += n
            assert top[0] <= ARENA, top[0]
            if len(dims) == 2:
                a = a.rearrange("p (a b) -> p a b", b=dims[1])
            if len(dims) == 3:
                a = a.rearrange("p (a b c) -> p a b c", b=dims[1], c=dims[2])
            return a

        def barrier():
            return [now(e) for e in ("pe", "act", "dve", "pool")]

        def sync_all():
            b = barrier()
            for e in ("act", "dve", "pool"):
                queue[e].append((b, None, False))
            queue["pe"].append((b, None, False))

        def vec(name):
            o, n = VOFF[name]
            return vt[:, o:o + n]

        def con(name):
            o, n = COFF[name]
            return ct[:, o:o + n]

        def ld(o, i):
            s = ctx.enter_context(nc.semaphore(f"s_ld{n_ld[0]}"))
            n_ld[0] += 1
            emit("sp", lambda g: g.dma_start(o, i).then_inc(s, 16), None, False)
            return (s, 16)

        ident, ones = con("ident"), con("ones")
        X = HT[:, :, 16:NT]

        xn = al(8, NT)
        base_xn = top[0]
        t_x = [ld(HT[:, 2 * i:2 * i + 2, :], xT[:, 2 * i:2 * i + 2, :]) for i in range(4)]
        t_c = ld(ct[:, :], cst)
        t_v = ld(vt[:, :], vecs)
        walt = al(8, 16)
        t_wal = ld(walt, wal)
        wgut = al(512)
        t_wgu = ld(wgut[0:16, :], wgu)
        mark_g = top[0]
        BC = al(4, 512)
        t_bc = ld(BC, bc)
        for n in range(RING):
            load_unit(n, None)

        def rms(src, n, width, tmp, rstd, w, dim):
            i, b, f = take()
            for k in range(n):
                t = act(tmp[:, k, 0:width], src[:, k, :], ACT.Square, w)
                tm = mm([(b[:, 0:width], ones, tmp[:, k, 0:width], k == 0, k == n - 1)], [t, t_c, f])
            return root(i, b[:, 0:width], rstd, tm, dim)

        def root(i, b, rstd, tm, dim):
            t = ts(rstd, b, 1.0 / dim, EPS, MUL, ADD, tm)
            give(i, t)
            t = act(rstd, rstd, ACT.Sqrt, t)
            return recip(rstd, rstd, t)

        mark = top[0]
        sq = al(8, 512)
        rst = al(512)
        rstm = al(16)
        sqm = al(8, 16)
        t0 = rms(X, 8, 512, sq, rst, [t_x], 1024)
        t1 = rms(HT[:, :, 0:16], 8, 16, sqm, rstm, [t_x], 1024)
        g = vec("g_mix_pre")
        for k in range(8):
            stt(xn[:, k, 16:NT], HT[:, k, 16:NT], g[:, k:k + 1], rst, MUL, MUL, [t0, t_v])
            t_xn = stt(xn[:, k, 0:16], HT[:, k, 0:16], g[:, k:k + 1], rstm, MUL, MUL, t1)
        sync_all()
        top[0] = mark
        XN = xn[:, :, 16:NT]
        XM = xn[:, :, 0:16]

        def linear(name, i, evac, rhs, w, nk=8, meta=None):
            n, u, tu = unit(name, i)
            u = u.rearrange("p (k m) -> p k m", k=nk)
            per = u.shape[2] // 128
            for j in range(per):
                bi, b, f = take()
                l = [u[:, k, j * 128:(j + 1) * 128] for k in range(nk)]
                t = mm([(b, l[k], rhs[k], k == 0, k == nk - 1) for k in range(nk)], [tu, w, f])
                give(bi, evac(per * i + j, b, t))
                if meta is not None:
                    bi, b, f = take()
                    t = mm([(b[:, 0:16], l[k], meta[0][k], k == 0, k == nk - 1) for k in range(nk)], [f])
                    give(bi, meta[1](per * i + j, b[:, 0:16], t))
            release(n, t)

        xr = [XN[:, k, :] for k in range(8)]
        xm = [XM[:, k, :] for k in range(8)]

        U = al(8, NT)
        for i in range(4):
            linear("u", i, lambda j, b, t: cp(U[:, j, 16:NT], b, t, "act"), xr, t_xn,
                   meta=(xm, lambda j, b, t: cp(U[:, j, 0:16], b, t)))
        t_u = [now("act"), now("dve")]

        def p32():
            return al(32)

        def reduce_angle(r, th, n, w=None):
            ts(n, th, 1.0 / (2 * math.pi), MAGIC, MUL, ADD, w)
            ts(n, n, -MAGIC, None, ADD)
            stt(r, n, -C1, th, MUL, ADD)
            stt(r, n, -C2, r, MUL, ADD)
            stt(r, n, -C3, r, MUL, ADD)
            return ts(r, r, PI_IN, -PI_IN, ALU.min, MAX)

        def sin_cos(s, c, r, w):
            act(s, r, ACT.Sin, w)
            t = act(c, r, ACT.Abs)
            t = ts(c, c, -1.0, math.pi / 2, MUL, ADD, t)
            return act(c, c, ACT.Sin, t)

        ar, ai, ls = vec("a_re"), vec("a_im"), vec("log_step")
        dt_, mag, th, nn, si, co, fr, fi, q1, q2, zr = [p32() for _ in range(11)]
        PW = al(9, 2, 32)
        L8i = al(2, 32)
        t = act(dt_, ls, ACT.Exp, t_v)
        t = tt(mag, ar, dt_, MUL, t)
        ta = act(mag, mag, ACT.Exp, t)
        tt(th, ai, dt_, MUL)
        t = reduce_angle(q1, th, nn)
        t = sin_cos(si, co, q1, [t, ta])
        lr, li = PW[:, 1, 0, :], PW[:, 1, 1, :]
        step("dve", lambda g: g.memset(PW[:, 0, 0, :], 1.0))
        step("dve", lambda g: g.memset(PW[:, 0, 1, :], 0.0))
        tt(lr, mag, co, MUL, t)
        tt(li, mag, si, MUL)
        for s in range(1, 8):
            a, b = PW[:, s, 0, :], PW[:, s, 1, :]
            tt(q1, a, lr, MUL)
            tt(q2, b, li, MUL)
            tt(PW[:, s + 1, 0, :], q1, q2, SUB)
            tt(q1, a, li, MUL)
            tt(q2, b, lr, MUL)
            tt(PW[:, s + 1, 1, :], q1, q2, ADD)
        ts(L8i[:, 0, :], PW[:, 8, 1, :], -1.0, None, MUL)
        cp(L8i[:, 1, :], PW[:, 8, 1, :])
        ts(zr, lr, -1.0, None, ADD)
        tt(q1, ar, ar, MUL)
        tt(q2, ai, ai, MUL)
        tt(q1, q1, q2, ADD)
        recip(nn, q1)
        tt(q1, zr, ar, MUL)
        tt(q2, li, ai, MUL)
        tt(q1, q1, q2, ADD)
        tt(fr, q1, nn, MUL)
        tt(q1, li, ar, MUL)
        tt(q2, zr, ai, MUL)
        tt(q1, q1, q2, SUB)
        tt(fi, q1, nn, MUL)

        def b16(a):
            return a.unsqueeze(2).to_broadcast([128, 32, 16])

        br, bi_, cr, ci = [BC[:, k, :].rearrange("p (g h) -> p g h", h=16) for k in range(4)]
        BB = al(2, 512)
        BBr, BBi = [BB[:, k, :].rearrange("p (g h) -> p g h", h=16) for k in range(2)]
        tw = al(4, 512)
        ta_, tb_ = [tw[:, k, :].rearrange("p (g h) -> p g h", h=16) for k in range(2)]
        tt(ta_, br, b16(fr), MUL, t_bc)
        tt(tb_, bi_, b16(fi), MUL)
        tt(BBr, ta_, tb_, SUB)
        tt(ta_, bi_, b16(fr), MUL)
        tt(tb_, br, b16(fi), MUL)
        t_bb = tt(BBi, ta_, tb_, ADD)
        NCI = al(512)
        nci = NCI.rearrange("p (g h) -> p g h", h=16)
        ts(nci, ci, -1.0, None, MUL)
        t_par = now("dve")

        G = [al(4, 8, 32) for _ in range(2)]
        D = [[al(4, 9, 32) for _ in range(2)] for _ in range(2)]
        KT = [al(8, 128) for _ in range(2)]
        GT = [al(4, 128) for _ in range(2)]
        US = [al(2, 66) for _ in range(2)]
        SX = al(67, 2, 32)
        Y = al(8, 512)
        Pt = al(2, 4 * 9 * 16)
        for a in G + D[0] + D[1] + KT:
            t_z = zero(a, barrier())

        gread = [None]
        dread = [None, None]

        def weights_in(cb):
            pw = [PW[:, 7::-1, k, 4 * cb:4 * cb + 4].rearrange("p j g -> p g j").unsqueeze(3).to_broadcast([128, 4, 8, 16])
                  for k in range(2)]
            bb = [x[:, 4 * cb:4 * cb + 4, :].unsqueeze(2).to_broadcast([128, 4, 8, 16]) for x in (BBr, BBi)]
            t1, t2 = [tw[:, k, :].rearrange("p (g j h) -> p g j h", g=4, j=8) for k in range(2)]
            for k, (x, y, op) in enumerate(((0, 1, SUB), (1, 0, ADD))):
                tt(t1, pw[0], bb[x], MUL)
                tt(t2, pw[1], bb[y], MUL)
                for hf in range(2):
                    p = slice(64 * hf, 64 * hf + 64)
                    t = tt(G[k][p, :, :, 16 * hf:16 * hf + 16], t1[p], t2[p], op, [t_z, gread[0]])
            return t

        def weights_out(cb, par):
            pw = [PW[:, :, k, 4 * cb:4 * cb + 4].rearrange("p j g -> p g j").unsqueeze(3).to_broadcast([128, 4, 9, 16])
                  for k in range(2)]
            cc = [x[:, 4 * cb:4 * cb + 4, :].unsqueeze(2).to_broadcast([128, 4, 9, 16]) for x in (cr, ci, nci)]
            t1, t2 = [Pt[:, k, :].rearrange("p (g j h) -> p g j h", g=4, j=9) for k in range(2)]
            for k, (x, y) in enumerate(((0, 1), (2, 0))):
                tt(t1, pw[0], cc[x], MUL, t_par, "pool")
                tt(t2, pw[1], cc[y], MUL, None, "pool")
                for hf in range(2):
                    p = slice(64 * hf, 64 * hf + 64)
                    t = tt(D[par][k][p, :, :, 16 * hf:16 * hf + 16], t1[p], t2[p], SUB, dread[par], "pool")
            return t

        uread = [None, None]
        gtread = [None, None]
        ktread = [None, None]
        npair = 0
        for cb in range(8):
            par = cb % 2
            t_d = weights_out(cb, par)
            t_g = weights_in(cb)
            bk, b, f = take()
            grp = []
            for q in range(4):
                o = b[32 * q:32 * q + 32, 0:256]
                grp += [(o, G[0][:, q, 7, :], D[par][0][:, q, 0:8, :], True, False),
                        (o, G[1][:, q, 7, :], D[par][1][:, q, 0:8, :], False, True)]
            t = mm(grp, [t_d, t_g, f])
            dread[par] = t
            for q in range(4):
                p = slice(32 * q, 32 * q + 32)
                tk = cp(KT[par][p, :, 32 * q:32 * q + 32], b[p, 0:256].rearrange("p (s c) -> p s c", s=8),
                        [t, ktread[par], t_z], "act")
            give(bk, tk)
            ux = U[:, cb, 16:NT].rearrange("p (c s) -> p c s", s=8)
            by, b, f = take()
            yv = b.rearrange("p (c s) -> p c s", s=8)
            t = mm([(yv[:, :, s:8], KT[par][:, s, :], ux[:, :, 0:8 - s], s == 0, s == 7) for s in range(8)], [tk, t_u, f])
            ktread[par] = t
            give(by, stt(Y[:, cb, :], U[:, cb, 16:NT], vec("d_skip")[:, cb:cb + 1], b, MUL, ADD, t))
            b0, s0, f0 = take()
            b1, s1, f1 = take()
            for q in range(4):
                z = npair % 2
                npair += 1
                bt, b, f = take()
                t = tr([(b[:, 128 * (2 * k + hf):128 * (2 * k + hf) + 128], G[k][:, q, 4 * hf:4 * hf + 4, :], ident)
                        for k in range(2) for hf in range(2)], [t_g, f])
                gread[0] = t
                tg = cp(GT[z], b.rearrange("p (a m) -> p a m", a=4), [t, gtread[z]], "act")
                give(bt, tg)
                uc = U[32 * q:32 * q + 32, cb, :].rearrange("p (c f l) -> p l f c", f=2, l=4)
                for l in range(4):
                    tu_ = cp(US[z][32 * l:32 * l + 32], uc[:, l], uread[z] if l == 0 else None, "act" if l % 2 else "dve")
                t = mm([(s[:, 66 * q:66 * q + 66], GT[z][:, 2 * k + hf, :], US[z][:, hf, :], hf == 0, hf == 1)
                        for k, s in ((0, s0), (1, s1)) for hf in range(2)],
                       [now("dve"), now("act"), f0, f1])
                uread[z] = gtread[z] = t
            for k, (i, s) in enumerate(((b0, s0), (b1, s1))):
                o = SX[:, 1:67, k, 4 * cb:4 * cb + 4].rearrange("p c q -> p q c")
                give(i, cp(o, s[:, 0:264].rearrange("p (q c) -> p q c", q=4), t))
        sw = [tw[:, k, 0:64].rearrange("p (a g) -> p a g", a=2) for k in range(2)]
        l8 = PW[:, 8:9, 0, :].to_broadcast([128, 2, 32])
        for c in range(1, 65):
            tt(sw[0], SX[:, c], l8, MUL)
            tt(sw[1], SX[:, c, ::-1, :], L8i, MUL)
            tt(SX[:, c + 1], SX[:, c + 1], sw[0], ADD)
            t_sx = tt(SX[:, c + 1], SX[:, c + 1], sw[1], ADD)
        for cb in range(8):
            par = cb % 2
            t_d = weights_out(cb, par)
            by, b, f = take()
            yv = b.rearrange("p (c s) -> p c s", s=8)
            grp = []
            for q in range(4):
                for s in range(8):
                    o = yv[32 * q:32 * q + 32, :, s]
                    for k in range(2):
                        grp.append((o, D[par][k][:, q, s + 1, :], SX[:, 2:66, k, 4 * cb + q], s == 0 and k == 0, k == 1))
            t = mm(grp, [t_d, t_sx, f])
            dread[par] = t
            give(by, tt(Y[:, cb, :], Y[:, cb, :], b, ADD, t))
        sync_all()
        mark = mark_g
        top[0] = mark
        GS = al(8, 512)
        gt = al(8, 512)
        for j in range(8):
            t = act(gt[:, j, :], Y[:, j, :], ACT.Square)
            ts(gt[:, j, :], gt[:, j, :], 0.044715, 1.0, MUL, ADD, t)
            t = tt(gt[:, j, :], gt[:, j, :], Y[:, j, :], MUL)
            t = act(gt[:, j, :], gt[:, j, :], ACT.Sigmoid, t, scale=2 * math.sqrt(2 / math.pi))
            t_gs = tt(GS[:, j, :], gt[:, j, :], Y[:, j, :], MUL, t)
        sync_all()
        top[0] = mark
        GS = al(8, 512)

        LA = al(4, NT)
        alow = al(NT)
        e1 = al(NT)
        e2 = al(NT)
        bi1, b1, f1 = take()
        bi2, b2, f2 = take()
        t1 = mm([(b1[0:16, :], walt[:, k, :], xr[k], k == 0, k == 7) for k in range(8)], [t_wal, t_xn, f1])
        t2 = mm([(b2[0:16, 0:16], walt[:, k, :], xm[k], k == 0, k == 7) for k in range(8)], [f2])
        t = cp(alow[0:16, 16:NT], b1[0:16, :], t1)
        give(bi1, t)
        t = cp(alow[0:16, 0:16], b2[0:16, 0:16], t2)
        give(bi2, t)
        bg = vec("b_gate")
        for h in range(4):
            for lo, hi in ((0, 16), (16, NT)):
                i, b, f = take()
                b = b[:, 0:hi - lo]
                tm = mm([(b, wgut[0:16, 128 * h:128 * h + 128], alow[0:16, lo:hi], True, True)], [t, t_wgu, f])
                tb = act(e1[:, lo:hi], b, ACT.Abs, tm, bias=bg[:, h:h + 1])
                act(e1[:, lo:hi], e1[:, lo:hi], ACT.Exp, scale=-1.0)
                ta = act(e2[:, lo:hi], e1[:, lo:hi], ACT.Ln, now("dve"), bias=1.0)
                td = ts(LA[:, h, lo:hi], b, bg[:, h:h + 1], 0.0, ADD, ALU.min, tb)
                give(i, td)
                tt(LA[:, h, lo:hi], LA[:, h, lo:hi], e2[:, lo:hi], SUB, ta)
        K = al(4, NT)
        Q = al(4, 512)
        VV = al(4, 1024)
        VM = al(1024)
        for i in range(2):
            linear("k", i, lambda j, b, t: cp(K[:, j, 16:NT], b, t, "act"), xr, t_xn,
                   meta=(xm, lambda j, b, t: cp(K[:, j, 0:16], b, t, "act")))
        for half in range(2):
            bb_ = [take() for _ in range(5)]
            for kg in range(2):
                n, u, tu = unit("v", 2 * half + kg)
                u = u.rearrange("p (k m) -> p k m", k=4)
                for m, (i, b, f) in enumerate(bb_):
                    grp = []
                    for k in range(4):
                        l = xn[:, 4 * kg + k, 16 + 128 * m:144 + 128 * m] if m < 4 else xn[:, 4 * kg + k, 0:16]
                        grp.append((b if m < 4 else b[0:16, :], l, u[:, k, :], kg == 0 and k == 0, kg == 1 and k == 3))
                    t = mm(grp, [tu, f])
                    if kg == 1:
                        o = VV[:, m, 512 * half:512 * half + 512] if m < 4 else VM[0:16, 512 * half:512 * half + 512]
                        give(i, cp(o, b if m < 4 else b[0:16, :], t, "act"))
                release(n, t)
        for i in range(2):
            linear("q", i, lambda j, b, t: act(Q[:, j, :], b, ACT.Copy, t, scale=128.0 ** -0.5), xr, t_xn)
        t_kv = now("act")
        O = al(8, 512)
        cs = al(NT)
        ex = al(4, NT)
        qi, ki = e1, e2
        qs, ks = al(NT), al(NT)
        dc = al(9)
        S = al(8, 256)
        SC = al(2, 512)
        kst = al(4, 128)
        ksm = al(128)
        t_scz = zero(SC, barrier(), "pool")
        reset = con("reset")
        tril = con("tril").bitcast(I32)
        for h in range(4):
            t_free = now("pe")
            step("dve", lambda g, h=h: g.tensor_tensor_scan(cs, reset, LA[:, h, :], 0.0, MUL, ADD), now("act"))
            cx = cs[:, 16:NT].rearrange("p (c t) -> p c t", t=64)
            d0, d1 = ex[:, 0, :], ex[:, 1, :]
            tt(d0[:, 16:NT].rearrange("p (c t) -> p c t", t=64), cx, cx[:, :, 32:33].to_broadcast([128, 8, 64]), SUB)
            tt(d1[:, 16:NT].rearrange("p (c t) -> p c t", t=64), cx[:, :, 63:64].to_broadcast([128, 8, 64]), cx, SUB)
            td = tt(d1[:, 0:16], cs[:, 15:16].to_broadcast([128, 16]), cs[:, 0:16], SUB)
            s = 1.0 / 16.0
            e3 = ex[:, 2, 16:NT]
            e4 = ex[:, 3, 16:NT]
            ta = act(dc[:, 1:9], cx[:, :, 63], ACT.Exp, td, scale=s)
            ta = act(e3, d0[:, 16:NT], ACT.Exp, scale=s)
            tt(qi[:, 16:NT], Q[:, h, :], e3, MUL, [ta, t_kv, t_free])
            ta = act(e4, d0[:, 16:NT], ACT.Exp, scale=-s)
            t_in = tt(ki[:, 16:NT], K[:, h, 16:NT], e4, MUL, ta)
            ta = act(e3, cs[:, 16:NT], ACT.Exp, t_in, scale=s)
            t_qs = tt(qs[:, 16:NT], Q[:, h, :], e3, MUL, ta)
            ta = act(d1, d1, ACT.Exp, scale=s)
            t_ks = tt(ks, K[:, h, :], d1, MUL, ta)
            i, b, f = take()
            t = mm([(b[:, 128 * m:128 * m + 128], ki[:, 16 + 128 * m:144 + 128 * m], qi[:, 16 + 128 * m:144 + 128 * m],
                     True, True) for m in range(4)], [t_in, f])
            for m in range(4):
                t_sc = step("dve", lambda g, m=m, b=b, h=h: g.copy_predicated(
                    SC[:, h % 2, 128 * m:128 * m + 128], tril, b[:, 128 * m:128 * m + 128]), [t, t_scz, t_free])
            give(i, t_sc)
            i, b, f = take()
            t = tr([(b[:, 128 * m:128 * m + 128], ks[:, 16 + 128 * m:144 + 128 * m], ident) for m in range(4)], [t_ks, f])
            tk = cp(kst, b.rearrange("p (a m) -> p a m", a=4), t, "act")
            give(i, tk)
            i, b, f = take()
            t = tr([(b[0:16, 0:128], ks[:, 0:16], ident)], f)
            tk = cp(ksm[0:16, :], b[0:16, 0:128], t, "act")
            give(i, tk)
            hv = slice(256 * h, 256 * h + 256)
            for c in range(8):
                i, b, f = take()
                if c == 0:
                    t = mm([(b[:, 0:256], ksm[0:16, :], VM[0:16, hv], True, True)], [tk, f])
                    t = cp(S[:, 0, :], b[:, 0:256], t)
                else:
                    p = slice(64 * ((c - 1) % 2), 64 * ((c - 1) % 2) + 64)
                    t = mm([(b[:, 0:256], kst[p, (c - 1) // 2, :], VV[p, (c - 1) // 2, hv], True, True)], [tk, f])
                    t = stt(S[:, c, :], S[:, c - 1, :], dc[:, c:c + 1], b[:, 0:256], MUL, ADD, t)
                give(i, t)
            i2, b2, f2 = take()
            for dv in range(2):
                i, b, f = take()
                vs = slice(256 * h + 128 * dv, 256 * h + 128 * dv + 128)
                grp = [(b[:, 128 * m:128 * m + 128], VV[:, m, vs], SC[:, h % 2, 128 * m:128 * m + 128], m == 0, False)
                       for m in range(4)]
                grp += [(b[:, 64 * c:64 * c + 64], S[:, c, 128 * dv:128 * dv + 128], qs[:, 16 + 64 * c:80 + 64 * c],
                         False, c == 7) for c in range(8)]
                tm = mm(grp, [t_sc, t, t_qs, f])
                td = cp(O[:, 2 * h + dv, :], b, tm)
                ta = act(ex[:, dv, 16:NT], O[:, 2 * h + dv, :], ACT.Square, td)
                give(i, td)
                tm = mm([(b2, ones, ex[:, dv, 16:NT], dv == 0, dv == 1)], [ta, f2])
            t = root(i2, b2, e3, tm, 256)
            for dv in range(2):
                j = 2 * h + dv
                t_o = stt(O[:, j, :], O[:, j, :], vec("gla_norm_g")[:, j:j + 1], e3, MUL, MUL, t)
        rt = [ex[:, 0, 16:NT], ex[:, 1, 16:NT]]
        rfree = [None, None]

        def gate_r(j, b, t):
            z = j % 2
            ta = act(rt[z], b, ACT.Sigmoid, [t, rfree[z], t_o])
            tt(O[:, j, :], O[:, j, :], b, MUL, ta)
            rfree[z] = tt(O[:, j, :], O[:, j, :], rt[z], MUL, ta)
            return rfree[z]

        for i in range(4):
            linear("r", i, gate_r, xr, t_xn)
        t_o = now("dve")
        sync_all()
        top[0] = mark + 8 * 512
        MX = al(8, 512)
        tmp = al(8, 512)
        top_mix = top[0]
        sg = [tmp[:, k, :] for k in range(8)]
        orr = [O[:, k, :] for k in range(8)]
        gsr = [GS[:, k, :] for k in range(8)]
        free = [None] * 8
        for i in range(4):
            held = {}

            def e_z(j, b, t):
                held[j] = act(sg[j % 4], b, ACT.Sigmoid, [t, free[j % 4]])
                return held[j]

            def e_y(j, b, t):
                free[j % 4] = tt(MX[:, j, :], b, sg[j % 4], MUL, [t, held[j]])
                return free[j % 4]

            linear("zg", i, e_z, xr, t_xn)
            linear("og", i, e_y, orr, t_o)
        bgl = vec("b_glu")
        for i in range(4):
            held = {}

            def e_z(j, b, t):
                held[j] = act(sg[j % 2], b, ACT.Sigmoid, [t, free[j % 2]])
                return held[j]

            def e_a(j, b, t):
                free[j % 2] = stt(sg[2 + j % 2], b, bgl[:, j:j + 1], sg[j % 2], ADD, MUL, [t, held[j]])
                return free[j % 2]

            def e_b(j, b, t):
                ta = act(sg[4 + j % 2], b, ACT.Sigmoid, [t, now("dve")], bias=bgl[:, 8 + j:9 + j])
                tt(sg[2 + j % 2], sg[2 + j % 2], sg[4 + j % 2], MUL, ta)
                tt(MX[:, j, :], MX[:, j, :], sg[2 + j % 2], ADD)
                return ta

            linear("zs", i, e_z, xr, t_xn)
            linear("glua", i, e_a, gsr, t_gs)
            linear("glub", i, e_b, gsr, t_gs)
        t_mx = now("dve")
        sync_all()

        def project(name, rhs, w, Z, n=4):
            for i in range(n):
                linear(name, i, lambda j, b, t: cp(Z[:, j, :], b, t, "act"), rhs, w)
            return now("act")

        def add_norm(Z, g, sqb, rs, w):
            t = rms(Z, 8, 512, sqb, rs, w, 1024)
            for k in range(8):
                stt(Z[:, k, :], Z[:, k, :], g[:, k:k + 1], rs, MUL, MUL, t)
                t2 = tt(X[:, k, :], X[:, k, :], Z[:, k, :], ADD)
            return t2

        top[0] = 0
        Z = al(8, 512)
        sq = al(8, 512)
        rs = al(512)
        assert top[0] <= mark + 8 * 512
        t = project("wo", [MX[:, k, :] for k in range(8)], t_mx, Z)
        t_h = add_norm(Z, vec("g_mix_post"), sq, rs, t)
        t = rms(X, 8, 512, sq, rs, t_h, 1024)
        g = vec("g_ffn_pre")
        for k in range(8):
            t_hn = stt(Z[:, k, :], X[:, k, :], g[:, k:k + 1], rs, MUL, MUL, t)
        sync_all()
        H1 = al(32, 512)
        hn = [Z[:, k, :] for k in range(8)]
        adab = al(3, 2048)
        cact = al(8)
        ta = act(cact, vec("c_2"), ACT.Sigmoid)
        t_ca = tt(cact, cact, vec("c_2"), MUL, ta)

        def relu2(j, b, t):
            ta = act(H1[:, j, :], b, ACT.Relu, t)
            act(H1[:, j, :], H1[:, j, :], ACT.Square)
            return ta

        for i in range(16):
            linear("f1", i, relu2, hn, t_hn)
        t_h1 = now("act")
        for i in range(24):
            n, u, tu = unit("ada", i)
            k, q = i // 3, i % 3
            if k == 0:
                t_ada = ts(adab[:, q, :], u, cact[:, 0:1], None, MUL, None, [tu, t_ca])
            else:
                t_ada = stt(adab[:, q, :], u, cact[:, k:k + 1], adab[:, q, :], MUL, ADD, tu)
            release(n, t_ada)
        for i in range(4):
            pair = [take() for _ in range(2)]
            for kg in range(4):
                n, u, tu = unit("f2", 4 * i + kg)
                u = u.rearrange("p (k m) -> p k m", k=8)
                for j, (bi, b, f) in enumerate(pair):
                    t = mm([(b, u[:, k, 128 * j:128 * j + 128], H1[:, 8 * kg + k, :], kg == 0 and k == 0,
                             kg == 3 and k == 7) for k in range(8)], [tu, t_h1, f])
                    if kg == 3:
                        give(bi, cp(Z[:, 2 * i + j, :], b, [t, now("pe")], "act"))
                release(n, t)
        ab = adab.rearrange("p a b -> p (a b)")
        bi, b, f = take()
        tm = mm([(b[:, j:j + 1], ab[:, 128 * j:128 * j + 128], ones[:, 0:1], True, True) for j in range(48)], [t_ada, f])
        give(bi, tt(adat[:, :], b[:, 0:48], vec("ada_b_2"), ADD, tm))
        t_h = add_norm(Z, vec("g_ffn_post"), sq, rs, now("act"))
        sync_all()

        ada = [adat[:, 8 * k:8 * k + 8] for k in range(6)]
        gsc = small[:, 0:16]

        def modulated(dst, g, sh, sc, col, sqb, rs):
            gs = gsc[:, col:col + 8]
            ts(gs, sc, 1.0, None, ADD)
            tt(gs, gs, g, MUL)
            t = rms(X, 8, 512, sqb, rs, now("dve"), 1024)
            for k in range(8):
                t2 = stt(dst[:, k, :], X[:, k, :], gs[:, k:k + 1], rs, MUL, MUL, t)
                t2 = ts(dst[:, k, :], dst[:, k, :], sh[:, k:k + 1], None, ADD)
            return t2

        top[0] = 0
        HB = al(8, 512)
        mark = top[0]
        sq = al(8, 512)
        rs = al(512)
        t_hb = modulated(HB, vec("norm1_g_2"), ada[0], ada[1], 0, sq, rs)
        sync_all()
        top[0] = mark
        rs = al(512)
        LAT = al(5, 512)
        KP = al(2, 512)
        CA = al(4, 512)
        CU = al(4, 542)
        PR = al(512)
        TR = al(2, 512)
        WQ = al(3, 1024)
        MK = al(4, 512)
        pos_f = al(516)
        t_z = zero(CU[:, :, 0:30], barrier())
        t_posr = (ctx.enter_context(nc.semaphore("s_posr")), 32)
        pint = al(516)
        pi32 = pint.bitcast(I32)
        emit("sp", lambda g: g.dma_start(pi32[:, 0:512], posr).then_inc(t_posr[0], 16), barrier(), False)
        emit("sp", lambda g: g.dma_start(pi32[:, 512:516], posc).then_inc(t_posr[0], 16), None, False)
        s_wuq = ctx.enter_context(nc.semaphore("s_wuq"))
        emit("sp", lambda g: g.dma_start(WQ, wuq).then_inc(s_wuq, 16), None, False)
        t_wuq = (s_wuq, 16)
        cp(pos_f, pi32, t_posr)
        ts(PR, pos_f[:, 0:512], con("freq"), None, MUL)
        ts(TR[:, 0, :], PR, 1.0 / (2 * math.pi), MAGIC, MUL, ADD)
        ts(TR[:, 0, :], TR[:, 0, :], -MAGIC, None, ADD)
        for cc in (C1, C2, C3):
            stt(PR, TR[:, 0, :], -cc, PR, MUL, ADD)
        t = ts(PR, PR, PI_IN, -PI_IN, ALU.min, MAX)
        t = sin_cos(TR[:, 1, :], TR[:, 0, :], PR, t)
        t_tr = ts(TR[:, 1, :], TR[:, 1, :], con("sign"), None, MUL, None, t)
        for m in range(4):
            t_mk = ts(MK[:, m, :], pos_f[:, 0:512], pos_f[:, 512 + m:513 + m], BIG, ALU.is_gt, MUL)
        hb = [HB[:, k, :] for k in range(8)]

        def rope(o, b, w):
            tt(KP[64:96, 0, :], b[64:96, :], TR[64:96, 0, :], MUL, [w, t_tr])
            t = tt(KP[64:96, 1, :], b[96:128, :], TR[96:128, 1, :], MUL)
            tt(o, KP[64:96, 0, :], KP[64:96, 1, :], ADD)
            return t

        QH = al(8, 512)
        KH = al(8, 512)
        V2 = al(4, 512)
        kpe = al(512)

        def e_lat(j, b, t):
            if j < 5:
                return cp(LAT[:, j, :], b, t, "act")
            return rope(kpe[64:96, :], b, t)

        for i in range(3):
            linear("lat", i, e_lat, hb, t_hb)
        cp(KH[64:96, :, :], kpe[64:96, :].unsqueeze(1).to_broadcast([32, 8, 512]), now("dve"), "pool")
        t_kpe = now("pool")

        def e_cin(j, b, t):
            if j < 4:
                return cp(CA[:, j, :], b, t, "act")
            o = CU[:, j - 4, 30:542]
            t = act(o, b, ACT.Sigmoid, [t, t_z])
            tt(o, o, CA[:, j - 4, :], MUL, t)
            return t

        for i in range(4):
            linear("cin", i, e_cin, hb, t_hb)
        cw = vec("conv_w_2").rearrange("p (c k) -> p c k", k=31)
        CO = CA
        for c in range(4):
            for k in range(31):
                i = CU[:, c, k:k + 512]
                if k == 0:
                    ts(CO[:, c, :], i, cw[:, c, 0:1], vec("conv_b_2")[:, c:c + 1], MUL, ADD)
                else:
                    t_co = stt(CO[:, c, :], i, cw[:, c, k:k + 1], CO[:, c, :], MUL, ADD)
        sq3 = V2
        t = rms(LAT[:, 0:3, :], 3, 512, sq3, rs, None, 384)
        for k in range(3):
            stt(LAT[:, k, :], LAT[:, k, :], vec("q_norm_g_2")[:, k:k + 1], rs, MUL, MUL, t)
        t = rms(LAT[:, 3:5, :], 2, 512, sq3[:, 2:4, :], rs, now("dve"), 256)
        for k in range(2):
            t_lat = stt(LAT[:, 3 + k, :], LAT[:, 3 + k, :], vec("kv_norm_g_2")[:, k:k + 1], rs, MUL, MUL, t)
        for h in range(8):
            i, b, f = take()
            t = mm([(b, WQ[:, k, 128 * h:128 * h + 128], LAT[:, k, :], k == 0, k == 2) for k in range(3)], [t_lat, t_wuq, f])
            ta = cp(QH[0:64, h, :], b[0:64, :], t, "act")
            give(i, [ta, rope(QH[64:96, h, :], b, t)])
        n, u, tu = unit("kv", 0)
        u = u.rearrange("p (k m) -> p k m", k=2)
        for h in range(8):
            i, b, f = take()
            t = mm([(b[0:64, :], u[:, k, 64 * h:64 * h + 64], LAT[:, 3 + k, :], k == 0, k == 1) for k in range(2)],
                   [tu, t_lat, f])
            give(i, cp(KH[0:64, h, :], b[0:64, :], t, "act"))
        for m in range(4):
            i, b, f = take()
            t = mm([(b, LAT[:, 3 + k, 128 * m:128 * m + 128], u[:, k, 512:1024], k == 0, k == 1) for k in range(2)], [f])
            give(i, cp(V2[:, m, :], b, [t, now("pe")], "act"))
        release(n, t)
        t_qkv = [now("act"), now("dve"), t_kpe]
        AT = al(4, 512)
        PB = al(4, 512)
        PT = LAT
        st = small[:, 16:64]
        scale = 96.0 ** -0.5
        t_pt = None
        for h in range(8):
            t_p = []
            for m in range(4):
                i, b, f = take()
                t = mm([(b, QH[0:96, h, 128 * m:128 * m + 128], KH[0:96, h, :], True, True)], [t_qkv, f])
                p = PB[:, m, :]
                t = stt(p, b, scale, MK[:, m, :], MUL, ADD, [t, t_pt])
                give(i, t)
                mx, sm = st[:, m:m + 1], st[:, 4 + m:5 + m]
                red(mx, p, MAX)
                t = ts(mx, mx, -1.0, None, MUL)
                t = act(p, p, ACT.Exp, t, bias=mx, accum_out=sm)
                recip(sm, sm, t)
                t_p.append(ts(p, p, sm, None, MUL))
            for kb in range(4):
                i, b, f = take()
                t_pt = tr([(b[:, 128 * m:128 * m + 128], PB[:, m, 128 * kb:128 * kb + 128], ident) for m in range(4)], [t_p, f])
                t = cp(PT[:, kb, :], b, [t_pt, now("pe")], "act")
                give(i, t)
            if h % 2 == 0:
                ia, ba, fa = take()
            o = ba[64 * (h % 2):64 * (h % 2) + 64, :]
            t = mm([(o, V2[:, kb, 64 * h:64 * h + 64], PT[:, kb, :], kb == 0, kb == 3) for kb in range(4)], [t, fa])
            if h % 2:
                give(ia, cp(AT[:, h // 2, :], ba, t, "act"))
        t_at = now("act")
        i, b, f = take()
        tm = mm([(b, ones, CO[:, c, :], c == 0, c == 3) for c in range(4)], [t_co, f])
        for c in range(4):
            t = stt(CO[:, c, :], b, -1.0 / 512, CO[:, c, :], MUL, ADD, [tm, now("pe")])
        give(i, t)
        t = rms(CO, 4, 512, PB, rs, [t, t_at], 512)
        for c in range(4):
            tt(CO[:, c, :], CO[:, c, :], rs, MUL, t)
            t2 = ts(CO[:, c, :], CO[:, c, :], vec("conv_ln_g_2")[:, c:c + 1], vec("conv_ln_b_2")[:, c:c + 1], MUL, ADD)
            ta = act(PB[:, c, :], CO[:, c, :], ACT.Sigmoid, t2)
            t_cv = tt(CO[:, c, :], CO[:, c, :], PB[:, c, :], MUL, ta)
        sync_all()
        MX = QH
        sg = [PB[:, k, :] for k in range(4)]
        free = [None] * 4

        def gate_e(j, b, t):
            held[j] = act(sg[j % 4], b, ACT.Sigmoid, [t, free[j % 4]])
            return held[j]

        def branch(gname, oname, src, w, evac):
            for i in range(4):
                linear(gname, i, gate_e, hb, t_hb)
                if i % 2 == 0:
                    n, u, tu = unit(oname, i // 2)
                    u = u.rearrange("p (k m) -> p k m", k=4)
                for jj in range(2):
                    j = 2 * i + jj
                    bi, b, f = take()
                    c = 128 * (j % 4)
                    t = mm([(b, u[:, k, c:c + 128], src[:, k, :], k == 0, k == 3) for k in range(4)], [tu, w, f])
                    give(bi, evac(j, b, t))
                if i % 2:
                    release(n, t)

        held = {}

        def e_ya(j, b, t):
            free[j % 4] = tt(MX[:, j, :], b, sg[j % 4], MUL, [t, held[j]])
            return free[j % 4]

        def e_yc(j, b, t):
            t1 = tt(sg[j % 4], b, sg[j % 4], MUL, [t, held[j]])
            free[j % 4] = tt(MX[:, j, :], MX[:, j, :], sg[j % 4], ADD)
            return t1

        branch("ga", "oa", AT, t_at, e_ya)
        branch("gc", "oc", CO, t_cv, e_yc)
        t_mx = now("dve")
        for i in range(4):
            linear("wo2", i, lambda j, b, t: stt(X[:, j, :], b, ada[2][:, j:j + 1], X[:, j, :], MUL, ADD, t),
                   [MX[:, k, :] for k in range(8)], t_mx)
        sync_all()

        top[0] = 0
        HB = al(8, 512)
        hb = [HB[:, k, :] for k in range(8)]
        rs = al(512)
        CT = al(512)
        SEL = al(32, 128)
        RW = al(8, 36)
        s_rw = ctx.enter_context(nc.semaphore("s_rw"))
        emit("sp", lambda g: g.dma_start(RW, rw).then_inc(s_rw, 16), barrier(), False)
        emit("sp", lambda g: g.dma_start(SEL[0:32], sel).then_inc(s_rw, 16), None, False)
        HID = al(32, 512)
        t_hb = modulated(HB, vec("norm2_g_2"), ada[3], ada[4], 8, HID[:, 0:8, :], rs)
        i, b, f = take()
        t = mm([(b[:, 36 * m:36 * m + 36], HB[:, k, 128 * m:128 * m + 128], RW[:, k, :], k == 0, k == 7)
                for m in range(4) for k in range(8)], [t_hb, (s_rw, 32), f])
        L = al(4, 36)
        rbv = vec("rb").unsqueeze(1).to_broadcast([128, 4, 36])
        t = tt(L, b[:, 0:144].rearrange("p (m c) -> p m c", m=4), rbv, ADD, t)
        give(i, t)
        LG = L[:, :, 0:4]

        def bc(a, n):
            return a.unsqueeze(2).to_broadcast([128, 4, n])

        def first_max(oh, v, m, n, rev):
            ts_eq = tt(oh, v, bc(m, n), ALU.is_equal)
            tt(oh, oh, rev.unsqueeze(1).to_broadcast([128, 4, n]), MUL)
            red(km, oh, MAX)
            return tt(oh, oh, bc(km, n), ALU.is_equal)

        gm, km, sg_, gv, m1, m2, sw_ = [al(4) for _ in range(7)]
        og_, eg = al(4, 4), al(4, 4)
        es, es2, exx, o1, o2, wn = [al(4, 8) for _ in range(6)]
        tmp4 = al(4, 8, 4)
        CB = al(4, 4, 8)
        red(gm, LG, MAX)
        t = tt(eg, LG, bc(gm, 4), SUB)
        t = act(eg, eg, ACT.Exp, t)
        red(sg_, eg, ADD, t)
        recip(gv, sg_)
        first_max(og_, LG, gm, 4, con("rev4"))
        LE = L[:, :, 4:36].rearrange("p m (g e) -> p m e g", g=4)
        tt(tmp4, LE, og_.unsqueeze(2).to_broadcast([128, 4, 8, 4]), MUL)
        red(es, tmp4, ADD)
        red(m1, es, MAX)
        t = tt(exx, es, bc(m1, 8), SUB)
        t = act(exx, exx, ACT.Exp, t)
        first_max(o1, es, m1, 8, con("rev8"))
        stt(es2, o1, BIG, es, MUL, ADD)
        red(m2, es2, MAX)
        first_max(o2, es2, m2, 8, con("rev8"))
        tt(o1, o1, o2, ADD)
        tt(wn, exx, o1, MUL, t)
        red(sw_, wn, ADD)
        recip(sw_, sw_)
        tt(sw_, sw_, gv, MUL)
        tt(wn, wn, bc(sw_, 8), MUL)
        t = tt(CB, og_.unsqueeze(3).to_broadcast([128, 4, 4, 8]), wn.unsqueeze(2).to_broadcast([128, 4, 4, 8]), MUL)
        i, b, f = take()
        t = tr([(b[0:32, 128 * m:128 * m + 128], CB[:, m].rearrange("p g e -> p (g e)"), ident) for m in range(4)], [t, f])
        t_ct = cp(CT[0:32, :], b[0:32, :], t)
        give(i, t_ct)
        sgm = [al(512) for _ in range(2)]
        prd = [al(512) for _ in range(2)]
        ef = [None, None]
        for e in range(32):
            z = e % 2
            n, u, tu = unit("ex", e)
            u = u.rearrange("p (a k m) -> p a k m", a=2, k=8)
            (ia, a, fa), (iu, b, fu), (ic, c, fc) = take(), take(), take()
            ta = mm([(a, u[:, 0, k, :], hb[k], k == 0, k == 7) for k in range(8)], [tu, t_hb, fa])
            tb = mm([(b, u[:, 1, k, :], hb[k], k == 0, k == 7) for k in range(8)], [fu])
            release(n, tb)
            tc = mm([(c, SEL[0:32, e, :], CT[0:32, :], True, True)], [t_ct, fc])
            t = act(sgm[z], a, ACT.Sigmoid, [ta, ef[z]])
            t = tt(prd[z], a, sgm[z], MUL, t)
            give(ia, t)
            t = tt(prd[z], b, prd[z], MUL, tb)
            give(iu, t)
            ef[z] = t_hid = tt(HID[:, e, :], c, prd[z], MUL, tc)
            give(ic, t_hid)
        ac = [take() for _ in range(8)]
        for e2 in range(16):
            n, u, tu = unit("dn", e2)
            u = u.rearrange("p (a m) -> p a m", a=2)
            for a in range(2):
                e = 2 * e2 + a
                for j, (i, b, f) in enumerate(ac):
                    t = mm([(b, u[:, a, 128 * j:128 * j + 128], HID[:, e, :], e == 0, e == 31)], [tu, t_hid, f])
            release(n, t)
        for j, (i, b, f) in enumerate(ac):
            t = stt(X[:, j, :], b, ada[5][:, j:j + 1], X[:, j, :], MUL, ADD, t if j == 0 else None)
            give(i, t)
        t = rms(X, 8, 512, HID[:, 0:8, :], rs, [t, now("pe")], 1024)
        g = vec("final_norm_g_2")
        for k in range(8):
            t = stt(HB[:, k, :], X[:, k, :], g[:, k:k + 1], rs, MUL, MUL, [t, now("pe")])
            if k % 2:
                emit("sp", lambda g, k=k: g.dma_start(out[:, k - 1:k + 1, :], HB[:, k - 1:k + 1, :]).then_inc(s_out, 16), t, False)
        emit("sp", None, [(s_out, 64)], False)
        assert upos[0] == NU

        block = ctx.enter_context(nc.Block())

        def play(e, g):
            seen = {}
            for w, fn, inc in queue[e]:
                for s, v in w:
                    if v > seen.get(s.name, 0):
                        g.wait_ge(s, v)
                        seen[s.name] = v
                if fn is not None:
                    ins = fn(g)
                    if inc:
                        ins.then_inc(sem[e], 1)

        @block.tensor
        def _(g):
            play("pe", g)

        @block.scalar
        def _(g):
            play("act", g)

        @block.vector
        def _(g):
            play("dve", g)

        @block.gpsimd
        def _(g):
            play("pool", g)

        @block.sync
        def _(g):
            play("sp", g)


def lay(w, n):
    K, N = w.shape
    return w.reshape(K // 128, 128, N // n, n).transpose(2, 1, 0, 3).reshape(N // n, 128, K // 128 * n)


def constants():
    c = {}
    c["ident"] = np.eye(128)
    c["ones"] = np.ones((128, 128))
    j, i = np.arange(128)[:, None], np.arange(128)[None, :]
    c["tril"] = (j // 64 == i // 64) & (j <= i)
    t = np.arange(NT)
    c["reset"] = np.broadcast_to(((t != 0) & ((t < 16) | ((t - 16) % 64 != 0))), (128, NT))
    p = np.arange(128)
    freq = np.float32(10000.0) ** (-np.arange(0, 32, 2, dtype=np.float32) / np.float32(32))
    c["freq"] = freq[p % 16][:, None]
    c["sign"] = np.where(p % 32 < 16, -1.0, 1.0)[:, None]
    c["rev4"] = np.broadcast_to(np.arange(4, 0, -1), (128, 4))
    c["rev8"] = np.broadcast_to(np.arange(8, 0, -1), (128, 8))
    s = np.zeros((32, 32, 128), np.float32)
    s[np.arange(32), np.arange(32), :] = 1.0
    return np.concatenate([c[n] for n, _ in CST], axis=1).astype(np.float32), s


def layout(a):
    def col(v):
        v = v.reshape(-1)
        return v.reshape(-1, 128).T

    w = a["w_in"][0]
    parts = {
        "u": lay(w[:, 3088:4112], 256), "k": lay(w[:, 512:1024], 256), "q": lay(w[:, 0:512], 256),
        "v": np.stack([w[512 * kg:512 * kg + 512, 1024 + 512 * hf:1536 + 512 * hf].reshape(4, 128, 512)
                       .transpose(1, 0, 2).reshape(128, 2048) for hf in range(2) for kg in range(2)]),
        "r": lay(w[:, 2048:3072], 256), "zg": lay(w[:, 4112:5136], 256), "zs": lay(w[:, 5136:6160], 256),
        "og": lay(a["w_o_gla"][0], 256),
        "glua": lay(a["w_glu"][0][:, 0:1024], 256), "glub": lay(a["w_glu"][0][:, 1024:2048], 256),
        "wo": lay(a["w_out"][0], 256), "f1": lay(a["w_ff1"][0], 256),
        "f2": a["w_ff2"][0].reshape(4, 8, 128, 4, 256).transpose(3, 0, 2, 1, 4).reshape(16, 128, 2048),
        "ada": a["ada_w_2"][0].reshape(8, 128, 3, 2048).transpose(0, 2, 1, 3).reshape(24, 128, 2048),
    }
    w = a["w_in_2"][0]
    kr = w[:, 640:672]
    ks = np.concatenate([kr[:, 16:32], kr[:, 0:16]], axis=1)
    parts["lat"] = lay(np.concatenate([w[:, 0:640], kr, ks, kr, ks], axis=1), 256)
    parts["cin"] = lay(w[:, 672:1696], 256)
    parts["ga"], parts["gc"] = lay(w[:, 1696:2720], 256), lay(w[:, 2720:3744], 256)
    kv = a["w_ukv_2"][0].reshape(256, 8, 128)
    parts["kv"] = lay(np.concatenate([kv[:, :, 0:64].reshape(256, 512), kv[:, :, 64:128].reshape(256, 512)], axis=1), 1024)
    parts["oa"], parts["oc"] = lay(a["w_o_attn_2"][0], 512), lay(a["w_conv_out_2"][0], 512)
    parts["wo2"] = lay(a["w_out_2"][0], 256)
    eg, eu = [a[n][0].reshape(32, 8, 128, 128).transpose(0, 2, 1, 3) for n in ("expert_w_gate_2", "expert_w_up_2")]
    parts["ex"] = np.stack([eg, eu], axis=2).reshape(32, 128, 2048)
    parts["dn"] = a["expert_w_down_2"][0].reshape(16, 2, 128, 1024).transpose(0, 2, 1, 3).reshape(16, 128, 2048)
    W = np.stack([parts[n][i] for n, i in PLAN])

    two = lambda v: v.reshape(32, 128).T
    v = {n: col(a[n]) for n, _ in VEC if n in a and n not in ("a_re", "a_im", "log_step", "conv_w_2")}
    v["conv_w_2"] = a["conv_w_2"][0].reshape(31, 4, 128).transpose(2, 1, 0).reshape(128, 124)
    v["a_re"], v["a_im"] = two(a["a_re"][0]), two(a["a_im"][0])
    v["log_step"] = two(np.broadcast_to(a["log_step"][0][:, None], (64, 64)))
    rb = np.concatenate([a["router_group_b_2"][0], a["router_expert_b_2"][0]])
    v["rb"] = np.broadcast_to(rb, (128, 36))
    vecs = np.concatenate([v[n] for n, _ in VEC], axis=1)
    cst, sel = constants()
    b3 = lambda t: t.reshape(32, 128, 16).transpose(1, 0, 2).reshape(128, 512)
    c3 = lambda t: b3(t.transpose(0, 2, 1))
    bc = np.stack([b3(a["b_re"][0]), b3(a["b_im"][0]), c3(a["c_re"][0]), c3(a["c_im"][0])], axis=1)
    xT = np.concatenate([a["meta_tokens"], a["x"][0]], axis=0).T.reshape(8, 128, NT).transpose(1, 0, 2)
    q = a["w_uq_2"][0].reshape(384, 8, 96)
    q = np.concatenate([q, q[:, :, 80:96], q[:, :, 64:80]], axis=2).reshape(384, 1024)
    rw = np.concatenate([a["router_group_w_2"][0], a["router_expert_w_2"][0]], axis=1)
    pos = a["positions_2"].reshape(512)
    three = lambda w: w.reshape(-1, 128, w.shape[1]).transpose(1, 0, 2)
    return {"W": W, "vecs": vecs, "cst": cst, "xT": xT, "wal": three(a["w_in"][0][:, 3072:3088]),
            "wgu": a["w_gate_up"][0], "wuq": three(q), "bc": bc, "rw": three(rw), "sel": sel,
            "posr": np.broadcast_to(pos, (128, 512)), "posc": pos.reshape(4, 128).T}


def kernel(**inputs):
    import concourse.bacc as _bacc
    from concourse.bass_utils import run_bass_kernel_spmd as _run

    arrays = {k: np.ascontiguousarray(v) for k, v in layout({k: np.asarray(v) for k, v in inputs.items()}).items()}
    nc = _bacc.Bacc("TRN2", target_bir_lowering=False, num_devices=1)
    args = {k: nc.dram_tensor(f"in_{k}", v.shape, mybir.dt.from_np(v.dtype), kind="ExternalInput").ap()
            for k, v in arrays.items()}
    args["out"] = nc.dram_tensor("out_T", (128, 8, 512), F32, kind="ExternalOutput").ap()
    program(nc, **args)
    r = _run(nc, [{f"in_{k}": v for k, v in arrays.items()}], core_ids=[0])
    got = r.results[0]["out_T"]
    return np.ascontiguousarray(got.transpose(2, 1, 0).reshape(1, 512, 1024))
```

```python
from contextlib import ExitStack
import math

import numpy as np
import concourse.bass as bass
from concourse import mybir

F32 = mybir.dt.float32
I32 = mybir.dt.int32
U32 = mybir.dt.uint32
F32R = mybir.dt.float32r
BF16 = mybir.dt.bfloat16
ALU = mybir.AluOpType
ACT = mybir.ActivationFunctionType
AX = mybir.AxisListType.X
EPS = 1e-6
NT = 528
RING = 3
MAGIC = 12582912.0
C1, C2, C3 = 6.28125, 0.0019350051879882812, 3.0199159819e-07
PI_IN = 3.1415925
BIG = -3.0e38

VEC = [("g_mix_pre", 8), ("b_gate", 4), ("gla_norm_g", 8), ("d_skip", 8), ("b_glu", 16), ("g_mix_post", 8),
       ("g_ffn_pre", 8), ("g_ffn_post", 8), ("c_2", 8), ("ada_b_2", 48), ("norm1_g_2", 8), ("norm2_g_2", 8),
       ("q_norm_g_2", 3), ("kv_norm_g_2", 2), ("conv_b_2", 4), ("conv_ln_g_2", 4), ("conv_ln_b_2", 4),
       ("final_norm_g_2", 8), ("conv_w_2", 124), ("a_re", 32), ("a_im", 32), ("log_step", 32), ("rb", 36)]
VOFF, _o = {}, 0
for _n, _c in VEC:
    VOFF[_n] = (_o, _c)
    _o += _c
NVEC = _o
CST = [("ident", 128), ("ones", 128), ("tril", 128), ("reset", NT), ("freq", 1), ("sign", 1), ("eps", 1), ("rev4", 4), ("rev8", 8)]
COFF, _o = {}, 0
for _n, _c in CST:
    COFF[_n] = (_o, _c)
    _o += _c
NCST = _o
PLAN = ([("k", i) for i in range(2)] + [("v", i) for i in range(4)] + [("q", i) for i in range(2)]
        + [("u", i) for i in range(4)] + [("r", i) for i in range(4)] + [("zg", i) for i in range(4)]
        + [("og", i) for i in range(4)])
for _j in range(4):
    PLAN += [("zs", _j), ("glua", _j), ("glub", _j)]
PLAN += [("wo", i) for i in range(4)]
_a = 0
for _h in range(2):
    for _i in range(16):
        PLAN.append(("f1", 8 * _h + _i) if _i < 8 else ("f2", 8 * _h + _i - 8))
        if _i % 4 != 3:
            PLAN.append(("ada", _a))
            _a += 1
PLAN += [("lat", i) for i in range(3)] + [("cin", i) for i in range(4)]
PLAN += [("ga", i) for i in range(4)] + [("gc", i) for i in range(4)]
PLAN += [("uq", 0), ("uq", 1), ("kv", 0), ("oa", 0), ("oa", 1), ("oc", 0), ("oc", 1)] + [("wo2", i) for i in range(4)]
NU = len(PLAN)
WHOLE = ("ada",)
NB = 7
COLS = [("ex", i) for i in range(8)] + [("dn", i) for i in range(4)]
STREAM = []
for _n in range(NB):
    for _p in range(4):
        STREAM += [(_n, "ex", 2 * _p), (_n, "ex", 2 * _p + 1)]
        if _n or _p:
            STREAM.append((_n, "dn", _p - 1) if _p else (_n - 1, "dn", 3))
STREAM.append((NB - 1, "dn", 3))
ROW = 1024 + 8
MC = 128 + 2 * 12 + NB


def program(nc, W, wmoe, mcst, vecs, cst, xT, wal, wgu, bc, rw, posr, posc, xslot, yslot, out):
    ctx = ExitStack()
    with ctx:
        def sbt(name, shape, dt=F32):
            return ctx.enter_context(nc.sbuf_tensor(name, shape, dt))

        def semaphore(name):
            return ctx.enter_context(nc.semaphore(name))

        ENG = ["pe", "act", "dve", "pool", "sp"]
        sem = {e: semaphore("s_" + e) for e in ENG}
        s_ring = [semaphore(f"s_ring{i}") for i in range(RING)]
        s_gat = [semaphore(f"s_gat{i}") for i in range(5)]
        s_xs = [semaphore(f"s_xs{i}") for i in range(2)]
        s_clear, s_scat, s_y, s_back, s_out = [semaphore("s_" + n) for n in ("clear", "scat", "y", "back", "out")]
        queue = {e: [] for e in ENG}
        count = {e: 0 for e in ENG}

        def flat(w):
            if w is None:
                return []
            if isinstance(w, tuple):
                return [w]
            return [t for x in w for t in flat(x)]

        def emit(e, fn, w=None, inc=True):
            queue[e].append((flat(w), fn, inc))
            if inc:
                count[e] += 1
            return (sem[e], count[e])

        def now(e):
            return (sem[e], count[e])

        def step(e, fn, w=None):
            return emit(e, fn, [now(e), flat(w)])

        def act(o, i, f, w=None, **kw):
            return step("act", lambda g: g.activation(o, i, f, **kw), w)

        def tt(o, a, b, op, w=None, e="dve"):
            return step(e, lambda g: g.tensor_tensor(o, a, b, op), w)

        def ts(o, a, s1, s2, op0, op1=None, w=None, e="dve"):
            if op1 is None:
                return step(e, lambda g: g.tensor_scalar(o, a, s1, None, op0), w)
            return step(e, lambda g: g.tensor_scalar(o, a, s1, s2, op0, op1), w)

        def stt(o, a, s, b, op0, op1, w=None):
            return step("dve", lambda g: g.scalar_tensor_tensor(out=o, in0=a, scalar=s, in1=b, op0=op0, op1=op1), w)

        def cp(o, i, w=None, e="dve"):
            if e == "act":
                return act(o, i, ACT.Copy, w)
            return step(e, lambda g: g.tensor_copy(o, i), w)

        def red(o, i, op, w=None):
            return step("dve", lambda g: g.tensor_reduce(o, i, AX, op), w)

        def recip(o, i, w=None):
            return step("dve", lambda g: g.reciprocal(o, i), w)

        def zero(o, w=None, e="pool"):
            return step(e, lambda g: g.memset(o, 0.0), w)

        MUL, ADD, SUB, MAX = ALU.mult, ALU.add, ALU.subtract, ALU.max

        def mm(group, w=None):
            for n, (o, l, r, st, sp, *own) in enumerate(group):
                t = emit("pe", lambda g, o=o, l=l, r=r, st=st, sp=sp: g.matmul(
                    o, l, r, start=st, stop=sp, skip_group_check=True), [flat(w) if n == 0 else [], flat(own)],
                    n == len(group) - 1)
            return t

        def mm3(o, ls, rs, first=True, last=True, w=None):
            n = len(ls)
            out = []
            for k, ((lh, ll), (rh, rl)) in enumerate(zip(ls, rs)):
                out += [(o, lh, rh, first and k == 0, False, w[k] if w else None), (o, lh, rl, False, False),
                        (o, ll, rh, False, last and k == n - 1)]
            return out

        def tr(group, w=None):
            w = flat(w)
            for n, (o, i, idt) in enumerate(group):
                t = emit("pe", lambda g, o=o, i=i, idt=idt: g.transpose(o, i, idt), w if n == 0 else None,
                         n == len(group) - 1)
            return t

        banks = [ctx.enter_context(nc.psum_tensor(f"bank{i}", [128, 512], F32)) for i in range(8)]
        bfree = [None] * 8
        bnext = [0]

        def take():
            i = next(j % 8 for j in range(bnext[0], bnext[0] + 8) if bfree[j % 8] != "held")
            bnext[0] = i + 1
            f, bfree[i] = bfree[i], "held"
            return i, banks[i][:, :], f

        def give(i, t):
            bfree[i] = flat(t)

        ringt = sbt("ring", [128, RING, 2048])
        wst = sbt("wsplit", [128, 2, 2, 2048], F32R)
        wfree = [None, None]
        nsplit = [0]
        upos = [0]
        low = ["dve"]
        ready = {}

        def load_unit(n, w):
            s = n % RING
            emit("sp", lambda g: g.dma_start(ringt[:, s, :], W[n]).then_inc(s_ring[s], 16), w, False)

        def landed(n):
            return (s_ring[n % RING], 16 * (n // RING + 1))

        ring_read = [None] * RING

        def release(n, t):
            ring_read[n % RING] = t
            if n + RING < NU:
                load_unit(n + RING, t)

        def split_unit(n):
            z = nsplit[0] % 2
            nsplit[0] += 1
            r = ringt[:, n % RING, :]
            t = act(wst[:, z, 0, :], r, ACT.Copy, [landed(n), wfree[z]])
            t = tt(wst[:, z, 1, :], r, wst[:, z, 0, :].bitcast(F32), SUB, t, low[0])
            release(n, t)
            ready[n] = (z, t)

        def unit(name, i):
            n = upos[0]
            assert PLAN[n] == (name, i), (PLAN[n], name, i)
            upos[0] += 1
            if name in WHOLE:
                return n, ringt[:, n % RING, :], landed(n)
            if n not in ready:
                split_unit(n)
            m = n + 1
            while m < NU and PLAN[m][0] in WHOLE and m < n + RING - 1:
                m += 1
            if m < NU and PLAN[m][0] not in WHOLE and m not in ready:
                split_unit(m)
            z, t = ready[n]
            return z, wst[:, z], t

        def used(z, t):
            wfree[z] = t

        vt = sbt("vecs", [128, NVEC])
        ct = sbt("cst", [128, NCST])
        adat = sbt("adat", [128, 48])
        small = sbt("small", [128, 64])
        base = (nc.sbuf_base + 31) // 32 * 32
        ARENA = (nc.sbuf_top - base) // 32 * 8
        names = [0]

        def place(at, n, dt):
            names[0] += 1
            return nc.alloc_sbuf_tensor_at(f"a{names[0]}", [128, n], dt, offset=base + 4 * at)[:, :]

        spans = []

        def barrier():
            return [now(e) for e in ("pe", "act", "dve", "pool")]

        freed = []

        def al(*dims, dt=F32, by=("act", "dve", "pool", "pe", "sp"), top=False):
            size = int(np.prod(dims))
            n = (size + 7) // 8 * 8
            if top:
                at = ARENA - n
                for o, k in sorted(spans, reverse=True):
                    if at >= o + k:
                        break
                    at = min(at, o - n)
            else:
                at = 0
                for o, k in sorted(spans):
                    if o - at >= n:
                        break
                    at = max(at, o + k)
            assert 0 <= at and at + n <= ARENA, (n, sorted(spans))
            spans.append((at, n))
            for o, k, t in freed:
                if o < at + n and at < o + k:
                    for e in by:
                        queue[e].append((t, None, False))
            a = place(at, size, dt)
            if len(dims) == 2:
                a = a.rearrange("p (a b) -> p a b", b=dims[1])
            if len(dims) == 3:
                a = a.rearrange("p (a b c) -> p a b c", b=dims[1], c=dims[2])
            where[id(a)] = (at, n, a)
            return a

        where = {}

        def high_low(a):
            o, n, _ = where[id(a)]
            return place(o, int(np.prod(a.shape[1:])), F32R).rearrange("p (a b) -> p a b", b=a.shape[2])

        def drop(*aps, w=None):
            t = flat([barrier(), flat(w)])
            for a in aps:
                o, n, _ = where.pop(id(a))
                spans.remove((o, n))
                freed.append((o, n, t))

        def vec(name):
            o, n = VOFF[name]
            return vt[:, o:o + n]

        def con(name):
            o, n = COFF[name]
            return ct[:, o:o + n]

        n_ld = [0]

        def ld(o, i, w=None):
            s = semaphore(f"s_ld{n_ld[0]}")
            n_ld[0] += 1
            emit("sp", lambda g: g.dma_start(o, i).then_inc(s, 16), w, False)
            return (s, 16)

        ident, ones = con("ident"), con("ones")

        t_v = ld(vt[:, :], vecs)
        t_c = ld(ct[:, :], cst)
        HT = al(8, NT)
        t_x = [ld(HT[:, 2 * i:2 * i + 2, :], xT[:, 2 * i:2 * i + 2, :]) for i in range(4)]
        walt = al(8, 16)
        t_wal = ld(walt, wal)
        wgut = al(512)
        t_wgu = ld(wgut[0:16, :], wgu)
        for n in range(RING):
            load_unit(n, None)

        def split(pair, src, w=None, e="dve"):
            t = act(pair[0], src, ACT.Copy, w)
            return tt(pair[1], src, pair[0].bitcast(F32), SUB, t, e)

        def sum_squares(acc, src, tmp, first, w=None):
            if first:
                return act(acc, src, ACT.Square, w)
            t = act(tmp, src, ACT.Square, [flat(w), now("dve")])
            return tt(acc, acc, tmp, ADD, t)

        def over_partitions(acc, rstd, t, dim):
            i, b, f = take()
            b = b[:, 0:acc.shape[1]]
            tm = mm([(b, ones, acc, True, True)], [t, t_c, f])
            return root(i, b, rstd, tm, dim)

        def root(i, b, rstd, tm, dim):
            t = act(rstd, b, ACT.Sqrt, [tm, t_c, now("dve")], scale=1.0 / dim, bias=con("eps"))
            give(i, t)
            return recip(rstd, rstd, t)

        def split_all(n, value, high, lower, eng=("dve", "pool")):
            t, out = [], []
            for k in range(n + 1):
                if k < n:
                    t.append(high(k, value(k)))
                if k:
                    out.append(lower(k - 1, t[k - 1], eng[(k - 1) % len(eng)]))
            return out

        def halves_of(h, l, src):
            return (lambda k, t: act(h[:, k, :], src[:, k, :], ACT.Copy, t),
                    lambda k, t, e: tt(l[:, k, :], src[:, k, :], h[:, k, :].bitcast(F32), SUB, t, e))

        def rms(src, n, acc, tmp, rstd, w, dim):
            for k in range(n):
                t = sum_squares(acc, src[:, k, :], tmp[:, k % 2, :], k == 0, w)
            return over_partitions(acc, rstd, t, dim)

        xnh, xnl = al(8, NT, dt=F32R), al(8, NT, dt=F32R)
        sq = al(4, NT)
        rst = al(NT)
        (ia, ba, _), (ib, bb, _) = take(), take()
        tp = []
        for k in range(8):
            t = act(sq[:, k % 4, :], HT[:, k, :], ACT.Square, [t_x[k // 2], tp[k - 4] if k > 3 else None])
            tp.append(mm([(ba, ones, sq[:, k % 4, 0:512], k == 0, k == 7),
                          (bb[:, 0:16], ones, sq[:, k % 4, 512:NT], k == 0, k == 7)], [t, t_c]))
        root(ib, bb[:, 0:16], rst[:, 512:NT], tp[7], 1024)
        t_r = root(ia, ba, rst[:, 0:512], tp[7], 1024)
        g = vec("g_mix_pre")
        t_xn = split_all(8, lambda k: stt(HT[:, k, :], HT[:, k, :], g[:, k:k + 1], rst, MUL, MUL, [t_r, t_v]),
                         *halves_of(xnh, xnl, HT))
        walh, wall = al(8, 16, dt=F32R), al(8, 16, dt=F32R)
        t_wal = split((walh, wall), walt, t_wal)
        drop(HT, sq, rst, walt)

        def pairs(h, l, lo=0, hi=512, n=8):
            return [(h[:, k, lo:hi], l[:, k, lo:hi]) for k in range(n)]

        xr = pairs(xnh, xnl, 16, NT)
        halves = [(0, 264, pairs(xnh, xnl, 0, 264)), (264, NT, pairs(xnh, xnl, 264, NT))]

        def linear(name, i, evac, rhs, w, nk=8, n=2048):
            z, u, tu = unit(name, i)
            u = u[:, :, 0:n].rearrange("p a (k m) -> p a k m", k=nk)
            per = u.shape[3] // 128
            wk = w if isinstance(w, list) and len(w) == nk else None
            w = None if wk else w
            for j in range(per):
                ls = [(u[:, 0, k, j * 128:(j + 1) * 128], u[:, 1, k, j * 128:(j + 1) * 128]) for k in range(nk)]
                for part in (rhs if isinstance(rhs[0][0], int) else [(None, None, rhs)]):
                    lo, hi, r = part
                    bi, b, f = take()
                    if lo is None:
                        t = mm(mm3(b, ls, r, w=wk), [tu, w, f])
                        give(bi, evac(per * i + j, b, t))
                    else:
                        t = mm(mm3(b[:, 0:hi - lo], ls, r, w=wk), [tu, w, f])
                        give(bi, evac(per * i + j, b[:, 0:hi - lo], t, lo, hi))
            used(z, t)

        zt = al(ROW, top=True)
        t_zt = zero(zt)
        for b_ in range(NB):
            emit("sp", lambda g, b_=b_: g.dma_start(xslot[128 * b_:128 * b_ + 128, :], zt).then_inc(s_clear, 16), t_zt, False)
        drop(zt, w=(s_clear, 16 * NB))

        def reduce_angle(r, th, n, w=None):
            ts(n, th, 1.0 / (2 * math.pi), MAGIC, MUL, ADD, w)
            ts(n, n, -MAGIC, None, ADD)
            stt(r, n, -C1, th, MUL, ADD)
            stt(r, n, -C2, r, MUL, ADD)
            stt(r, n, -C3, r, MUL, ADD)
            return ts(r, r, PI_IN, -PI_IN, ALU.min, MAX)

        def sin_cos(s, c, r, w):
            act(s, r, ACT.Sin, w)
            t = act(c, r, ACT.Abs)
            t = ts(c, c, -1.0, math.pi / 2, MUL, ADD, t)
            return act(c, c, ACT.Sin, t)

        K = al(4, NT)
        LA = al(4, NT)
        PW = al(9, 2, 32)
        NPW = al(9, 32)
        L8i = al(2, 32)
        P32 = al(11, 32)
        dt_, mag, th, nn, si, co, fr, fi, q1, q2, zr = [P32[:, k, :] for k in range(11)]
        ar, ai, ls = vec("a_re"), vec("a_im"), vec("log_step")

        def ssm_parameters():
            t = act(dt_, ls, ACT.Exp, t_v)
            t = tt(mag, ar, dt_, MUL, t)
            ta = act(mag, mag, ACT.Exp, t)
            tt(th, ai, dt_, MUL)
            t = reduce_angle(q1, th, nn)
            t = sin_cos(si, co, q1, [t, ta])
            lr, li = PW[:, 1, 0, :], PW[:, 1, 1, :]
            step("dve", lambda g: g.memset(PW[:, 0, 0, :], 1.0))
            step("dve", lambda g: g.memset(PW[:, 0, 1, :], 0.0))
            tt(lr, mag, co, MUL, t)
            tt(li, mag, si, MUL)
            for s in range(1, 8):
                a, b = PW[:, s, 0, :], PW[:, s, 1, :]
                tt(q1, a, lr, MUL)
                tt(q2, b, li, MUL)
                tt(PW[:, s + 1, 0, :], q1, q2, SUB)
                tt(q1, a, li, MUL)
                tt(q2, b, lr, MUL)
                tt(PW[:, s + 1, 1, :], q1, q2, ADD)
            ts(NPW, PW[:, :, 0, :], -1.0, None, MUL)
            ts(L8i[:, 0, :], PW[:, 8, 1, :], -1.0, None, MUL)
            cp(L8i[:, 1, :], PW[:, 8, 1, :])
            ts(zr, lr, -1.0, None, ADD)
            tt(q1, ar, ar, MUL)
            tt(q2, ai, ai, MUL)
            tt(q1, q1, q2, ADD)
            recip(nn, q1)
            tt(q1, zr, ar, MUL)
            tt(q2, li, ai, MUL)
            tt(q1, q1, q2, ADD)
            tt(fr, q1, nn, MUL)
            tt(q1, li, ar, MUL)
            tt(q2, zr, ai, MUL)
            tt(q1, q1, q2, SUB)
            return tt(fi, q1, nn, MUL)


        def to_k(j, b, t, lo, hi):
            return cp(K[:, j, lo:hi], b, t, "act")

        for i in range(2):
            linear("k", i, to_k, halves, t_xn)
        alow = al(NT)
        e1 = al(4, NT)
        for lo, hi, r in halves:
            i, b, f = take()
            t = mm(mm3(b[0:16, 0:hi - lo], [(walh[:, k, :], wall[:, k, :]) for k in range(8)], r), [t_wal, f])
            t_al = cp(alow[0:16, lo:hi], b[0:16, 0:hi - lo], t)
            give(i, t_al)
        bg = vec("b_gate")

        def log_gate():
            for h in range(4):
                for lo, hi in ((0, 264), (264, NT)):
                    i, b, f = take()
                    b = b[:, 0:hi - lo]
                    tm = mm([(b, wgut[0:16, 128 * h:128 * h + 128], alow[0:16, lo:hi], True, True)], [t_al, t_wgu, f])
                    tb = act(e1[:, h, lo:hi], b, ACT.Abs, tm, bias=bg[:, h:h + 1])
                    give(i, ts(LA[:, h, lo:hi], b, bg[:, h:h + 1], 0.0, ADD, ALU.min, tb))
            for h in range(4):
                act(e1[:, h, :], e1[:, h, :], ACT.Exp, scale=-1.0)
            for h in range(4):
                ta = act(e1[:, h, :], e1[:, h, :], ACT.Ln, bias=1.0)
                t = tt(LA[:, h, :], LA[:, h, :], e1[:, h, :], SUB, ta)
            return t

        Q = al(4, 512)
        VV = al(4, 1024)
        VM = al(1024)
        for half in range(2):
            bb_ = [take() for _ in range(5)]
            for kg in range(2):
                z, u, tu = unit("v", 2 * half + kg)
                u = u.rearrange("p a (k m) -> p a k m", k=4)
                rs = [(u[:, 0, k, :], u[:, 1, k, :]) for k in range(4)]
                for m, (i, b, f) in enumerate(bb_):
                    lo, hi = (16 + 128 * m, 144 + 128 * m) if m < 4 else (0, 16)
                    b = b if m < 4 else b[0:16, :]
                    t = mm(mm3(b, pairs(xnh, xnl, lo, hi)[4 * kg:4 * kg + 4], rs, kg == 0, kg == 1), [tu, t_xn, f])
                    if kg == 1:
                        o = VV[:, m, 512 * half:512 * half + 512] if m < 4 else VM[0:16, 512 * half:512 * half + 512]
                        give(i, cp(o, b, t, "act"))
                used(z, t)
            if half == 0:
                t_la = log_gate()
        ssm_parameters()
        drop(alow, walh, wall, wgut, e1)
        for i in range(2):
            linear("q", i, lambda j, b, t: act(Q[:, j, :], b, ACT.Copy, t, scale=128.0 ** -0.5), xr, t_xn)
        t_kv = now("act")

        U = al(8, NT)
        O = al(8, 512)
        ex = al(3, NT)
        QK = al(4, 512)
        dc = al(2, 9)
        S = al(8, 256)
        SC = al(2, 512)
        kst = al(4, 128)
        ksm = al(128)
        t_scz = zero(SC)
        reset = con("reset")
        tril = con("tril").bitcast(I32)
        d0, d1, e3 = ex[:, 0, 16:NT], ex[:, 1, :], ex[:, 2, 16:NT]
        ready_h = {}
        pe_h = {}

        def chunks(a):
            return a.rearrange("p (c t) -> p c t", t=64)

        def gla_prepare(h):
            z = h % 2
            qi, ki = QK[:, 2 * z, :], QK[:, 2 * z + 1, :]
            s = 1.0 / 16.0
            w = [t_la, pe_h.get(h - 2)]
            cs = LA[:, h, :]
            step("dve", lambda g: g.tensor_tensor_scan(cs, reset, cs, 0.0, MUL, ADD), [t_c, w])
            cx = chunks(cs[:, 16:NT])
            tt(chunks(d0), cx, cx[:, :, 32:33].to_broadcast([128, 8, 64]), SUB, now("act"))
            tt(chunks(d1[:, 16:NT]), cx[:, :, 63:64].to_broadcast([128, 8, 64]), cx, SUB)
            td = tt(d1[:, 0:16], cs[:, 15:16].to_broadcast([128, 16]), cs[:, 0:16], SUB)
            act(dc[:, z, 1:9], cx[:, :, 63], ACT.Exp, td, scale=s)
            ta = act(e3, d0, ACT.Exp, scale=s)
            tb = act(d0, d0, ACT.Exp, scale=-s)
            tt(qi, Q[:, h, :], e3, MUL, [ta, t_kv])
            t1 = tt(ki, K[:, h, 16:NT], d0, MUL, tb)
            ta = act(e3, cs[:, 16:NT], ACT.Exp, t1, scale=s)
            tb = act(d1, d1, ACT.Exp, scale=s)
            tt(Q[:, h, :], Q[:, h, :], e3, MUL, ta)
            t2 = tt(K[:, h, :], K[:, h, :], d1, MUL, tb)
            ready_h[h] = (t1, t2)

        def to_u(j, b, t, lo, hi):
            return cp(U[:, j, lo:hi], b, t, "act")

        t_oh = {}

        def head_norm(h):
            z = h % 2
            i, b, f = take()
            t = mm([(b, ones, QK[:, 2 * z + dv, :], dv == 0, dv == 1) for dv in range(2)], [pe_h[("s", h)], f])
            t = root(i, b, QK[:, 2 * z + 1, :], [t, now("pe")], 256)
            for dv in range(2):
                j = 2 * h + dv
                t_oh[h] = stt(O[:, j, :], O[:, j, :], vec("gla_norm_g")[:, j:j + 1], QK[:, 2 * z + 1, :], MUL, MUL, t)
            pe_h[h] = t_oh[h]

        gla_prepare(0)
        for h in range(4):
            z = h % 2
            t1, t2 = ready_h[h]
            qi, ki = QK[:, 2 * z, :], QK[:, 2 * z + 1, :]
            hv = slice(256 * h, 256 * h + 256)
            i, b, f = take()
            t = mm([(b[:, 128 * m:128 * m + 128], ki[:, 128 * m:128 * m + 128], qi[:, 128 * m:128 * m + 128],
                     True, True) for m in range(4)], [t1, f])
            pe_h[h] = t
            for m in range(4):
                t_sc = step("dve", lambda g, m=m, b=b, z=z: g.copy_predicated(
                    SC[:, z, 128 * m:128 * m + 128], tril, b[:, 128 * m:128 * m + 128]), [t, t_scz, pe_h.get(("o", h - 2))])
            give(i, t_sc)
            i, b, f = take()
            t = tr([(b[:, 128 * m:128 * m + 128], K[:, h, 16 + 128 * m:144 + 128 * m], ident) for m in range(4)], [t2, f])
            give(i, cp(kst, b.rearrange("p (a m) -> p a m", a=4), [t, pe_h.get(("u", h - 1))], "act"))
            i, b, f = take()
            t = tr([(b[0:16, 0:128], K[:, h, 0:16], ident)], f)
            tk = cp(ksm[0:16, :], b[0:16, 0:128], t, "act")
            give(i, tk)
            adds = {}
            for cc in ((0,), (1, 3), (2, 4), (5, 7), (6,)):
                i, b, f = take()
                grp = []
                for n, c in enumerate(cc):
                    o = b[:, 256 * n:256 * n + 256]
                    if c == 0:
                        grp.append((o, ksm[0:16, :], VM[0:16, hv], True, True))
                    else:
                        p = slice(64 * ((c - 1) % 2), 64 * ((c - 1) % 2) + 64)
                        grp.append((o, kst[p, (c - 1) // 2, :], VV[p, (c - 1) // 2, hv], True, True))
                t = mm(grp, [tk, f])
                for n, c in enumerate(cc):
                    adds[c] = (i, b[:, 256 * n:256 * n + 256], t, c == cc[-1])
            pe_h[("u", h)] = now("pe")
            if h:
                head_norm(h - 1)
            linear("u", h, to_u, halves, t_xn)
            for c in range(8):
                i, o, t, last = adds[c]
                if c == 0:
                    t_s = cp(S[:, 0, :], o, [t, pe_h.get(("o", h - 1))])
                else:
                    t_s = stt(S[:, c, :], S[:, c - 1, :], dc[:, z, c:c + 1], o, MUL, ADD, t)
                if last:
                    give(i, t_s)
            if h < 3:
                gla_prepare(h + 1)
            outs = []
            for dv in range(2):
                i, b, f = take()
                vs = slice(256 * h + 128 * dv, 256 * h + 128 * dv + 128)
                grp = [(b[:, 128 * m:128 * m + 128], VV[:, m, vs], SC[:, z, 128 * m:128 * m + 128], m == 0, False)
                       for m in range(4)]
                grp += [(b[:, 64 * c:64 * c + 64], S[:, c, 128 * dv:128 * dv + 128], Q[:, h, 64 * c:64 * c + 64],
                         False, c == 7) for c in range(8)]
                outs.append((i, b, mm(grp, [t_sc, t_s, t2, f])))
            pe_h[("o", h)] = now("pe")
            for dv, (i, b, tm) in enumerate(outs):
                td = cp(O[:, 2 * h + dv, :], b, tm)
                give(i, td)
                sq_ = QK[:, 2 * z + dv, :]
                ta = act(sq_, O[:, 2 * h + dv, :], ACT.Square, td)
            pe_h[("s", h)] = ta
        t_u = now("act")
        drop(K, LA, Q, VV, VM, ex, dc, S, SC, kst, ksm)
        rt = [al(512, by=("act",), top=True) for _ in range(4)]
        rfree = [None, None]

        def gate_r(j, b, t):
            z = j % 2
            act(rt[2 * z], b, ACT.Sigmoid, [t, rfree[z]])
            ta = cp(rt[2 * z + 1], b, None, "act")
            tt(rt[2 * z], rt[2 * z], rt[2 * z + 1], MUL, ta, "pool")
            rfree[z] = tt(O[:, j, :], O[:, j, :], rt[2 * z], MUL, t_oh[j // 2], "pool")
            return ta

        linear("r", 0, gate_r, xr, t_xn)
        head_norm(3)
        drop(QK)

        SX = al(67, 2, 32)
        BC = al(4, 512)
        t_bc = ld(BC, bc)
        tkeep = al(2, 512)
        br, bi_, cr, ci = [BC[:, k, :].rearrange("p (g h) -> p g h", h=16) for k in range(4)]
        tw = tkeep
        ta_, tb_ = [tw[:, k, :].rearrange("p (g h) -> p g h", h=16) for k in range(2)]
        def b16(a):
            return a.unsqueeze(2).to_broadcast([128, 32, 16])

        tt(ta_, br, b16(fr), MUL, t_bc)
        tt(tb_, bi_, b16(fi), MUL)
        tt(ta_, ta_, tb_, SUB)
        tt(tb_, br, b16(fi), MUL)
        cp(br, ta_)
        tt(ta_, bi_, b16(fr), MUL)
        t_par = tt(bi_, ta_, tb_, ADD)
        drop(P32)
        G = [al(4, 8, 32) for _ in range(2)]
        D = [[al(2, 9, 32, top=True) for _ in range(2)] for _ in range(2)]
        Pt = al(2, 288)
        KT = al(8, 128)
        linear("r", 1, gate_r, xr, t_xn)
        GT = [al(4, 128) for _ in range(4)]
        US = [al(132) for _ in range(4)]
        t_z = [[zero(a) for a in D[0] + D[1]][-1], [zero(a, None, "dve") for a in G + [KT]][-1]]

        def weights_in(cb, w):
            pw = [PW[:, 7::-1, k, 4 * cb:4 * cb + 4].rearrange("p j g -> p g j").unsqueeze(3).to_broadcast([128, 4, 8, 16])
                  for k in range(2)]
            bb = [x[:, 4 * cb:4 * cb + 4, :].unsqueeze(2).to_broadcast([128, 4, 8, 16]) for x in (br, bi_)]
            t1, t2 = [tw[:, k, :].rearrange("p (g j h) -> p g j h", g=4, j=8) for k in range(2)]
            for k, (x, y, op) in enumerate(((0, 1, SUB), (1, 0, ADD))):
                tt(t1, pw[0], bb[x], MUL)
                tt(t2, pw[1], bb[y], MUL)
                for hf in range(2):
                    p = slice(64 * hf, 64 * hf + 64)
                    t = tt(G[k][p, :, :, 16 * hf:16 * hf + 16], t1[p], t2[p], op, [t_z, w])
            return t

        def weights_out(hb, d, w, e):
            def powers(a):
                return a[:, :, 2 * hb:2 * hb + 2].rearrange("p j g -> p g j").unsqueeze(3).to_broadcast([128, 2, 9, 16])

            pr, pi, npr = powers(PW[:, :, 0, :]), powers(PW[:, :, 1, :]), powers(NPW)
            c_r, c_i = [x[:, 2 * hb:2 * hb + 2, :].unsqueeze(2).to_broadcast([128, 2, 9, 16]) for x in (cr, ci)]
            tmp = Pt if e == "pool" else tw
            t1, t2 = [tmp[:, k, 0:288].rearrange("p (g j h) -> p g j h", g=2, j=9) for k in range(2)]
            for k, (x, cx, cy) in enumerate(((pr, c_r, c_i), (npr, c_i, c_r))):
                tt(t1, x, cx, MUL, t_par, e)
                tt(t2, pi, cy, MUL, None, e)
                for hf in range(2):
                    p = slice(64 * hf, 64 * hf + 64)
                    t = tt(d[k][p, :, :, 16 * hf:16 * hf + 16], t1[p], t2[p], SUB, [w, t_z], e)
            return t

        after = {"g": None, "d": None, "s": None, "y": None}
        t_d = [weights_out(k, D[k], None, "pool") for k in range(2)]
        t_g = weights_in(0, None)
        for cb in range(8):
            bk, kb_, f = take()
            grp = []
            for q in range(4):
                o = kb_[32 * q:32 * q + 32, 0:256]
                grp += [(o, G[0][:, q, 7, :], D[q // 2][0][:, q % 2, 0:8, :], True, False),
                        (o, G[1][:, q, 7, :], D[q // 2][1][:, q % 2, 0:8, :], False, True)]
            t_kt = after["d"] = mm(grp, [t_d, t_g, f])
            for q in range(4):
                uc = U[32 * q:32 * q + 32, cb, :].rearrange("p (c f l) -> p l f c", f=2, l=4)
                for l in range(4):
                    o = US[q][32 * l:32 * l + 32, :].rearrange("p (f c) -> p f c", f=2)
                    if l % 2:
                        ta = cp(o, uc[:, l], [t_u, after["s"]], "act")
                    else:
                        td = cp(o, uc[:, l], [t_u, after["s"]])
            t_gt = []
            for q in range(4):
                bt, b, f = take()
                t = tr([(b[:, 128 * (2 * k + hf):128 * (2 * k + hf) + 128], G[k][:, q, 4 * hf:4 * hf + 4, :], ident)
                        for k in range(2) for hf in range(2)], [t_g, f])
                t_gt.append(cp(GT[q], b.rearrange("p (a m) -> p a m", a=4), [t, after["s"]], "act"))
                give(bt, t_gt[q])
            after["g"] = t
            for q in range(4):
                p = slice(32 * q, 32 * q + 32)
                tk = cp(KT[p, :, 32 * q:32 * q + 32], kb_[p, 0:256].rearrange("p (s c) -> p s c", s=8),
                        [t_kt, after["y"], t_z], "act")
            give(bk, tk)
            if cb < 7:
                t_d = [weights_out(2 * cb + 2 + k, D[k], after["d"], "pool") for k in range(2)]
                t_g = weights_in(cb + 1, after["g"])
            b0, s0, f0 = take()
            b1, s1, f1 = take()
            for q in range(4):
                t = mm([(s[:, 66 * q:66 * q + 66], GT[q][:, 2 * k + hf, :], US[q][:, 66 * hf:66 * hf + 66], hf == 0, hf == 1)
                        for k, s in ((0, s0), (1, s1)) for hf in range(2)], [ta, td, t_gt[q], f0, f1])
            after["s"] = t
            ux = U[:, cb, 16:NT].rearrange("p (c s) -> p c s", s=8)
            by, b, f = take()
            yv = b.rearrange("p (c s) -> p c s", s=8)
            after["y"] = ty = mm([(yv[:, :, s:8], KT[:, s, :], ux[:, :, 0:8 - s], s == 0, s == 7) for s in range(8)],
                                 [tk, t_u, f])
            for k, (i, s) in enumerate(((b0, s0), (b1, s1))):
                o = SX[:, 1:67, k, 4 * cb:4 * cb + 4].rearrange("p c q -> p q c")
                give(i, cp(o, s[:, 0:264].rearrange("p (q c) -> p q c", q=4), t))
            give(by, stt(U[:, cb, 16:NT], U[:, cb, 16:NT], vec("d_skip")[:, cb:cb + 1], b, MUL, ADD, [ty, ta]))
        drop(G[0], G[1], KT, *GT, *US)
        SZ = al(8, 512, by=("act",))
        sw = [tw[:, k, 0:64].rearrange("p (a g) -> p a g", a=2) for k in range(2)]
        l8 = PW[:, 8:9, 0, :].to_broadcast([128, 2, 32])
        for c in range(1, 65):
            tt(sw[0], SX[:, c], l8, MUL)
            tt(sw[1], SX[:, c, ::-1, :], L8i, MUL)
            tt(SX[:, c + 1], SX[:, c + 1], sw[0], ADD)
            t_sx = tt(SX[:, c + 1], SX[:, c + 1], sw[1], ADD)
        low[0] = "pool"
        for i in range(2, 4):
            linear("r", i, gate_r, xr, t_xn)
        t_o = now("pool")
        for i in range(4):
            linear("zg", i, lambda j, b, t: act(SZ[:, j, :], b, ACT.Sigmoid, t), xr, t_xn)
        drop(*rt)
        t_zg = now("act")
        for _ in range(2):
            D.append([al(2, 9, 32, by=("pool", "dve")) for _ in range(2)])
            for a in D[-1]:
                t_z = zero(a)
        gt = al(2, 512, by=("act", "dve"))
        dread = [after["d"], after["d"], None, None]

        def gelu(j):
            y, x = U[:, j, 16:NT], gt[:, j % 2, :]
            t = act(x, y, ACT.Square, now("dve"))
            ts(x, x, 0.044715, 1.0, MUL, ADD, t)
            t = tt(x, x, y, MUL)
            t = act(x, x, ACT.Sigmoid, t, scale=2 * math.sqrt(2 / math.pi))
            tt(y, x, y, MUL, t)

        def out_weights(cb):
            return [weights_out(hb, D[hb % 4], dread[hb % 4], "dve" if hb % 2 else "pool") for hb in (2 * cb, 2 * cb + 1)]

        td = out_weights(0)
        for cb in range(8):
            by, b, f = take()
            yv = b.rearrange("p (c s) -> p c s", s=8)
            for half in range(2):
                d = D[(2 * cb + half) % 4]
                grp = []
                for q in (2 * half, 2 * half + 1):
                    for s in range(8):
                        o = yv[32 * q:32 * q + 32, :, s]
                        for k in range(2):
                            grp.append((o, d[k][:, q % 2, s + 1, :], SX[:, 2:66, k, 4 * cb + q], s == 0 and k == 0, k == 1))
                t = mm(grp, [td[half], t_sx, f])
                dread[(2 * cb + half) % 4] = t
            if cb < 7:
                td = out_weights(cb + 1)
            give(by, tt(U[:, cb, 16:NT], U[:, cb, 16:NT], b, ADD, t))
            gelu(cb)
        low[0] = "dve"
        drop(*D[0], *D[1], *D[2], *D[3], Pt, SX, tkeep, PW, NPW, L8i, BC, gt)

        oh, ol = al(8, 512, dt=F32R, by=("act",)), high_low(O)
        t_os = split_all(8, lambda k: t_o, *halves_of(oh, ol, O))
        gh, gl = al(8, 512, dt=F32R, by=("act",)), high_low(U)[:, :, 16:NT]
        t_gelu = now("dve")
        t_gs = split_all(8, lambda k: t_gelu, *halves_of(gh, gl, U[:, :, 16:NT]))
        MX = SZ
        gsr = pairs(gh, gl)

        for i in range(4):
            linear("og", i, lambda j, b, t: tt(MX[:, j, :], b, MX[:, j, :], MUL, [t, t_zg]), pairs(oh, ol), t_os)
        drop(oh, O)
        mh, ml = al(8, 512, dt=F32R, by=("act",)), al(8, 512, dt=F32R, by=("dve",))
        tmp = al(6, 512, by=("act", "dve"))
        sg = [tmp[:, k, :] for k in range(6)]
        free = [None] * 2
        bgl = vec("b_glu")
        t_mx = []
        held = {}

        def e_z(j, b, t):
            held[j] = act(sg[j % 2], b, ACT.Sigmoid, [t, free[j % 2]])
            return held[j]

        def e_a(j, b, t):
            free[j % 2] = stt(sg[2 + j % 2], b, bgl[:, j:j + 1], sg[j % 2], ADD, MUL, [t, held[j]])
            return free[j % 2]

        def e_b(j, b, t):
            ta = act(sg[4 + j % 2], b, ACT.Sigmoid, [t, now("dve")], bias=bgl[:, 8 + j:9 + j])
            tt(sg[2 + j % 2], sg[2 + j % 2], sg[4 + j % 2], MUL, ta)
            t = tt(MX[:, j, :], MX[:, j, :], sg[2 + j % 2], ADD)
            t_mx.append(split((mh[:, j, :], ml[:, j, :]), MX[:, j, :], t))
            return ta

        for i in range(4):
            linear("zs", i, e_z, xr, t_xn)
            linear("glua", i, e_a, gsr, t_gs)
            linear("glub", i, e_b, gsr, t_gs)
        drop(SZ, xnh, xnl, gh, U, tmp)
        XR = al(8, 512, by=("sp",))
        t_xr = [ld(XR[:, 4 * i:4 * i + 4, :], xT[:, 4 * i:4 * i + 4, 16:NT]) for i in range(2)]
        X = XR

        nrm = al(4, 512, by=("act", "dve"))
        rs = nrm[:, 3, :]

        def out_block(Z, j, b, t):
            t = cp(Z[:, j, :], b, t, "act")
            sum_squares(nrm[:, 2, :], Z[:, j, :], nrm[:, j % 2, :], j == 0)
            return t

        def add_norm(Z, g, w):
            t = over_partitions(nrm[:, 2, :], rs, [now("dve"), now("act")], 1024)
            i, b, f = take()
            tp = []
            for k in range(8):
                t1 = stt(Z[:, k, :], Z[:, k, :], g[:, k:k + 1], rs, MUL, MUL, [t, w])
                t2 = tt(X[:, k, :], X[:, k, :], Z[:, k, :], ADD, t1, "pool" if k % 2 else "dve")
                ta = act(nrm[:, k % 3, :], X[:, k, :], ACT.Square, [t2, tp[k - 3] if k > 2 else now("pe")])
                tp.append(mm([(b, ones, nrm[:, k % 3, :], k == 0, k == 7)], [ta, f]))
            return root(i, b, rs, tp[7], 1024)

        Z = al(8, 512, by=("act", "dve"))
        for i in range(4):
            linear("wo", i, lambda j, b, t: out_block(Z, j, b, t), pairs(mh, ml), t_mx)
        drop(mh, ml)
        t = add_norm(Z, vec("g_mix_post"), t_xr)
        hh, hl = al(8, 512, dt=F32R, by=("act",)), al(8, 512, dt=F32R, by=("dve",))
        g = vec("g_ffn_pre")
        t_r2 = t
        t_hn = split_all(8, lambda k: stt(Z[:, k, :], X[:, k, :], g[:, k:k + 1], rs, MUL, MUL, t_r2), *halves_of(hh, hl, Z))
        fh, fl = al(16, 512, dt=F32R, by=("act",)), al(16, 512, dt=F32R, by=("dve",))
        adab = al(2048, by=("dve",))
        ft = nrm
        cact = small[:, 0:8]
        ta = act(cact, vec("c_2"), ACT.Sigmoid)
        t_ca = tt(cact, cact, vec("c_2"), MUL, ta)
        ffree = [None] * 2
        pe_f = [None]

        def relu2(j, b, t):
            z = j % 2
            r, q = ft[:, 2 * z, :], ft[:, 2 * z + 1, :]
            k = j % 16
            ta = act(r, b, ACT.Relu, [t, ffree[z], pe_f[0]])
            tb = act(fh[:, k, :], r, ACT.Square)
            tt(q, r, r, MUL, ta)
            ffree[z] = tt(fl[:, k, :], q, fh[:, k, :].bitcast(F32), SUB, tb)
            return ta

        def ada_unit():
            i = PLAN[upos[0]][1]
            n, u, tu = unit("ada", i)
            q, k = i // 8, i % 8
            if k == 0:
                t = ts(adab, u, cact[:, 0:1], None, MUL, None, [tu, t_ca, now("pe") if q else None])
            else:
                t = stt(adab, u, cact[:, k:k + 1], adab, MUL, ADD, tu)
            release(n, t)
            if k == 7:
                bi, b, f = take()
                tm = mm([(b[:, j:j + 1], adab[:, 128 * j:128 * j + 128], ones[:, 0:1], True, True) for j in range(16)], [t, f])
                give(bi, tt(adat[:, 16 * q:16 * q + 16], b[:, 0:16], vec("ada_b_2")[:, 16 * q:16 * q + 16], ADD, tm))

        for hf in range(2):
            for i in range(16):
                if i < 8:
                    linear("f1", 8 * hf + i, relu2, pairs(hh, hl), t_hn)
                    if i == 7:
                        t_h1 = [now("act"), now("dve")]
                else:
                    c, kg = (i - 8) // 2, (i - 8) % 2
                    z, u, tu = unit("f2", 8 * hf + i - 8)
                    u = u.rearrange("p a (k m) -> p a k m", k=8)
                    if kg == 0:
                        pair = [take() for _ in range(2)]
                    for j, (bi, b, f) in enumerate(pair):
                        ls = [(u[:, 0, k, 128 * j:128 * j + 128], u[:, 1, k, 128 * j:128 * j + 128]) for k in range(8)]
                        t = mm(mm3(b, ls, pairs(fh[:, 8 * kg:8 * kg + 8], fl[:, 8 * kg:8 * kg + 8]), kg == 0, kg == 1),
                               [tu, t_h1, f])
                        if kg == 1:
                            o = Z[:, 2 * c + j, :]
                            if hf == 0:
                                give(bi, cp(o, b, [t, t_hn], "act"))
                            else:
                                t2 = tt(o, o, b, ADD, [t, now("act")])
                                give(bi, t2)
                                jj = 2 * c + j
                                sum_squares(nrm[:, 2, :], o, nrm[:, jj % 2, :], jj == 0, t2)
                    used(z, t)
                    pe_f[0] = t
                if PLAN[upos[0]][0] == "ada":
                    ada_unit()
        drop(hh, hl, fh, fl, adab)
        t_rs = add_norm(Z, vec("g_ffn_post"), None)
        drop(Z)

        ada = [adat[:, 8 * k:8 * k + 8] for k in range(6)]

        g1, g2 = small[:, 8:16], small[:, 56:64]
        for gs, gn, sc in ((g1, "norm1_g_2", ada[1]), (g2, "norm2_g_2", ada[4])):
            ts(gs, sc, 1.0, None, ADD)
            tt(gs, gs, vec(gn), MUL)

        def modulate(tmp, k, gs, t):
            return stt(tmp, X[:, k, :], gs[:, k:k + 1], rs, MUL, MUL, t)

        hh, hl = al(8, 512, dt=F32R, by=("act",)), al(8, 512, dt=F32R, by=("dve",))
        mt = al(8, 512, by=("dve",))
        t_hb = split_all(
            8, lambda k: modulate(mt[:, k, :], k, g1, t_rs),
            lambda k, t: act(hh[:, k, :], mt[:, k, :], ACT.Identity, t, bias=ada[0][:, k:k + 1]),
            lambda k, t, e: stt(hl[:, k, :], mt[:, k, :], ada[0][:, k:k + 1], hh[:, k, :].bitcast(F32), ADD, SUB, t))
        drop(mt)
        hb = pairs(hh, hl)
        LAT = al(5, 512, by=("act",), top=True)
        KP = al(2, 512, by=("dve",))
        TR = al(3, 512, by=("dve", "act"))
        CU = al(4, 542, by=("act", "pool"))
        CA = al(4, 512, by=("act", "dve"))
        kpe = al(512, by=("dve",))
        pos_f = al(516, by=("dve",), top=True)
        pint = al(516, by=("sp",), top=True)
        MKf = al(1024, by=("dve",))
        MK = MKf.bitcast(BF16).rearrange("p (m k) -> p m k", m=4)
        t_z = zero(CU[:, :, 0:30])
        pi32 = pint.bitcast(I32)
        t_pos = [ld(pi32[:, 0:512], posr), ld(pi32[:, 512:516], posc)]
        cp(pos_f, pi32, t_pos)
        PR = TR[:, 2, :]
        ts(PR, pos_f[:, 0:512], con("freq"), None, MUL)
        t = reduce_angle(PR, PR, TR[:, 0, :])
        t = sin_cos(TR[:, 1, :], TR[:, 0, :], PR, t)
        t_tr = ts(TR[:, 1, :], TR[:, 1, :], con("sign"), None, MUL, None, t)
        for m in range(4):
            t_mk = ts(MK[:, m, :], pos_f[:, 0:512], pos_f[:, 512 + m:513 + m], BIG, ALU.is_gt, MUL)
        drop(pos_f, pint)

        def rope(o, b, w):
            tt(KP[64:96, 0, :], b[64:96, :], TR[64:96, 0, :], MUL, [w, t_tr])
            t = tt(KP[64:96, 1, :], b[96:128, :], TR[96:128, 1, :], MUL)
            tt(o, KP[64:96, 0, :], KP[64:96, 1, :], ADD)
            return t

        def e_lat(j, b, t):
            if j < 5:
                return cp(LAT[:, j, :], b, t, "act")
            return rope(kpe[64:96, :], b, t)

        for i in range(3):
            linear("lat", i, e_lat, hb, t_hb)
        t_kpe0 = now("dve")
        t_lat0 = now("act")

        def e_cin(j, b, t):
            if j < 4:
                return cp(CA[:, j, :], b, t, "act")
            o = CU[:, j - 4, 30:542]
            t = act(o, b, ACT.Sigmoid, [t, t_z])
            tt(o, o, CA[:, j - 4, :], MUL, t)
            return t

        for i in range(4):
            linear("cin", i, e_cin, hb, t_hb)
        lh, ll = al(5, 512, dt=F32R, by=("act",)), al(5, 512, dt=F32R, by=("dve",))
        for lo, n, name, dim in ((0, 3, "q_norm_g_2", 384), (3, 2, "kv_norm_g_2", 256)):
            t = rms(LAT[:, lo:lo + n, :], n, nrm[:, 2, :], nrm, rs, [t_lat0, now("dve")], dim)
            for k in range(n):
                t = stt(LAT[:, lo + k, :], LAT[:, lo + k, :], vec(name)[:, k:k + 1], rs, MUL, MUL, t)
                t_lat = split((lh[:, lo + k, :], ll[:, lo + k, :]), LAT[:, lo + k, :], t)
        drop(LAT)
        low[0] = "pool"
        cw = vec("conv_w_2").rearrange("p (c k) -> p c k", k=31)
        CO = CA
        for c in range(4):
            for k in range(31):
                i = CU[:, c, k:k + 512]
                if k == 0:
                    ts(CO[:, c, :], i, cw[:, c, 0:1], vec("conv_b_2")[:, c:c + 1], MUL, ADD)
                else:
                    t_co = stt(CO[:, c, :], i, cw[:, c, k:k + 1], CO[:, c, :], MUL, ADD)
        GA = al(8, 512, by=("act",))
        for i in range(4):
            linear("ga", i, lambda j, b, t: act(GA[:, j, :], b, ACT.Sigmoid, t), hb, t_hb)
        GC = al(8, 512, by=("act",))
        for i in range(4):
            linear("gc", i, lambda j, b, t: act(GC[:, j, :], b, ACT.Sigmoid, t), hb, t_hb)
        t_ga = now("act")
        low[0] = "dve"
        drop(hh, hl, CU)
        QH = al(8, 512, by=("act", "dve"))
        KH = al(8, 512, by=("act", "pool"))
        V2 = al(4, 512, by=("act",))
        cp(KH[64:96, :, :], kpe[64:96, :].unsqueeze(1).to_broadcast([32, 8, 512]), t_kpe0, "pool")
        t_kpe = now("pool")

        def e_q(h, b, t):
            ta = cp(QH[0:64, h, :], b[0:64, :], t, "act")
            return [ta, rope(QH[64:96, h, :], b, t)]

        for i in range(2):
            linear("uq", i, e_q, pairs(lh, ll, n=3), t_lat, 3, 1536)
        z, u, tu = unit("kv", 0)
        u = u.rearrange("p a (k m) -> p a k m", k=2)
        kvp = pairs(lh[:, 3:5], ll[:, 3:5], n=2)
        for h in range(8):
            i, b, f = take()
            ls = [(u[:, 0, k, 64 * h:64 * h + 64], u[:, 1, k, 64 * h:64 * h + 64]) for k in range(2)]
            t = mm(mm3(b[0:64, :], ls, kvp), [tu, t_lat, f])
            give(i, cp(KH[0:64, h, :], b[0:64, :], t, "act"))
        for m in range(4):
            i, b, f = take()
            r = [(u[:, 0, k, 512:1024], u[:, 1, k, 512:1024]) for k in range(2)]
            t = mm(mm3(b, [(x[:, 128 * m:128 * m + 128], y[:, 128 * m:128 * m + 128]) for x, y in kvp], r), [f])
            give(i, cp(V2[:, m, :], b, t, "act"))
        used(z, t)
        t_qkv = [now("act"), now("dve"), t_kpe]
        drop(lh, ll, KP, TR, kpe)
        AT = al(4, 512, by=("act",))
        PB = [al(4, 512, by=("dve", "act")) for _ in range(2)]
        PT = [al(512, by=("act",)) for _ in range(4)]
        st = small[:, 16:32].rearrange("p (z c) -> p z c", z=2)
        scale = 96.0 ** -0.5
        t_pt = [None, None]
        probs = {}

        def softmax_rows(h):
            z = h % 2
            t_p = []
            for m in range(4):
                i, b, f = take()
                t = mm([(b, QH[0:96, h, 128 * m:128 * m + 128], KH[0:96, h, :], True, True)], [t_qkv, f])
                p = PB[z][:, m, :]
                t = stt(p, b, scale, MK[:, m, :], MUL, ADD, [t, t_pt[z]])
                give(i, t)
                mx, sm = st[:, z, m:m + 1], st[:, z, 4 + m:5 + m]
                red(mx, p, MAX)
                t = ts(mx, mx, -1.0, None, MUL)
                t = act(p, p, ACT.Exp, t, bias=mx, accum_out=sm)
                t_p.append((p, sm, t))
            probs[h] = t_p

        def normalise(h):
            t = recip(st[:, h % 2, 4:8], st[:, h % 2, 4:8], probs[h][3][2])
            for p, sm, _ in probs[h]:
                t = ts(p, p, sm, None, MUL)
            return t

        softmax_rows(0)
        t_pv = None
        for h in range(8):
            z = h % 2
            t_p = normalise(h)
            if h < 7:
                softmax_rows(h + 1)
            for kb in range(4):
                i, b, f = take()
                t_pt[z] = tr([(b[:, 128 * m:128 * m + 128], PB[z][:, m, 128 * kb:128 * kb + 128], ident) for m in range(4)],
                             [t_p, f])
                t = cp(PT[kb], b, [t_pt[z], t_pv], "act")
                give(i, t)
            if h % 2 == 0:
                ia, ba, fa = take()
            o = ba[64 * (h % 2):64 * (h % 2) + 64, :]
            t_pv = mm([(o, V2[:, kb, 64 * h:64 * h + 64], PT[kb], kb == 0, kb == 3) for kb in range(4)], [t, fa])
            if h % 2:
                give(ia, cp(AT[:, h // 2, :], ba, t_pv, "act"))
        t_at = now("act")
        drop(QH, KH, V2, PB[0], PB[1], *PT)
        ath, atl = al(4, 512, dt=F32R, by=("act",)), al(4, 512, dt=F32R, by=("dve",))
        for k in range(4):
            t_as = split((ath[:, k, :], atl[:, k, :]), AT[:, k, :], t_at)
        cvh, cvl = al(4, 512, dt=F32R, by=("act",)), al(4, 512, dt=F32R, by=("dve",))
        i, b, f = take()
        tm = mm([(b, ones, CO[:, c, :], c == 0, c == 3) for c in range(4)], [t_co, f])
        for c in range(4):
            t = stt(CO[:, c, :], b, -1.0 / 512, CO[:, c, :], MUL, ADD, [tm, now("pe")])
        give(i, t)
        t = rms(CO, 4, nrm[:, 2, :], nrm, rs, t, 512)
        cs = al(2, 512, by=("act",))
        for c in range(4):
            tt(CO[:, c, :], CO[:, c, :], rs, MUL, t)
            t2 = ts(CO[:, c, :], CO[:, c, :], vec("conv_ln_g_2")[:, c:c + 1], vec("conv_ln_b_2")[:, c:c + 1], MUL, ADD)
            ta = act(cs[:, c % 2, :], CO[:, c, :], ACT.Sigmoid, t2)
            t = tt(CO[:, c, :], CO[:, c, :], cs[:, c % 2, :], MUL, ta)
            t_cv = split((cvh[:, c, :], cvl[:, c, :]), CO[:, c, :], t)
        mh, ml = al(8, 512, dt=F32R, by=("act",)), high_low(GA)
        for i in range(2):
            linear("oa", i, lambda j, b, t: tt(GA[:, j, :], b, GA[:, j, :], MUL, [t, t_ga]), pairs(ath, atl, n=4), t_as, 4)
        t_mx = []

        def e_yc(j, b, t):
            t1 = tt(GC[:, j, :], b, GC[:, j, :], MUL, [t, t_ga])
            t = tt(GA[:, j, :], GA[:, j, :], GC[:, j, :], ADD)
            t_mx.append(split((mh[:, j, :], ml[:, j, :]), GA[:, j, :], t))
            return t1

        for i in range(2):
            linear("oc", i, e_yc, pairs(cvh, cvl, n=4), t_cv, 4)

        def e_res(j, b, t):
            t = stt(X[:, j, :], b, ada[2][:, j:j + 1], X[:, j, :], MUL, ADD, t)
            sum_squares(nrm[:, 2, :], X[:, j, :], nrm[:, j % 2, :], j == 0, t)
            return t

        for i in range(4):
            linear("wo2", i, e_res, pairs(mh, ml), t_mx)
        t_rs = over_partitions(nrm[:, 2, :], rs, [now("dve"), now("act")], 1024)
        drop(AT, ath, atl, cvh, cvl, cs, mh, GA, GC, CA, MKf)

        HB = al(8, 512, by=("dve", "act"))
        RW = al(8, 36, by=("sp",))
        MCT = al(MC, by=("sp",))
        t_rw = [ld(RW, rw), ld(MCT, mcst)]
        for k in range(8):
            t = modulate(HB[:, k, :], k, g2, t_rs)
            t_hb = act(HB[:, k, :], HB[:, k, :], ACT.Identity, t, bias=ada[3][:, k:k + 1])
        i, b, f = take()
        t = mm([(b[:, 36 * m:36 * m + 36], HB[:, k, 128 * m:128 * m + 128], RW[:, k, :], k == 0, k == 7)
                for m in range(4) for k in range(8)], [t_hb, t_rw, f])
        L = al(4, 36, by=("dve",))
        rbv = vec("rb").unsqueeze(1).to_broadcast([128, 4, 36])
        t = tt(L, b[:, 0:144].rearrange("p (m c) -> p m c", m=4), rbv, ADD, t)
        give(i, t)
        HT = al(4, ROW, by=("act", "dve"))
        for m in range(4):
            for hf in range(2):
                i, b, f = take()
                t = tr([(b[:, 128 * k:128 * k + 128], HB[:, 4 * hf + k, 128 * m:128 * m + 128], ident) for k in range(4)],
                       [t_hb, f])
                t_ht = cp(HT[:, m, 512 * hf:512 * hf + 512], b, t, "act")
                give(i, t_ht)
        LG = L[:, :, 0:4]

        def bc_(a, n):
            return a.unsqueeze(2).to_broadcast([128, 4, n])

        def first_max(oh, v, m, n, rev):
            tt(oh, v, bc_(m, n), ALU.is_equal)
            tt(oh, oh, rev.unsqueeze(1).to_broadcast([128, 4, n]), MUL)
            red(km, oh, MAX)
            return tt(oh, oh, bc_(km, n), ALU.is_equal)

        RT = al(640, by=("dve", "act"))
        ro = [0]

        def piece(*dims):
            n = int(np.prod(dims))
            a = RT[:, ro[0]:ro[0] + n]
            ro[0] += n
            if len(dims) == 2:
                a = a.rearrange("p (a b) -> p a b", b=dims[1])
            if len(dims) == 3:
                a = a.rearrange("p (a b c) -> p a b c", b=dims[1], c=dims[2])
            return a

        gm, km, sg_, gv, m1, m2, sw_ = [piece(4) for _ in range(7)]
        og_, eg = piece(4, 4), piece(4, 4)
        es, es2, exx, o1, o2, wn = [piece(4, 8) for _ in range(6)]
        tmp4 = piece(4, 8, 4)
        rk = piece(8, 4)
        nb, s4, s128 = piece(4), piece(4), piece(4)
        bgr, sl = piece(NB), piece(4)
        ixf = piece(NB, 12)
        IX = al(NB * 12 + 4, by=("dve",)).bitcast(I32)
        red(gm, LG, MAX)
        t = tt(eg, LG, bc_(gm, 4), SUB)
        t = act(eg, eg, ACT.Exp, t)
        red(sg_, eg, ADD, t)
        recip(gv, sg_)
        first_max(og_, LG, gm, 4, con("rev4"))
        i, b, f = take()
        ogf = og_.rearrange("p m g -> p (m g)")
        t = mm([(b[:, 0:16], MCT[:, 0:128], ogf, True, True), (b[:, 16:32], ones, ogf, True, True)], [now("dve"), t_rw, f])
        t = cp(rk, b[:, 0:32].rearrange("p (m g) -> p m g", g=4), t)
        give(i, t)
        for m in range(1, 4):
            tt(rk[:, m, :], rk[:, m, :], rk[:, 3 + m, :], ADD)
            tt(rk[:, 4 + m, :], rk[:, 4 + m, :], rk[:, 3 + m, :], ADD)
        ng = rk[:, 7, :]
        ts(nb, ng, 0.0, None, ALU.is_gt)
        for lim in (128.0, 256.0, 384.0):
            stt(nb, ng, lim, nb, ALU.is_gt, ADD)
        step("dve", lambda g: g.memset(s4[:, 0:1], 0.0))
        for q in range(3):
            tt(s4[:, q + 1:q + 2], s4[:, q:q + 1], nb[:, q:q + 1], ADD)
        blk, off, mult = MCT[:, 152:152 + NB], MCT[:, 128:140], MCT[:, 140:152]
        ts(bgr, blk, s4[:, 1:2], None, ALU.is_ge)
        for q in (2, 3):
            stt(bgr, blk, s4[:, q:q + 1], bgr, ALU.is_ge, ADD)
        tt(ixf, bgr.unsqueeze(2).to_broadcast([128, NB, 12]), mult.unsqueeze(1).to_broadcast([128, NB, 12]), MUL)
        tt(ixf, ixf, off.unsqueeze(1).to_broadcast([128, NB, 12]), ADD)
        t_ix = cp(IX[:, 4:4 + NB * 12], ixf.rearrange("p b u -> p (b u)"))
        ts(s128, s4, 128.0, None, MUL)
        tt(rk[:, 0:4, :], rk[:, 0:4, :], s128.unsqueeze(1).to_broadcast([128, 4, 4]), ADD)
        tt(rk[:, 0:4, :], rk[:, 0:4, :], og_, MUL)
        red(sl, rk[:, 0:4, :], ADD)
        cp(IX[:, 0:4], sl)
        LE = L[:, :, 4:36].rearrange("p m (g e) -> p m e g", g=4)
        tt(tmp4, LE, og_.unsqueeze(2).to_broadcast([128, 4, 8, 4]), MUL)
        red(es, tmp4, ADD)
        red(m1, es, MAX)
        t = tt(exx, es, bc_(m1, 8), SUB)
        t = act(exx, exx, ACT.Exp, t)
        first_max(o1, es, m1, 8, con("rev8"))
        stt(es2, o1, BIG, es, MUL, ADD)
        red(m2, es2, MAX)
        first_max(o2, es2, m2, 8, con("rev8"))
        tt(o1, o1, o2, ADD)
        tt(wn, exx, o1, MUL, t)
        red(sw_, wn, ADD)
        recip(sw_, sw_)
        tt(sw_, sw_, gv, MUL)
        tt(wn, wn, bc_(sw_, 8), MUL)
        t_wn = cp(HT[:, :, 1024:ROW], wn)

        def indexed(c):
            return bass.IndirectOffsetOnAxis(ap=IX[:, c:c + 1].bitcast(U32), axis=0)

        XS = al(2, ROW, by=("sp",))
        XH, XL = [al(8, 128, dt=F32R, by=("act",)) for _ in range(2)], [al(8, 128, dt=F32R, by=("dve",)) for _ in range(2)]
        GX = al(2, 2048, by=("pool",))
        w3 = al(2, 2048, dt=F32R, by=("act", "dve"))
        YS = al(2, 512, by=("act", "dve"))
        PD = al(2, 512, by=("act", "dve"))
        TH, TL = al(2, 256, dt=F32R, by=("act",)), al(2, 256, dt=F32R, by=("dve",))
        slots = [ringt[:, k, :] for k in range(RING)] + [GX[:, k, :] for k in range(2)]
        sfree = ring_read + [None, None]
        parts = [wst[:, 0], wst[:, 1], w3]
        pfree = [wfree[0], wfree[1], None]
        parted = {}
        NG = NB * 12

        def gather(n):
            z, (k, kind, i) = n % 5, STREAM[n]
            c = 4 + 12 * k + COLS.index((kind, i))
            emit("pool", lambda g: g.indirect_dma_start(slots[z], None, wmoe, indexed(c)).then_inc(s_gat[z], 16),
                 [t_ix, sfree[z]], False)

        def part(n):
            z, y = n % 5, n % 3
            t = act(parts[y][:, 0, :], slots[z], ACT.Copy, [(s_gat[z], 16 * (n // 5 + 1)), pfree[y]])
            t = tt(parts[y][:, 1, :], slots[z], parts[y][:, 0, :].bitcast(F32), SUB, t)
            sfree[z] = t
            parted[n] = t
            if n + 5 < NG:
                gather(n + 5)

        npart = [0]

        def moe_unit(*which):
            n = mpos[0]
            assert STREAM[n] == which
            mpos[0] += 1
            while npart[0] < min(n + 3, NG):
                part(npart[0])
                npart[0] += 1
            return n % 3, parts[n % 3], parted[n]

        mpos = [0]
        for n in range(3):
            gather(n)
        for m in range(4):
            emit("pool", lambda g, m=m: g.indirect_dma_start(xslot, indexed(m), HT[:, m, :], None).then_inc(s_scat, 16),
                 [t_ht, t_wn, (s_clear, 16 * NB)], False)
        for n in range(3, 5):
            gather(n)
        xread = [None, None]
        tread = [None, None]

        def load_block(n):
            z = n % 2
            emit("sp", lambda g: g.dma_start(XS[:, z, :], xslot[128 * n:128 * n + 128, :]).then_inc(s_xs[z], 16),
                 [(s_scat, 64), xread[z]], False)

        t_xt = {}

        def turn_block(n):
            z = n % 2
            for hf in range(2):
                i, b, f = take()
                t = tr([(b[:, 128 * k:128 * k + 128], XS[:, z, 512 * hf + 128 * k:512 * hf + 128 * k + 128], ident)
                        for k in range(4)], [(s_xs[z], 16 * (n // 2 + 1)), f])
                b = b.rearrange("p (k m) -> p k m", k=4)
                ta = act(XH[z][:, 4 * hf:4 * hf + 4, :], b, ACT.Copy, [t, tread[z]])
                t2 = tt(XL[z][:, 4 * hf:4 * hf + 4, :], b, XH[z][:, 4 * hf:4 * hf + 4, :].bitcast(F32), SUB, ta)
                give(i, t2)
            t_xt[n] = t2

        hfree = [None, None]
        state = {}

        def gate_up(n, p, kh):
            z = n % 2
            y, u, tu = moe_unit(n, "ex", 2 * p + kh)
            u = u.rearrange("p a (k m) -> p a k m", k=4)
            if kh == 0:
                state["g", p] = take()
            i, b, f = state["g", p]
            ls = [(XH[z][:, 4 * kh + k, :], XL[z][:, 4 * kh + k, :]) for k in range(4)]
            t = mm(mm3(b, ls, [(u[:, 0, k, :], u[:, 1, k, :]) for k in range(4)], kh == 0, kh == 1),
                   [tu, t_xt[n], f if kh == 0 else None])
            pfree[y] = t
            tread[z] = t
            if kh:
                gu = b.rearrange("p (e x m) -> p e x m", e=2, x=2)
                d = PD[:, p % 2, :].rearrange("p (x e m) -> p x e m", x=2, e=2)
                ta = act(d[:, 0], gu[:, :, 0, :], ACT.Sigmoid, [t, hfree[p % 2]])
                tt(d[:, 0], d[:, 0], gu[:, :, 0, :], MUL, ta)
                t = tt(d[:, 0], d[:, 0], gu[:, :, 1, :], MUL)
                give(i, t)
                c = XS[:, z, 1024 + 2 * p:1026 + 2 * p].unsqueeze(2).to_broadcast([128, 2, 128])
                state["h", p] = xread[z] = tt(d[:, 0], d[:, 0], c, MUL)

        def turn_hidden(p):
            z = p % 2
            i, b, f = take()
            hfree[z] = t = tr([(b[:, 128 * e:128 * e + 128], PD[:, z, 128 * e:128 * e + 128], ident) for e in range(2)],
                              [state["h", p], f])
            ta = act(TH[:, z, :], b[:, 0:256], ACT.Copy, [t, state.get(("d", p % 2))])
            state["t", p] = tt(TL[:, z, :], b[:, 0:256], TH[:, z, :].bitcast(F32), SUB, ta)
            give(i, state["t", p])

        def down(n, p):
            z = p % 2
            y, u, tu = moe_unit(n, "dn", p)
            u = u.rearrange("p a (e m) -> p a e m", e=2)
            if p == 0:
                state["y"] = [take(), take()]
            for hf, (i, b, f) in enumerate(state["y"]):
                ls = [(TH[:, z, 128 * e:128 * e + 128], TL[:, z, 128 * e:128 * e + 128]) for e in range(2)]
                cols = slice(512 * hf, 512 * hf + 512)
                t = mm(mm3(b, ls, [(u[:, 0, e, cols], u[:, 1, e, cols]) for e in range(2)], p == 0, p == 3),
                       [tu, state["t", p], f if p == 0 else None])
                if p == 3:
                    to = cp(YS[:, hf, :], b, [t, (s_y, 16 * n)], "dve" if hf else "act")
                    give(i, to)
                    state["o", hf] = to
            pfree[y] = state["d", z] = t
            if p == 3:
                emit("sp", lambda g: g.dma_start(yslot[128 * n:128 * n + 128, :], YS.rearrange("p a m -> p (a m)"))
                     .then_inc(s_y, 16), [state["o", 0], state["o", 1]], False)

        load_block(0)
        load_block(1)
        turn_block(0)
        for n in range(NB):
            for p in range(4):
                gate_up(n, p, 0)
                if p:
                    turn_hidden(p - 1)
                elif n:
                    turn_hidden(3)
                gate_up(n, p, 1)
                if p:
                    down(n, p - 1)
                elif n:
                    down(n - 1, 3)
                if p == 0 and 0 < n < NB - 1:
                    load_block(n + 1)
                if p == 2 and n < NB - 1:
                    turn_block(n + 1)
        turn_hidden(3)
        down(NB - 1, 3)
        for m in range(4):
            emit("pool", lambda g, m=m: g.indirect_dma_start(HT[:, m, 0:1024], None, yslot, indexed(m)).then_inc(s_back, 16),
                 [(s_y, 16 * NB), (s_scat, 64)], False)
        ac = [take() for _ in range(8)]
        for j, (i, b, f) in enumerate(ac):
            t = tr([(b[:, 128 * m:128 * m + 128], HT[:, m, 128 * j:128 * j + 128], ident) for m in range(4)],
                   [(s_back, 64), f])
            ac[j] = (i, b, t)
        for j, (i, b, t) in enumerate(ac):
            t2 = stt(X[:, j, :], b, ada[5][:, j:j + 1], X[:, j, :], MUL, ADD, t)
            give(i, t2)
            t3 = sum_squares(nrm[:, 2, :], X[:, j, :], nrm[:, j % 2, :], j == 0, t2)
        t = over_partitions(nrm[:, 2, :], rs, [t3, t2], 1024)
        g = vec("final_norm_g_2")
        for k in range(8):
            t = stt(X[:, k, :], X[:, k, :], g[:, k:k + 1], rs, MUL, MUL, t)
            if k % 2:
                emit("sp", lambda g, k=k: g.dma_start(out[:, k - 1:k + 1, :], X[:, k - 1:k + 1, :]).then_inc(s_out, 16), t, False)
        emit("sp", None, [(s_out, 64)], False)
        assert upos[0] == NU

        block = ctx.enter_context(nc.Block())

        def play(e, g):
            seen = {}
            for w, fn, inc in queue[e]:
                for s, v in w:
                    if v > seen.get(s.name, 0):
                        g.wait_ge(s, v)
                        seen[s.name] = v
                if fn is not None:
                    ins = fn(g)
                    if inc:
                        ins.then_inc(sem[e], 1)

        @block.tensor
        def _(g):
            play("pe", g)

        @block.scalar
        def _(g):
            play("act", g)

        @block.vector
        def _(g):
            play("dve", g)

        @block.gpsimd
        def _(g):
            play("pool", g)

        @block.sync
        def _(g):
            play("sp", g)


def lay(w, n):
    K, N = w.shape
    return w.reshape(K // 128, 128, N // n, n).transpose(2, 1, 0, 3).reshape(N // n, 128, K // 128 * n)


def constants():
    c = {}
    c["ident"] = np.eye(128)
    c["ones"] = np.ones((128, 128))
    j, i = np.arange(128)[:, None], np.arange(128)[None, :]
    c["tril"] = (j // 64 == i // 64) & (j <= i)
    t = np.arange(NT)
    c["reset"] = np.broadcast_to(((t != 0) & ((t < 16) | ((t - 16) % 64 != 0))), (128, NT))
    p = np.arange(128)
    freq = np.float32(10000.0) ** (-np.arange(0, 32, 2, dtype=np.float32) / np.float32(32))
    c["freq"] = freq[p % 16][:, None]
    c["sign"] = np.where(p % 32 < 16, -1.0, 1.0)[:, None]
    c["eps"] = np.full((128, 1), EPS)
    c["rev4"] = np.broadcast_to(np.arange(4, 0, -1), (128, 4))
    c["rev8"] = np.broadcast_to(np.arange(8, 0, -1), (128, 8))
    m = np.zeros((128, MC))
    m[:, 0:128] = j < i
    for n, (kind, q) in enumerate(COLS):
        m[:, 128 + n] = (q if kind == "ex" else 32 + q) * 128 + p
        m[:, 140 + n] = 1024 if kind == "ex" else 512
    m[:, 152:] = np.arange(NB)
    return np.concatenate([c[n] for n, _ in CST], axis=1).astype(np.float32), m.astype(np.float32)


def layout(a):
    def col(v):
        v = v.reshape(-1)
        return v.reshape(-1, 128).T

    w = a["w_in"][0]
    parts = {
        "u": lay(w[:, 3088:4112], 256), "k": lay(w[:, 512:1024], 256), "q": lay(w[:, 0:512], 256),
        "v": np.stack([w[512 * kg:512 * kg + 512, 1024 + 512 * hf:1536 + 512 * hf].reshape(4, 128, 512)
                       .transpose(1, 0, 2).reshape(128, 2048) for hf in range(2) for kg in range(2)]),
        "r": lay(w[:, 2048:3072], 256), "zg": lay(w[:, 4112:5136], 256), "zs": lay(w[:, 5136:6160], 256),
        "og": lay(a["w_o_gla"][0], 256),
        "glua": lay(a["w_glu"][0][:, 0:1024], 256), "glub": lay(a["w_glu"][0][:, 1024:2048], 256),
        "wo": lay(a["w_out"][0], 256), "f1": lay(a["w_ff1"][0], 256),
        "f2": a["w_ff2"][0].reshape(2, 2, 8, 128, 4, 256)
        .transpose(0, 4, 1, 3, 2, 5).reshape(16, 128, 2048),
        "ada": a["ada_w_2"][0].reshape(8, 128, 3, 2048).transpose(2, 0, 1, 3).reshape(24, 128, 2048),
    }
    w = a["w_in_2"][0]
    kr = w[:, 640:672]
    ks = np.concatenate([kr[:, 16:32], kr[:, 0:16]], axis=1)
    parts["lat"] = lay(np.concatenate([w[:, 0:640], kr, ks, kr, ks], axis=1), 256)
    parts["cin"] = lay(w[:, 672:1696], 256)
    parts["ga"], parts["gc"] = lay(w[:, 1696:2720], 256), lay(w[:, 2720:3744], 256)
    kv = a["w_ukv_2"][0].reshape(256, 8, 128)
    parts["kv"] = lay(np.concatenate([kv[:, :, 0:64].reshape(256, 512), kv[:, :, 64:128].reshape(256, 512)], axis=1), 1024)
    parts["oa"], parts["oc"] = lay(a["w_o_attn_2"][0], 512), lay(a["w_conv_out_2"][0], 512)
    parts["wo2"] = lay(a["w_out_2"][0], 256)
    e = np.stack([a[n][0].reshape(4, 4, 2, 2, 4, 128, 128) for n in ("expert_w_gate_2", "expert_w_up_2")])
    ex = e.transpose(1, 2, 4, 6, 5, 3, 0, 7).reshape(4096, 2048)
    dn = a["expert_w_down_2"][0].reshape(16, 2, 128, 1024).transpose(0, 2, 1, 3).reshape(2048, 2048)
    q = a["w_uq_2"][0].reshape(384, 8, 96)
    q = lay(np.concatenate([q, q[:, :, 80:96], q[:, :, 64:80]], axis=2).reshape(384, 1024), 512)
    parts["uq"] = np.concatenate([q, np.zeros((2, 128, 512), np.float32)], axis=2)
    W = np.stack([parts[n][i] for n, i in PLAN])

    two = lambda v: v.reshape(32, 128).T
    v = {n: col(a[n]) for n, _ in VEC if n in a and n not in ("a_re", "a_im", "log_step", "conv_w_2")}
    v["conv_w_2"] = a["conv_w_2"][0].reshape(31, 4, 128).transpose(2, 1, 0).reshape(128, 124)
    v["a_re"], v["a_im"] = two(a["a_re"][0]), two(a["a_im"][0])
    v["log_step"] = two(np.broadcast_to(a["log_step"][0][:, None], (64, 64)))
    rb = np.concatenate([a["router_group_b_2"][0], a["router_expert_b_2"][0]])
    v["rb"] = np.broadcast_to(rb, (128, 36))
    vecs = np.concatenate([v[n] for n, _ in VEC], axis=1)
    cst, mcst = constants()
    b3 = lambda t: t.reshape(32, 128, 16).transpose(1, 0, 2).reshape(128, 512)
    c3 = lambda t: b3(t.transpose(0, 2, 1))
    bc = np.stack([b3(a["b_re"][0]), b3(a["b_im"][0]), c3(a["c_re"][0]), c3(a["c_im"][0])], axis=1)
    xT = np.concatenate([a["meta_tokens"], a["x"][0]], axis=0).T.reshape(8, 128, NT).transpose(1, 0, 2)
    rw = np.concatenate([a["router_group_w_2"][0], a["router_expert_w_2"][0]], axis=1)
    pos = a["positions_2"].reshape(512)
    three = lambda w: w.reshape(-1, 128, w.shape[1]).transpose(1, 0, 2)
    return {"W": W, "wmoe": np.concatenate([ex, dn]), "mcst": mcst, "vecs": vecs, "cst": cst, "xT": xT, "wal": three(a["w_in"][0][:, 3072:3088]),
            "wgu": a["w_gate_up"][0], "bc": bc, "rw": three(rw),
            "posr": np.broadcast_to(pos, (128, 512)), "posc": pos.reshape(4, 128).T}


def kernel(**inputs):
    import concourse.bacc as _bacc
    from concourse.bass_utils import run_bass_kernel_spmd as _run

    arrays = {k: np.ascontiguousarray(v) for k, v in layout({k: np.asarray(v) for k, v in inputs.items()}).items()}
    nc = _bacc.Bacc("TRN2", target_bir_lowering=False, num_devices=1)
    args = {k: nc.dram_tensor(f"in_{k}", v.shape, mybir.dt.from_np(v.dtype), kind="ExternalInput").ap()
            for k, v in arrays.items()}
    args["xslot"] = nc.dram_tensor("xslot", (128 * NB, ROW), F32, kind="Internal").ap()
    args["yslot"] = nc.dram_tensor("yslot", (128 * NB, 1024), F32, kind="Internal").ap()
    args["out"] = nc.dram_tensor("out_T", (128, 8, 512), F32, kind="ExternalOutput").ap()
    program(nc, **args)
    r = _run(nc, [{f"in_{k}": v for k, v in arrays.items()}], core_ids=[0])
    got = r.results[0]["out_T"]
    return np.ascontiguousarray(got.transpose(2, 1, 0).reshape(1, 512, 1024))
```

```python
from contextlib import ExitStack
import math

import numpy as np
import concourse.bass as bass
from concourse import mybir

F32 = mybir.dt.float32
I32 = mybir.dt.int32
U32 = mybir.dt.uint32
F32R = mybir.dt.float32r
BF16 = mybir.dt.bfloat16
ALU = mybir.AluOpType
ACT = mybir.ActivationFunctionType
AX = mybir.AxisListType.X
EPS = 1e-6
NT = 528
RING = 3
MAGIC = 12582912.0
C1, C2, C3 = 6.28125, 0.0019350051879882812, 3.0199159819e-07
PI_IN = 3.1415925
BIG = -3.0e38

VEC = [("g_mix_pre", 8), ("b_gate", 4), ("gla_norm_g", 8), ("d_skip", 8), ("b_glu", 16), ("g_mix_post", 8),
       ("g_ffn_pre", 8), ("g_ffn_post", 8), ("c_2", 8), ("ada_b_2", 48), ("norm1_g_2", 8), ("norm2_g_2", 8),
       ("q_norm_g_2", 3), ("kv_norm_g_2", 2), ("conv_b_2", 4), ("conv_ln_g_2", 4), ("conv_ln_b_2", 4),
       ("final_norm_g_2", 8), ("conv_w_2", 124), ("a_re", 32), ("a_im", 32), ("log_step", 32), ("rb", 36)]
VOFF, _o = {}, 0
for _n, _c in VEC:
    VOFF[_n] = (_o, _c)
    _o += _c
NVEC = _o
CST = [("ident", 128), ("ones", 128), ("tril", 128), ("reset", NT), ("freq", 1), ("sign", 1), ("eps", 1), ("rev4", 4), ("rev8", 8)]
COFF, _o = {}, 0
for _n, _c in CST:
    COFF[_n] = (_o, _c)
    _o += _c
NCST = _o
PLAN = ([("k", i) for i in range(2)] + [("v", i) for i in range(4)] + [("q", i) for i in range(2)]
        + [("u", i) for i in range(4)] + [("r", i) for i in range(4)] + [("zg", i) for i in range(4)]
        + [("zs", 0), ("zs", 1)] + [("og", i) for i in range(4)])
for _j in range(4):
    PLAN += [("glua", _j), ("glub", _j)] + ([("zs", _j + 1)] if _j in (1, 2) else [])
PLAN += [("wo", i) for i in range(4)]
_a = 0
for _h in range(2):
    for _i in range(16):
        PLAN.append(("f1", 8 * _h + _i) if _i < 8 else ("f2", 8 * _h + _i - 8))
        if _i % 4 != 3:
            PLAN.append(("ada", _a))
            _a += 1
PLAN += [("cin", i) for i in range(4)] + [("lat", i) for i in range(3)]
PLAN += [("ga", i) for i in range(4)] + [("gc", i) for i in range(4)]
PLAN += [("uq", 0), ("uq", 1), ("kv", 0), ("oa", 0), ("oa", 1), ("oc", 0), ("oc", 1)] + [("wo2", i) for i in range(4)]
NU = len(PLAN)
WHOLE = ("ada",)
NB = 7
COLS = [("ex", i) for i in range(8)] + [("dn", i) for i in range(4)]
STREAM = []
for _n in range(NB):
    for _p in range(4):
        STREAM += [(_n, "ex", 2 * _p), (_n, "ex", 2 * _p + 1)]
        if _n or _p:
            STREAM.append((_n, "dn", _p - 1) if _p else (_n - 1, "dn", 3))
STREAM.append((NB - 1, "dn", 3))
ROW = 1024 + 8
MC = 128 + 2 * 12 + NB


def program(nc, W, wmoe, mcst, vecs, cst, xT, wal, wgu, bc, rw, posr, posc, xslot, yslot, out):
    ctx = ExitStack()
    with ctx:
        def sbt(name, shape, dt=F32):
            return ctx.enter_context(nc.sbuf_tensor(name, shape, dt))

        def semaphore(name):
            return ctx.enter_context(nc.semaphore(name))

        ENG = ["pe", "act", "dve", "pool", "sp"]
        sem = {e: semaphore("s_" + e) for e in ENG}
        s_ring = [semaphore(f"s_ring{i}") for i in range(RING)]
        s_gat = [semaphore(f"s_gat{i}") for i in range(RING + 3)]
        s_xs = [semaphore(f"s_xs{i}") for i in range(2)]
        s_back = [semaphore(f"s_back{i}") for i in range(4)]
        s_clear, s_scat, s_y, s_out = [semaphore("s_" + n) for n in ("clear", "scat", "y", "out")]
        queue = {e: [] for e in ENG}
        count = {e: 0 for e in ENG}

        def flat(w):
            if w is None:
                return []
            if isinstance(w, tuple):
                return [w]
            return [t for x in w for t in flat(x)]

        def emit(e, fn, w=None, inc=True):
            queue[e].append((flat(w), fn, inc))
            if inc:
                count[e] += 1
            return (sem[e], count[e])

        def now(e):
            return (sem[e], count[e])

        def step(e, fn, w=None):
            return emit(e, fn, [now(e), flat(w)])

        def act(o, i, f, w=None, **kw):
            return step("act", lambda g: g.activation(o, i, f, **kw), w)

        def tt(o, a, b, op, w=None, e="dve"):
            return step(e, lambda g: g.tensor_tensor(o, a, b, op), w)

        def ts(o, a, s1, s2, op0, op1=None, w=None, e="dve"):
            if op1 is None:
                return step(e, lambda g: g.tensor_scalar(o, a, s1, None, op0), w)
            return step(e, lambda g: g.tensor_scalar(o, a, s1, s2, op0, op1), w)

        def stt(o, a, s, b, op0, op1, w=None):
            return step("dve", lambda g: g.scalar_tensor_tensor(out=o, in0=a, scalar=s, in1=b, op0=op0, op1=op1), w)

        def cp(o, i, w=None, e="dve"):
            if e == "act":
                return act(o, i, ACT.Copy, w)
            return step(e, lambda g: g.tensor_copy(o, i), w)

        def red(o, i, op, w=None):
            return step("dve", lambda g: g.tensor_reduce(o, i, AX, op), w)

        def recip(o, i, w=None):
            return step("dve", lambda g: g.reciprocal(o, i), w)

        def zero(o, w=None, e="pool"):
            return step(e, lambda g: g.memset(o, 0.0), w)

        MUL, ADD, SUB, MAX = ALU.mult, ALU.add, ALU.subtract, ALU.max

        def mm(group, w=None):
            for n, (o, l, r, st, sp, *own) in enumerate(group):
                t = emit("pe", lambda g, o=o, l=l, r=r, st=st, sp=sp: g.matmul(
                    o, l, r, start=st, stop=sp, skip_group_check=True), [flat(w) if n == 0 else [], flat(own)],
                    n == len(group) - 1)
            return t

        def mm3(o, ls, rs, first=True, last=True, w=None):
            n = len(ls)
            out = []
            for k, ((lh, ll), (rh, rl)) in enumerate(zip(ls, rs)):
                out += [(o, lh, rh, first and k == 0, False, w[k] if w else None), (o, lh, rl, False, False),
                        (o, ll, rh, False, last and k == n - 1)]
            return out

        def tr(group, w=None):
            w = flat(w)
            for n, (o, i, idt) in enumerate(group):
                t = emit("pe", lambda g, o=o, i=i, idt=idt: g.transpose(o, i, idt), w if n == 0 else None,
                         n == len(group) - 1)
            return t

        banks = [ctx.enter_context(nc.psum_tensor(f"bank{i}", [128, 512], F32)) for i in range(8)]
        bfree = [None] * 8
        bnext = [0]

        def take():
            i = next(j % 8 for j in range(bnext[0], bnext[0] + 8) if bfree[j % 8] != "held")
            bnext[0] = i + 1
            f, bfree[i] = bfree[i], "held"
            return i, banks[i][:, :], f

        def give(i, t):
            bfree[i] = flat(t)

        ringt = sbt("ring", [128, RING, 2048])
        wst = sbt("wsplit", [128, 2, 2, 2048], F32R)
        wfree = [None, None]
        nsplit = [0]
        upos = [0]
        low = ["dve"]
        ready = {}

        def load_unit(n, w):
            s = n % RING
            emit("sp", lambda g: g.dma_start(ringt[:, s, :], W[n]).then_inc(s_ring[s], 16), w, False)

        def landed(n):
            return (s_ring[n % RING], 16 * (n // RING + 1))

        ring_read = [None] * RING

        def release(n, t):
            ring_read[n % RING] = t
            if n + RING < NU:
                load_unit(n + RING, t)

        def split_unit(n):
            z = nsplit[0] % 2
            nsplit[0] += 1
            r = ringt[:, n % RING, :]
            t = act(wst[:, z, 0, :], r, ACT.Copy, [landed(n), wfree[z]])
            t = tt(wst[:, z, 1, :], r, wst[:, z, 0, :].bitcast(F32), SUB, t, low[0])
            release(n, t)
            ready[n] = (z, t)

        def unit(name, i):
            n = upos[0]
            assert PLAN[n] == (name, i), (PLAN[n], name, i)
            upos[0] += 1
            if name in WHOLE:
                return n, ringt[:, n % RING, :], landed(n)
            if n not in ready:
                split_unit(n)
            m = n + 1
            while m < NU and PLAN[m][0] in WHOLE and m < n + RING - 1:
                m += 1
            if m < NU and PLAN[m][0] not in WHOLE and m not in ready:
                split_unit(m)
            z, t = ready[n]
            return z, wst[:, z], t

        def used(z, t):
            wfree[z] = t

        vt = sbt("vecs", [128, NVEC])
        ct = sbt("cst", [128, NCST])
        adat = sbt("adat", [128, 48])
        small = sbt("small", [128, 64])
        base = (nc.sbuf_base + 31) // 32 * 32
        ARENA = (nc.sbuf_top - base) // 32 * 8
        names = [0]

        def place(at, n, dt):
            names[0] += 1
            return nc.alloc_sbuf_tensor_at(f"a{names[0]}", [128, n], dt, offset=base + 4 * at)[:, :]

        spans = []

        def barrier():
            return [now(e) for e in ("pe", "act", "dve", "pool")]

        freed = []

        def al(*dims, dt=F32, by=("act", "dve", "pool"), top=False):
            size = int(np.prod(dims))
            n = (size + 7) // 8 * 8
            if top:
                at = ARENA - n
                for o, k in sorted(spans, reverse=True):
                    if at >= o + k:
                        break
                    at = min(at, o - n)
            else:
                at = 0
                for o, k in sorted(spans):
                    if o - at >= n:
                        break
                    at = max(at, o + k)
            assert 0 <= at and at + n <= ARENA, (n, sorted(spans))
            spans.append((at, n))
            for o, k, t in freed:
                if o < at + n and at < o + k:
                    for e in by:
                        queue[e].append((t, None, False))
            a = place(at, size, dt)
            if len(dims) == 2:
                a = a.rearrange("p (a b) -> p a b", b=dims[1])
            if len(dims) == 3:
                a = a.rearrange("p (a b c) -> p a b c", b=dims[1], c=dims[2])
            where[id(a)] = (at, n, a)
            return a

        where = {}

        def high_low(a):
            o, n, _ = where[id(a)]
            return place(o, int(np.prod(a.shape[1:])), F32R).rearrange("p (a b) -> p a b", b=a.shape[2])

        def drop(*aps, w=None, last=None):
            t = flat([last or barrier(), flat(w)])
            for a in aps:
                o, n, _ = where.pop(id(a))
                spans.remove((o, n))
                freed.append((o, n, t))

        def vec(name):
            o, n = VOFF[name]
            return vt[:, o:o + n]

        def con(name):
            o, n = COFF[name]
            return ct[:, o:o + n]

        n_ld = [0]

        def ld(o, i, w=None):
            s = semaphore(f"s_ld{n_ld[0]}")
            n_ld[0] += 1
            emit("sp", lambda g: g.dma_start(o, i).then_inc(s, 16), w, False)
            return (s, 16)

        ident, ones = con("ident"), con("ones")

        t_v = ld(vt[:, :], vecs)
        t_c = ld(ct[:, :], cst)
        HT = al(8, NT)
        t_x = [ld(HT[:, 2 * i:2 * i + 2, :], xT[:, 2 * i:2 * i + 2, :]) for i in range(4)]
        walt = al(8, 16)
        t_wal = ld(walt, wal)
        wgut = al(512)
        t_wgu = ld(wgut[0:16, :], wgu)
        for n in range(RING):
            load_unit(n, None)

        def split(pair, src, w=None, e="dve"):
            t = act(pair[0], src, ACT.Copy, w)
            return tt(pair[1], src, pair[0].bitcast(F32), SUB, t, e)

        def sum_squares(acc, src, tmp, first, w=None):
            if first:
                return act(acc, src, ACT.Square, w)
            t = act(tmp, src, ACT.Square, [flat(w), now("dve")])
            return tt(acc, acc, tmp, ADD, t)

        def over_partitions(acc, rstd, t, dim):
            act(small[:, 40:41], con("eps"), ACT.Sqrt, t_c)
            i, b, f = take()
            b = b[:, 0:acc.shape[1]]
            tm = mm([(b, ones, acc, True, True)], [t, t_c, f])
            return root(i, b, rstd, tm, dim)

        def root(i, b, rstd, tm, dim):
            t = act(rstd, b, ACT.Sqrt, [tm, t_c, now("dve")], scale=1.0 / dim, bias=con("eps"))
            give(i, t)
            return recip(rstd, rstd, t)

        def split_all(n, value, high, lower, eng=("dve", "pool")):
            t, out = [], []
            for k in range(n + 1):
                if k < n:
                    t.append(high(k, value(k)))
                if k:
                    out.append(lower(k - 1, t[k - 1], eng[(k - 1) % len(eng)]))
            return out

        def halves_of(h, l, src):
            return (lambda k, t: act(h[:, k, :], src[:, k, :], ACT.Copy, t),
                    lambda k, t, e: tt(l[:, k, :], src[:, k, :], h[:, k, :].bitcast(F32), SUB, t, e))

        def rms(src, n, acc, tmp, rstd, w, dim):
            for k in range(n):
                t = sum_squares(acc, src[:, k, :], tmp[:, k % 2, :], k == 0, w)
            return over_partitions(acc, rstd, t, dim)

        xnh, xnl = al(8, NT, dt=F32R), al(8, NT, dt=F32R)
        sq = al(4, NT)
        rst = al(NT)
        (ia, ba, _), (ib, bb, _) = take(), take()
        tp = []
        for k in range(8):
            t = act(sq[:, k % 4, :], HT[:, k, :], ACT.Square, [t_x[k // 2], tp[k - 4] if k > 3 else None])
            tp.append(mm([(ba, ones, sq[:, k % 4, 0:512], k == 0, k == 7),
                          (bb[:, 0:16], ones, sq[:, k % 4, 512:NT], k == 0, k == 7)], [t, t_c]))
        split_unit(0)
        root(ib, bb[:, 0:16], rst[:, 512:NT], tp[7], 1024)
        t_r = root(ia, ba, rst[:, 0:512], tp[7], 1024)
        g = vec("g_mix_pre")
        t_xn = split_all(8, lambda k: stt(HT[:, k, :], HT[:, k, :], g[:, k:k + 1], rst, MUL, MUL, [t_r, t_v]),
                         *halves_of(xnh, xnl, HT))
        walh, wall = al(8, 16, dt=F32R), al(8, 16, dt=F32R)
        t_wal = split((walh, wall), walt, t_wal)
        drop(HT, sq, rst, walt)

        def pairs(h, l, lo=0, hi=512, n=8):
            return [(h[:, k, lo:hi], l[:, k, lo:hi]) for k in range(n)]

        xr = pairs(xnh, xnl, 16, NT)
        halves = [(0, 264, pairs(xnh, xnl, 0, 264)), (264, NT, pairs(xnh, xnl, 264, NT))]

        def linear(name, i, evac, rhs, w, nk=8, n=2048):
            z, u, tu = unit(name, i)
            u = u[:, :, 0:n].rearrange("p a (k m) -> p a k m", k=nk)
            per = u.shape[3] // 128
            wk = w if isinstance(w, list) and len(w) == nk else None
            w = None if wk else w
            for j in range(per):
                ls = [(u[:, 0, k, j * 128:(j + 1) * 128], u[:, 1, k, j * 128:(j + 1) * 128]) for k in range(nk)]
                for part in (rhs if isinstance(rhs[0][0], int) else [(None, None, rhs)]):
                    lo, hi, r = part
                    bi, b, f = take()
                    if lo is None:
                        t = mm(mm3(b, ls, r, w=wk), [tu, w, f])
                        give(bi, evac(per * i + j, b, t))
                    else:
                        t = mm(mm3(b[:, 0:hi - lo], ls, r, w=wk), [tu, w, f])
                        give(bi, evac(per * i + j, b[:, 0:hi - lo], t, lo, hi))
            used(z, t)

        zt = al(ROW, top=True)
        t_zt = zero(zt)
        for b_ in range(NB):
            emit("sp", lambda g, b_=b_: g.dma_start(xslot[128 * b_:128 * b_ + 128, :], zt).then_inc(s_clear, 16), t_zt, False)
        drop(zt, w=(s_clear, 16 * NB))

        def reduce_angle(r, th, n, w=None):
            ts(n, th, 1.0 / (2 * math.pi), MAGIC, MUL, ADD, w)
            ts(n, n, -MAGIC, None, ADD)
            stt(r, n, -C1, th, MUL, ADD)
            stt(r, n, -C2, r, MUL, ADD)
            stt(r, n, -C3, r, MUL, ADD)
            return ts(r, r, PI_IN, -PI_IN, ALU.min, MAX)

        def sin_cos(s, c, r, w):
            act(s, r, ACT.Sin, w)
            t = act(c, r, ACT.Abs)
            t = ts(c, c, -1.0, math.pi / 2, MUL, ADD, t)
            return act(c, c, ACT.Sin, t)

        K = al(4, NT)
        LA = al(4, NT)
        PW = al(9, 2, 32)
        NPW = al(9, 32)
        L8i = al(2, 32)
        P32 = al(11, 32)
        dt_, mag, th, nn, si, co, fr, fi, q1, q2, zr = [P32[:, k, :] for k in range(11)]
        ar, ai, ls = vec("a_re"), vec("a_im"), vec("log_step")

        t_pw = []

        def ssm_parameters():
            t = act(dt_, ls, ACT.Exp, t_v)
            t = tt(mag, ar, dt_, MUL, t)
            tt(th, ai, dt_, MUL)
            tr_ = reduce_angle(q1, th, nn)
            yield
            ta = act(mag, mag, ACT.Exp, t)
            act(si, q1, ACT.Sin, tr_)
            t = act(co, q1, ACT.Abs)
            t = ts(co, co, -1.0, math.pi / 2, MUL, ADD, t)
            yield
            t = act(co, co, ACT.Sin, t)
            yield
            lr, li = PW[:, 1, 0, :], PW[:, 1, 1, :]
            step("dve", lambda g: g.memset(PW[:, 0, 0, :], 1.0))
            step("dve", lambda g: g.memset(PW[:, 0, 1, :], 0.0))
            tt(lr, mag, co, MUL, t)
            tt(li, mag, si, MUL)
            t = now("dve")
            for s in range(1, 8):
                a, b = PW[:, s, 0, :], PW[:, s, 1, :]
                tt(si, a, lr, MUL, t, "pool")
                tt(co, b, li, MUL, None, "pool")
                tt(PW[:, s + 1, 0, :], si, co, SUB, None, "pool")
                tt(si, a, li, MUL, None, "pool")
                tt(co, b, lr, MUL, None, "pool")
                tt(PW[:, s + 1, 1, :], si, co, ADD, None, "pool")
            ts(NPW, PW[:, :, 0, :], -1.0, None, MUL, None, None, "pool")
            ts(L8i[:, 0, :], PW[:, 8, 1, :], -1.0, None, MUL, None, None, "pool")
            t_pw.append(cp(L8i[:, 1, :], PW[:, 8, 1, :], None, "pool"))
            ts(zr, lr, -1.0, None, ADD)
            tt(q1, ar, ar, MUL)
            tt(q2, ai, ai, MUL)
            tt(q1, q1, q2, ADD)
            recip(nn, q1)
            tt(q1, zr, ar, MUL)
            tt(q2, li, ai, MUL)
            tt(q1, q1, q2, ADD)
            tt(fr, q1, nn, MUL)
            tt(q1, li, ar, MUL)
            tt(q2, zr, ai, MUL)
            tt(q1, q1, q2, SUB)
            tt(fi, q1, nn, MUL)
            yield

        def to_k(j, b, t, lo, hi):
            return cp(K[:, j, lo:hi], b, t, "act")

        for i in range(2):
            linear("k", i, to_k, halves, t_xn)
        alow = al(NT)
        e1 = al(4, NT)
        for lo, hi, r in halves:
            i, b, f = take()
            t = mm(mm3(b[0:16, 0:hi - lo], [(walh[:, k, :], wall[:, k, :]) for k in range(8)], r), [t_wal, f])
            t_al = cp(alow[0:16, lo:hi], b[0:16, 0:hi - lo], t)
            give(i, t_al)
        bg = vec("b_gate")

        parameters = ssm_parameters()

        def log_gate():
            for h in range(4):
                for lo, hi in ((0, 264), (264, NT)):
                    i, b, f = take()
                    b = b[:, 0:hi - lo]
                    tm = mm([(b, wgut[0:16, 128 * h:128 * h + 128], alow[0:16, lo:hi], True, True)], [t_al, t_wgu, f])
                    tb = act(e1[:, h, lo:hi], b, ACT.Abs, tm, bias=bg[:, h:h + 1])
                    give(i, ts(LA[:, h, lo:hi], b, bg[:, h:h + 1], 0.0, ADD, ALU.min, tb))
            for h in range(4):
                act(e1[:, h, :], e1[:, h, :], ACT.Exp, scale=-1.0)
            for h in range(4):
                ta = act(e1[:, h, :], e1[:, h, :], ACT.Ln, bias=1.0)
                t = tt(LA[:, h, :], LA[:, h, :], e1[:, h, :], SUB, ta)
            return t

        Q = al(4, 512)
        VV = al(4, 1024)
        VM = al(1024)
        for half in range(2):
            bb_ = [take() for _ in range(5)]
            for kg in range(2):
                z, u, tu = unit("v", 2 * half + kg)
                u = u.rearrange("p a (k m) -> p a k m", k=4)
                rs = [(u[:, 0, k, :], u[:, 1, k, :]) for k in range(4)]
                for m, (i, b, f) in enumerate(bb_):
                    lo, hi = (16 + 128 * m, 144 + 128 * m) if m < 4 else (0, 16)
                    b = b if m < 4 else b[0:16, :]
                    t = mm(mm3(b, pairs(xnh, xnl, lo, hi)[4 * kg:4 * kg + 4], rs, kg == 0, kg == 1), [tu, t_xn, f])
                    if kg == 1:
                        o = VV[:, m, 512 * half:512 * half + 512] if m < 4 else VM[0:16, 512 * half:512 * half + 512]
                        give(i, cp(o, b, t, "act"))
                used(z, t)
                if half == 0 or kg == 0:
                    next(parameters)
            if half == 0:
                t_la = log_gate()
        drop(alow, walh, wall, wgut, e1)
        U = al(8, NT)
        O = al(8, 512)
        ex = al(3, NT)
        QK = al(4, 512)
        dc = al(2, 9)
        S = al(8, 256)
        SC = al(2, 512)
        kst = al(4, 128)
        ksm = al(128)
        t_scz = zero(SC)
        reset = con("reset")
        tril = con("tril").bitcast(I32)
        d0, d1, e3 = ex[:, 0, 16:NT], ex[:, 1, :], ex[:, 2, 16:NT]
        ready_h = {}
        pe_h = {}

        def chunks(a):
            return a.rearrange("p (c t) -> p c t", t=64)

        def gla_decays(h):
            z = h % 2
            qi, ki = QK[:, 2 * z, :], QK[:, 2 * z + 1, :]
            sc = 1.0 / 16.0
            cs = LA[:, h, :]
            step("dve", lambda g: g.tensor_tensor_scan(cs, reset, cs, 0.0, MUL, ADD), [t_c, t_la, pe_h.get(h - 2)])
            cx = chunks(cs[:, 16:NT])
            td = tt(chunks(d0), cx, cx[:, :, 32:33].to_broadcast([128, 8, 64]), SUB, now("act"))
            act(qi, d0, ACT.Exp, td, scale=sc)
            act(ki, d0, ACT.Exp, scale=-sc)
            tt(chunks(d1[:, 16:NT]), cx[:, :, 63:64].to_broadcast([128, 8, 64]), cx, SUB)
            td = tt(d1[:, 0:16], cs[:, 15:16].to_broadcast([128, 16]), cs[:, 0:16], SUB)
            act(e3, cs[:, 16:NT], ACT.Exp, scale=sc)
            act(d1, d1, ACT.Exp, td, scale=sc)
            return act(dc[:, z, 1:9], cx[:, :, 63], ACT.Exp, scale=sc)

        def gla_scale(h, ta):
            z = h % 2
            qi, ki = QK[:, 2 * z, :], QK[:, 2 * z + 1, :]
            tt(qi, Q[:, h, :], qi, MUL, [ta, t_kv])
            t1 = tt(ki, K[:, h, 16:NT], ki, MUL)
            tt(Q[:, h, :], Q[:, h, :], e3, MUL)
            t2 = tt(K[:, h, :], K[:, h, :], d1, MUL)
            ready_h[h] = (t1, t2)

        def to_u(j, b, t, lo, hi):
            return cp(U[:, j, lo:hi], b, t, "act")

        t_oh = {}

        def head_norm(h):
            z = h % 2
            i, b, f = take()
            t = mm([(b, ones, QK[:, 2 * z + dv, :], dv == 0, dv == 1) for dv in range(2)], [pe_h[("s", h)], f])
            t = root(i, b, QK[:, 2 * z + 1, :], [t, now("pe")], 256)
            for dv in range(2):
                j = 2 * h + dv
                t_oh[h] = stt(O[:, j, :], O[:, j, :], vec("gla_norm_g")[:, j:j + 1], QK[:, 2 * z + 1, :], MUL, MUL, t)
            pe_h[h] = t_oh[h]

        rt = [LA[:, k, 0:512] for k in range(4)]

        def gate_r(j, b, t):
            z = j % 2
            act(rt[2 * z], b, ACT.Sigmoid, [t, rfree[z]])
            ta = cp(rt[2 * z + 1], b, None, "act")
            tt(rt[2 * z], rt[2 * z], rt[2 * z + 1], MUL, ta, "pool")
            rfree[z] = tt(O[:, j, :], O[:, j, :], rt[2 * z], MUL, t_oh[j // 2], "pool")
            return ta

        t_dec = gla_decays(0)
        next(parameters)
        for i in range(2):
            linear("q", i, lambda j, b, t: act(Q[:, j, :], b, ACT.Copy, t, scale=128.0 ** -0.5), xr, t_xn)
        t_kv = now("act")

        gla_scale(0, t_dec)
        linear("u", 0, to_u, halves, t_xn)
        for h in range(4):
            z = h % 2
            t1, t2 = ready_h[h]
            qi, ki = QK[:, 2 * z, :], QK[:, 2 * z + 1, :]
            hv = slice(256 * h, 256 * h + 256)
            i, b, f = take()
            t = mm([(b[:, 128 * m:128 * m + 128], ki[:, 128 * m:128 * m + 128], qi[:, 128 * m:128 * m + 128],
                     True, True) for m in range(4)], [t1, f])
            pe_h[h] = t
            for m in range(4):
                t_sc = step("dve", lambda g, m=m, b=b, z=z: g.copy_predicated(
                    SC[:, z, 128 * m:128 * m + 128], tril, b[:, 128 * m:128 * m + 128]), [t, t_scz, pe_h.get(("o", h - 2))])
            give(i, t_sc)
            i, b, f = take()
            t = tr([(b[:, 128 * m:128 * m + 128], K[:, h, 16 + 128 * m:144 + 128 * m], ident) for m in range(4)], [t2, f])
            give(i, cp(kst, b.rearrange("p (a m) -> p a m", a=4), [t, pe_h.get(("u", h - 1))], "act"))
            i, b, f = take()
            t = tr([(b[0:16, 0:128], K[:, h, 0:16], ident)], f)
            tk = cp(ksm[0:16, :], b[0:16, 0:128], t, "act")
            give(i, tk)
            adds = {}
            for cc in ((0,), (1, 3), (2, 4), (5, 7), (6,)):
                i, b, f = take()
                grp = []
                for n, c in enumerate(cc):
                    o = b[:, 256 * n:256 * n + 256]
                    if c == 0:
                        grp.append((o, ksm[0:16, :], VM[0:16, hv], True, True))
                    else:
                        p = slice(64 * ((c - 1) % 2), 64 * ((c - 1) % 2) + 64)
                        grp.append((o, kst[p, (c - 1) // 2, :], VV[p, (c - 1) // 2, hv], True, True))
                t = mm(grp, [tk, f])
                for n, c in enumerate(cc):
                    adds[c] = (i, b[:, 256 * n:256 * n + 256], t, c == cc[-1])
            pe_h[("u", h)] = now("pe")
            t_u = now("act")
            if h:
                head_norm(h - 1)
            if h < 3:
                linear("u", h + 1, to_u, halves, t_xn)
            else:
                rfree = [t_ga] * 2
                linear("r", 0, gate_r, xr, t_xn)
            for c in range(8):
                i, o, t, last = adds[c]
                if c == 0:
                    t_s = cp(S[:, 0, :], o, [t, pe_h.get(("o", h - 1))])
                else:
                    t_s = stt(S[:, c, :], S[:, c - 1, :], dc[:, z, c:c + 1], o, MUL, ADD, t)
                if last:
                    give(i, t_s)
            if h < 3:
                gla_scale(h + 1, gla_decays(h + 1))
                t_ga = [now("act"), now("dve")]
            outs = []
            for dv in range(2):
                i, b, f = take()
                vs = slice(256 * h + 128 * dv, 256 * h + 128 * dv + 128)
                grp = [(b[:, 128 * m:128 * m + 128], VV[:, m, vs], SC[:, z, 128 * m:128 * m + 128], m == 0, False)
                       for m in range(4)]
                grp += [(b[:, 64 * c:64 * c + 64], S[:, c, 128 * dv:128 * dv + 128], Q[:, h, 64 * c:64 * c + 64],
                         False, c == 7) for c in range(8)]
                outs.append((i, b, mm(grp, [t_sc, t_s, t2, f])))
            pe_h[("o", h)] = now("pe")
            for dv, (i, b, tm) in enumerate(outs):
                td = cp(O[:, 2 * h + dv, :], b, tm)
                give(i, td)
                sq_ = QK[:, 2 * z + dv, :]
                ta = act(sq_, O[:, 2 * h + dv, :], ACT.Square, td)
            pe_h[("s", h)] = ta
        drop(K, Q, VV, VM, ex, dc, S, SC, kst, ksm)

        BC = al(4, 512, by=("sp",))
        t_bc = ld(BC, bc)
        tkeep = al(2, 512)
        G = [al(4, 8, 32) for _ in range(2)]
        D = [[al(2, 9, 32, top=True) for _ in range(2)] for _ in range(2)]
        Pt = al(2, 288)
        KT = al(8, 128, top=True)
        t_z = [zero(a) for a in G + D[1] + D[0] + [KT]][-1]
        br, bi_, cr, ci = [BC[:, k, :].rearrange("p (g h) -> p g h", h=16) for k in range(4)]
        tw = tkeep
        ta_, tb_ = [tw[:, k, :].rearrange("p (g h) -> p g h", h=16) for k in range(2)]
        def b16(a):
            return a.unsqueeze(2).to_broadcast([128, 32, 16])

        linear("r", 1, gate_r, xr, t_xn)
        tt(ta_, br, b16(fr), MUL, [t_bc, t_pw])
        tt(tb_, bi_, b16(fi), MUL)
        tt(ta_, ta_, tb_, SUB)
        tt(tb_, br, b16(fi), MUL)
        cp(br, ta_)
        tt(ta_, bi_, b16(fr), MUL)
        t_par = tt(bi_, ta_, tb_, ADD)

        def weights_in(cb, w):
            pw = [PW[:, 7::-1, k, 4 * cb:4 * cb + 4].rearrange("p j g -> p g j").unsqueeze(3).to_broadcast([128, 4, 8, 16])
                  for k in range(2)]
            bb = [x[:, 4 * cb:4 * cb + 4, :].unsqueeze(2).to_broadcast([128, 4, 8, 16]) for x in (br, bi_)]
            t1, t2 = [tw[:, k, :].rearrange("p (g j h) -> p g j h", g=4, j=8) for k in range(2)]
            for k, (x, y, op) in enumerate(((0, 1, SUB), (1, 0, ADD))):
                tt(t1, pw[0], bb[x], MUL)
                tt(t2, pw[1], bb[y], MUL)
                for hf in range(2):
                    p = slice(64 * hf, 64 * hf + 64)
                    t = tt(G[k][p, :, :, 16 * hf:16 * hf + 16], t1[p], t2[p], op, [t_z, w])
            return t

        def weights_out(hb, d, w, e):
            def powers(a):
                return a[:, :, 2 * hb:2 * hb + 2].rearrange("p j g -> p g j").unsqueeze(3).to_broadcast([128, 2, 9, 16])

            pr, pi, npr = powers(PW[:, :, 0, :]), powers(PW[:, :, 1, :]), powers(NPW)
            c_r, c_i = [x[:, 2 * hb:2 * hb + 2, :].unsqueeze(2).to_broadcast([128, 2, 9, 16]) for x in (cr, ci)]
            tmp = Pt if e == "pool" else tw
            t1, t2 = [tmp[:, k, 0:288].rearrange("p (g j h) -> p g j h", g=2, j=9) for k in range(2)]
            for k, (x, cx, cy) in enumerate(((pr, c_r, c_i), (npr, c_i, c_r))):
                tt(t1, x, cx, MUL, t_par, e)
                tt(t2, pi, cy, MUL, None, e)
                for hf in range(2):
                    p = slice(64 * hf, 64 * hf + 64)
                    t = tt(d[k][p, :, :, 16 * hf:16 * hf + 16], t1[p], t2[p], SUB, [w, t_z], e)
            return t

        after = {"g": None, "d": None, "s": t_oh[2], "y": None}
        t_d = [weights_out(0, D[0], None, "dve"), weights_out(1, D[1], None, "pool")]
        t_g = weights_in(0, None)
        linear("r", 2, gate_r, xr, t_xn)
        SX = al(67, 2, 32)
        GT = [QK[:, k, :].rearrange("p (a m) -> p a m", a=4) for k in range(2)] + [al(4, 128) for _ in range(2)]
        US = [al(132) for _ in range(4)]
        for cb in range(8):
            bk, kb_, f = take()
            grp = []
            for q in range(4):
                o = kb_[32 * q:32 * q + 32, 0:256]
                grp += [(o, G[0][:, q, 7, :], D[q // 2][0][:, q % 2, 0:8, :], True, False),
                        (o, G[1][:, q, 7, :], D[q // 2][1][:, q % 2, 0:8, :], False, True)]
            t_kt = after["d"] = mm(grp, [t_d, t_g, f])
            for q in range(4):
                uc = U[32 * q:32 * q + 32, cb, :].rearrange("p (c f l) -> p l f c", f=2, l=4)
                for l in range(4):
                    o = US[q][32 * l:32 * l + 32, :].rearrange("p (f c) -> p f c", f=2)
                    if l % 2:
                        ta = cp(o, uc[:, l], [t_u, after["s"]], "act")
                    else:
                        td = cp(o, uc[:, l], [t_u, after["s"]])
            t_gt = []
            for q in range(4):
                bt, b, f = take()
                t = tr([(b[:, 128 * (2 * k + hf):128 * (2 * k + hf) + 128], G[k][:, q, 4 * hf:4 * hf + 4, :], ident)
                        for k in range(2) for hf in range(2)], [t_g, f])
                t_gt.append(cp(GT[q], b.rearrange("p (a m) -> p a m", a=4), [t, after["s"]], "act"))
                give(bt, t_gt[q])
            after["g"] = t
            for q in range(4):
                p = slice(32 * q, 32 * q + 32)
                tk = cp(KT[p, :, 32 * q:32 * q + 32], kb_[p, 0:256].rearrange("p (s c) -> p s c", s=8),
                        [t_kt, after["y"], t_z], "act")
            give(bk, tk)
            if cb < 7:
                t_d = [weights_out(2 * cb + 2 + k, D[k], after["d"], "pool" if cb or k else "dve") for k in range(2)]
                t_g = weights_in(cb + 1, after["g"])
            if cb == 2:
                head_norm(3)
            b0, s0, f0 = take()
            b1, s1, f1 = take()
            for q in range(4):
                t = mm([(s[:, 66 * q:66 * q + 66], GT[q][:, 2 * k + hf, :], US[q][:, 66 * hf:66 * hf + 66], hf == 0, hf == 1)
                        for k, s in ((0, s0), (1, s1)) for hf in range(2)], [ta, td, t_gt[q], f0, f1])
            after["s"] = t
            ux = U[:, cb, 16:NT].rearrange("p (c s) -> p c s", s=8)
            by, b, f = take()
            yv = b.rearrange("p (c s) -> p c s", s=8)
            after["y"] = ty = mm([(yv[:, :, s:8], KT[:, s, :], ux[:, :, 0:8 - s], s == 0, s == 7) for s in range(8)],
                                 [tk, t_u, f])
            for k, (i, s) in enumerate(((b0, s0), (b1, s1))):
                o = SX[:, 1:67, k, 4 * cb:4 * cb + 4].rearrange("p c q -> p q c")
                give(i, cp(o, s[:, 0:264].rearrange("p (q c) -> p q c", q=4), t))
            give(by, stt(U[:, cb, 16:NT], U[:, cb, 16:NT], vec("d_skip")[:, cb:cb + 1], b, MUL, ADD, [ty, ta]))
        drop(G[0], G[1], KT, P32, QK, *GT[2:], *US)
        SZ = al(8, 512, by=("act",))
        sw = [tw[:, k, 0:64].rearrange("p (a g) -> p a g", a=2) for k in range(2)]
        l8 = PW[:, 8:9, 0, :].to_broadcast([128, 2, 32])
        t_sx = now("dve")
        for c in range(1, 65):
            m0 = emit("dve", lambda g, c=c: g.tensor_tensor(sw[0], SX[:, c], l8, MUL), t_sx)
            m1 = emit("dve", lambda g, c=c: g.tensor_tensor(sw[1], SX[:, c, ::-1, :], L8i, MUL), t_sx)
            a0 = emit("dve", lambda g, c=c: g.tensor_tensor(SX[:, c + 1], SX[:, c + 1], sw[0], ADD), m0)
            t_sx = emit("dve", lambda g, c=c: g.tensor_tensor(SX[:, c + 1], SX[:, c + 1], sw[1], ADD), [a0, m1])
        dread = [after["d"], after["d"], None, None]
        tds = [[weights_out(0, D[0], dread[0], "pool")]]
        low[0] = "pool"
        linear("r", 3, gate_r, xr, t_xn)
        tds[0].append(weights_out(1, D[1], dread[1], "pool"))
        drop(LA, last=[now("act"), now("pool"), t_ga])
        t_o = now("pool")
        tds.append([])
        for i in range(4):
            linear("zg", i, lambda j, b, t: act(SZ[:, j, :], b, ACT.Sigmoid, t), xr, t_xn)
            if i == 0:
                gt = []
                for n in range(2):
                    D.append([al(2, 9, 32, by=("pool", "dve")) for _ in range(2)])
                    if n == 0:
                        gt = [al(512, by=("act", "dve")) for _ in range(2)]
                    for a in D[-1]:
                        t_z = zero(a)
            elif i < 3:
                tds[1].append(weights_out(1 + i, D[1 + i], None, "pool"))
        sgz = [al(512, by=("act",)) for _ in range(2)]
        held, free = {}, [None] * 4

        def e_z(j, b, t):
            held[j] = act(sgz[j % 4], b, ACT.Sigmoid, [t, free[j % 4]])
            return held[j]

        linear("zs", 0, e_z, xr, t_xn)
        t_zg = now("act")

        def gelu(j):
            y, x = U[:, j, 16:NT], gt[j % 2]
            t = act(x, y, ACT.Square, now("dve"))
            if j:
                gelu_end(j - 1)
            ts(x, x, 0.044715, 1.0, MUL, ADD, t)
            t = tt(x, x, y, MUL)
            t_sig.append(act(x, x, ACT.Sigmoid, t, scale=2 * math.sqrt(2 / math.pi)))

        t_sig = []

        def gelu_end(j):
            y = U[:, j, 16:NT]
            return tt(y, gt[j % 2], y, MUL, t_sig[j])

        def out_weights(cb):
            return [weights_out(hb, D[hb % 4], dread[hb % 4], "dve" if hb % 2 else "pool") for hb in (2 * cb, 2 * cb + 1)]

        for cb in range(8):
            by, b, f = take()
            yv = b.rearrange("p (c s) -> p c s", s=8)
            for half in range(2):
                d = D[(2 * cb + half) % 4]
                grp = []
                for q in (2 * half, 2 * half + 1):
                    for s in range(8):
                        o = yv[32 * q:32 * q + 32, :, s]
                        for k in range(2):
                            grp.append((o, d[k][:, q % 2, s + 1, :], SX[:, 2:66, k, 4 * cb + q], s == 0 and k == 0, k == 1))
                t = mm(grp, [tds[cb][half], t_sx, f])
                dread[(2 * cb + half) % 4] = t
            if 0 < cb < 7:
                tds.append(out_weights(cb + 1))
            give(by, tt(U[:, cb, 16:NT], U[:, cb, 16:NT], b, ADD, t))
            gelu(cb)
        gelu_end(7)
        low[0] = "dve"
        drop(*D[0], *D[1], *D[2], *D[3], Pt, SX, tkeep, PW, NPW, L8i, BC, *gt)

        sgz += [al(512, by=("act",), top=True) for _ in range(2)]
        linear("zs", 1, e_z, xr, t_xn)
        oh, ol = al(8, 512, dt=F32R, by=("act",)), high_low(O)
        t_os = split_all(8, lambda k: t_o, *halves_of(oh, ol, O))
        gh, gl = al(8, 512, dt=F32R, by=("act",)), high_low(U)[:, :, 16:NT]
        t_gelu = now("dve")
        t_gs = split_all(8, lambda k: t_gelu, *halves_of(gh, gl, U[:, :, 16:NT]))
        MX = SZ
        gsr = pairs(gh, gl)

        for i in range(4):
            linear("og", i, lambda j, b, t: tt(MX[:, j, :], b, MX[:, j, :], MUL, [t, t_zg]), pairs(oh, ol), t_os)
        drop(oh, O)
        mh, ml = al(8, 512, dt=F32R, by=("act",)), al(8, 512, dt=F32R, by=("dve",))
        tmp = al(4, 512, by=("act", "dve"))
        sg = [tmp[:, k, :] for k in range(4)]
        bgl = vec("b_glu")
        t_mx = []

        def e_a(j, b, t):
            free[j % 4] = stt(sg[j % 2], b, bgl[:, j:j + 1], sgz[j % 4], ADD, MUL, [t, held[j]])
            return free[j % 4]

        def e_b(j, b, t):
            ta = act(sg[2 + j % 2], b, ACT.Sigmoid, [t, now("dve")], bias=bgl[:, 8 + j:9 + j])
            tt(sg[j % 2], sg[j % 2], sg[2 + j % 2], MUL, ta)
            t = tt(MX[:, j, :], MX[:, j, :], sg[j % 2], ADD)
            t_mx.append(split((mh[:, j, :], ml[:, j, :]), MX[:, j, :], t))
            return ta

        for i in range(4):
            linear("glua", i, e_a, gsr, t_gs)
            linear("glub", i, e_b, gsr, t_gs)
            if i in (1, 2):
                linear("zs", i + 1, e_z, xr, t_xn)
        drop(SZ, xnh, xnl, gh, U, tmp, *sgz)
        XR = al(8, 512, by=("sp",))
        t_xr = [ld(XR[:, 4 * i:4 * i + 4, :], xT[:, 4 * i:4 * i + 4, 16:NT]) for i in range(2)]
        X = XR

        nrm = al(4, 512, by=("act", "dve"))
        rs = nrm[:, 3, :]

        def out_block(Z, j, b, t):
            t = cp(Z[:, j, :], b, t, "act")
            sum_squares(nrm[:, 2, :], Z[:, j, :], nrm[:, j % 2, :], j == 0)
            return t

        def add_norm(Z, g, w):
            t = over_partitions(nrm[:, 2, :], rs, [now("dve"), now("act")], 1024)
            i, b, f = take()
            tp = []
            for k in range(8):
                t1 = stt(Z[:, k, :], Z[:, k, :], g[:, k:k + 1], rs, MUL, MUL, [t, w])
                t2 = tt(X[:, k, :], X[:, k, :], Z[:, k, :], ADD, t1, "pool" if k % 2 else "dve")
                ta = act(nrm[:, k % 3, :], X[:, k, :], ACT.Square, [t2, tp[k - 3] if k > 2 else now("pe")])
                tp.append(mm([(b, ones, nrm[:, k % 3, :], k == 0, k == 7)], [ta, f]))
            return root(i, b, rs, tp[7], 1024)

        Z = al(8, 512, by=("act", "dve"))
        for i in range(4):
            linear("wo", i, lambda j, b, t: out_block(Z, j, b, t), pairs(mh, ml), t_mx)
        drop(mh, ml)
        t = add_norm(Z, vec("g_mix_post"), t_xr)
        hh, hl = al(8, 512, dt=F32R, by=("act",)), al(8, 512, dt=F32R, by=("dve",))
        g = vec("g_ffn_pre")
        t_r2 = t
        t_hn = split_all(8, lambda k: stt(Z[:, k, :], X[:, k, :], g[:, k:k + 1], rs, MUL, MUL, t_r2), *halves_of(hh, hl, Z))
        fh, fl = al(16, 512, dt=F32R, by=("act",)), al(16, 512, dt=F32R, by=("dve",))
        adab = al(2048, by=("dve",))
        ft = nrm
        cact = small[:, 0:8]
        ta = act(cact, vec("c_2"), ACT.Sigmoid)
        t_ca = tt(cact, cact, vec("c_2"), MUL, ta)
        ffree = [None] * 2
        pe_f = [None]

        def relu2(j, b, t):
            z = j % 2
            r, q = ft[:, 2 * z, :], ft[:, 2 * z + 1, :]
            k = j % 16
            ta = act(r, b, ACT.Relu, [t, ffree[z], pe_f[0]])
            tb = act(fh[:, k, :], r, ACT.Square)
            tt(q, r, r, MUL, ta)
            ffree[z] = tt(fl[:, k, :], q, fh[:, k, :].bitcast(F32), SUB, tb)
            return ta

        def ada_begin(n):
            q, k = PLAN[n][1] // 8, PLAN[n][1] % 8
            u, tu = ringt[:, n % RING, :], landed(n)
            if k == 0:
                t = ts(adab, u, cact[:, 0:1], None, MUL, None, [tu, t_ca, now("pe") if q else None])
            else:
                t = stt(adab, u, cact[:, k:k + 1], adab, MUL, ADD, tu)
            release(n, t)
            return t

        def ada_end(n, t):
            assert upos[0] == n
            upos[0] += 1
            q, k = PLAN[n][1] // 8, PLAN[n][1] % 8
            if k == 7:
                bi, b, f = take()
                tm = mm([(b[:, j:j + 1], adab[:, 128 * j:128 * j + 128], ones[:, 0:1], True, True) for j in range(16)], [t, f])
                give(bi, tt(adat[:, 16 * q:16 * q + 16], b[:, 0:16], vec("ada_b_2")[:, 16 * q:16 * q + 16], ADD, tm))

        for hf in range(2):
            for i in range(16):
                n = upos[0] + 1
                if PLAN[n][0] == "ada":
                    t_ada = ada_begin(n)
                if i < 8:
                    linear("f1", 8 * hf + i, relu2, pairs(hh, hl), t_hn)
                    if i == 7:
                        t_h1 = [now("act"), now("dve")]
                else:
                    c, kg = (i - 8) // 2, (i - 8) % 2
                    z, u, tu = unit("f2", 8 * hf + i - 8)
                    u = u.rearrange("p a (k m) -> p a k m", k=8)
                    if kg == 0:
                        pair = [take() for _ in range(2)]
                    for j, (bi, b, f) in enumerate(pair):
                        ls = [(u[:, 0, k, 128 * j:128 * j + 128], u[:, 1, k, 128 * j:128 * j + 128]) for k in range(8)]
                        t = mm(mm3(b, ls, pairs(fh[:, 8 * kg:8 * kg + 8], fl[:, 8 * kg:8 * kg + 8]), kg == 0, kg == 1),
                               [tu, t_h1, f])
                        if kg == 1:
                            o = Z[:, 2 * c + j, :]
                            if hf == 0:
                                give(bi, cp(o, b, [t, t_hn], "act"))
                            else:
                                t2 = tt(o, o, b, ADD, [t, now("act")])
                                give(bi, t2)
                                jj = 2 * c + j
                                sum_squares(nrm[:, 2, :], o, nrm[:, jj % 2, :], jj == 0, t2)
                    used(z, t)
                    pe_f[0] = t
                if PLAN[n][0] == "ada":
                    ada_end(n, t_ada)
        drop(hh, hl, fh, fl, adab)
        ada = [adat[:, 8 * k:8 * k + 8] for k in range(6)]

        g1, g2 = small[:, 8:16], small[:, 56:64]
        for gs, gn, sc in ((g1, "norm1_g_2", ada[1]), (g2, "norm2_g_2", ada[4])):
            ts(gs, sc, 1.0, None, ADD)
            tt(gs, gs, vec(gn), MUL)
        t_rs = add_norm(Z, vec("g_ffn_post"), None)
        drop(Z)

        def modulate(tmp, k, gs, t):
            return stt(tmp, X[:, k, :], gs[:, k:k + 1], rs, MUL, MUL, t)

        hh, hl = al(8, 512, dt=F32R, by=("act",)), al(8, 512, dt=F32R, by=("dve",))
        mt = al(8, 512, by=("dve",))
        def shifted(k, t):
            t = act(hh[:, k, :], mt[:, k, :], ACT.Identity, t, bias=ada[0][:, k:k + 1])
            return act(mt[:, k, :], mt[:, k, :], ACT.Identity, None, bias=ada[0][:, k:k + 1]) if k % 2 else t

        t_hb = split_all(
            8, lambda k: modulate(mt[:, k, :], k, g1, t_rs),
            shifted,
            lambda k, t, e: stt(hl[:, k, :], mt[:, k, :], ada[0][:, k:k + 1], hh[:, k, :].bitcast(F32), ADD, SUB, t)
            if e == "dve" else tt(hl[:, k, :], mt[:, k, :], hh[:, k, :].bitcast(F32), SUB, t, e))
        drop(mt)
        hb = pairs(hh, hl)
        LAT = al(5, 512, by=("act",), top=True)
        KP = al(2, 512, by=("dve",))
        TR = al(3, 512, by=("dve", "act"))
        CU = al(4, 542, by=("act", "pool"))
        CA = al(4, 512, by=("act", "dve"))
        kpe = al(512, by=("dve",))
        pos_f = al(516, by=("dve",), top=True)
        pint = al(516, by=("sp",), top=True)
        MKf = al(1024, by=("dve",))
        MK = MKf.bitcast(BF16).rearrange("p (m k) -> p m k", m=4)
        t_z = zero(CU[:, :, 0:30])
        pi32 = pint.bitcast(I32)
        t_pos = [ld(pi32[:, 0:512], posr), ld(pi32[:, 512:516], posc)]
        cp(pos_f, pi32, t_pos)

        def rotation():
            PR = TR[:, 2, :]
            ts(PR, pos_f[:, 0:512], con("freq"), None, MUL)
            t = reduce_angle(PR, PR, TR[:, 0, :])
            t = sin_cos(TR[:, 1, :], TR[:, 0, :], PR, t)
            t_tr = ts(TR[:, 1, :], TR[:, 1, :], con("sign"), None, MUL, None, t)
            for m in range(4):
                t_mk = ts(MK[:, m, :], pos_f[:, 0:512], pos_f[:, 512 + m:513 + m], BIG, ALU.is_gt, MUL)
            return t_tr, t_mk

        def rope(o, b, w):
            tt(KP[64:96, 0, :], b[64:96, :], TR[64:96, 0, :], MUL, [w, t_tr])
            t = tt(KP[64:96, 1, :], b[96:128, :], TR[96:128, 1, :], MUL)
            tt(o, KP[64:96, 0, :], KP[64:96, 1, :], ADD)
            return t

        def e_lat(j, b, t):
            if j < 5:
                return cp(LAT[:, j, :], b, t, "act")
            return rope(kpe[64:96, :], b, t)

        low[0] = "pool"
        def e_cin(j, b, t):
            if j < 4:
                return cp(CA[:, j, :], b, t, "act")
            o = CU[:, j - 4, 30:542]
            t = act(o, b, ACT.Sigmoid, [t, t_z])
            tt(o, o, CA[:, j - 4, :], MUL, t)
            return t

        cw = vec("conv_w_2").rearrange("p (c k) -> p c k", k=31)
        CO = CA

        def convolve(c):
            for k in range(31):
                i = CU[:, c, k:k + 512]
                if k == 0:
                    t = ts(CO[:, c, :], i, cw[:, c, 0:1], vec("conv_b_2")[:, c:c + 1], MUL, ADD)
                else:
                    t = stt(CO[:, c, :], i, cw[:, c, k:k + 1], CO[:, c, :], MUL, ADD)
            return t

        for i in range(4):
            linear("cin", i, e_cin, hb, t_hb)
            if i == 1:
                t_tr, t_mk = rotation()
            if i == 2:
                convolve(0)
        drop(pos_f, pint)
        convolve(1)
        for i in range(3):
            linear("lat", i, e_lat, hb, t_hb)
        t_kpe0 = now("dve")
        t_lat0 = now("act")

        acc = al(2, 512, by=("act",))
        sqs = [acc[:, 0, :], acc[:, 1, :], nrm[:, 0, :], nrm[:, 1, :], nrm[:, 2, :]]
        t_sq = [act(sqs[k], LAT[:, k, :], ACT.Square, t_lat0) for k in range(5)]
        GA = al(8, 512, by=("act",))

        def gates_a(i):
            linear("ga", i, lambda j, b, t: act(GA[:, j, :], b, ACT.Sigmoid, t), hb, t_hb)

        gates_a(0)
        lsum = []
        for lo, n in ((0, 3), (3, 2)):
            i, b, f = take()
            lsum.append((i, b, rs, mm([(b, ones, sqs[k], k == lo, k == lo + n - 1) for k in range(lo, lo + n)], [t_sq, f])))
        lat = {lo: (al(n, 512, dt=F32R, by=("act",)), al(n, 512, dt=F32R, by=("dve",))) for lo, n in ((3, 2), (0, 3))}
        for lo, n, name, dim in ((0, 3, "q_norm_g_2", 384), (3, 2, "kv_norm_g_2", 256)):
            gates_a(1 + lo // 3)
            t = root(*lsum[lo // 3], dim)
            t_lat = split_all(n, lambda k: stt(LAT[:, lo + k, :], LAT[:, lo + k, :], vec(name)[:, k:k + 1], rs, MUL, MUL, t),
                              *halves_of(*lat[lo], LAT[:, lo:lo + n, :]), eng=("dve",))
        drop(LAT, acc)
        for c in range(2, 4):
            t_co = convolve(c)
        gates_a(3)
        GC = al(8, 512, by=("act",))
        for i in range(4):
            linear("gc", i, lambda j, b, t: act(GC[:, j, :], b, ACT.Sigmoid, t), hb, t_hb)
        t_ga = now("act")
        low[0] = "dve"
        drop(hh, hl, CU)
        QH = al(8, 512, by=("act", "dve"))
        KH = al(8, 512, by=("act", "pool"))
        V2 = al(4, 512, by=("act",))
        cp(KH[64:96, :, :], kpe[64:96, :].unsqueeze(1).to_broadcast([32, 8, 512]), t_kpe0, "pool")
        t_kpe = now("pool")

        def e_q(h, b, t):
            ta = cp(QH[0:64, h, :], b[0:64, :], t, "act")
            return [ta, rope(QH[64:96, h, :], b, t)]

        for i in range(2):
            linear("uq", i, e_q, pairs(*lat[0], n=3), t_lat, 3, 1536)
        t_rope = now("dve")
        zkv, u, tu = unit("kv", 0)
        u = u.rearrange("p a (k m) -> p a k m", k=2)
        kvp = pairs(*lat[3], n=2)
        for h in range(8):
            i, b, f = take()
            ls = [(u[:, 0, k, 64 * h:64 * h + 64], u[:, 1, k, 64 * h:64 * h + 64]) for k in range(2)]
            t = mm(mm3(b[0:64, :], ls, kvp), [tu, t_lat, f])
            give(i, cp(KH[0:64, h, :], b[0:64, :], t, "act"))
        t_qk = [now("act"), t_rope, t_kpe]
        drop(KP, TR, kpe, *lat[0])
        QF = high_low(QH)
        ath, atl = QF[:, 0::2, :], QF[:, 1::2, :]
        PB = [[al(512, by=("dve", "act")) for _ in range(4)] for _ in range(2)]
        PT = [al(512, by=("act",)) for _ in range(4)]
        st = small[:, 16:32].rearrange("p (z c) -> p z c", z=2)
        scale = 96.0 ** -0.5
        t_pt = [None, None]
        sc, probs, t_as = {}, {}, []

        def scores(h):
            sc[h] = []
            for m in range(4):
                i, b, f = take()
                sc[h].append((i, b, mm([(b, QH[0:96, h, 128 * m:128 * m + 128], KH[0:96, h, :], True, True)], [t_qk, f])))

        def soften(h):
            z = h % 2
            probs[h] = []
            for m, (i, b, t) in enumerate(sc[h]):
                p = PB[z][m]
                t = stt(p, b, scale, MK[:, m, :], MUL, ADD, [t, t_pt[z]])
                give(i, t)
                mx, sm = st[:, z, m:m + 1], st[:, z, 4 + m:5 + m]
                red(mx, p, MAX)
                t = ts(mx, mx, -1.0, None, MUL)
                probs[h].append(act(p, p, ACT.Exp, t, bias=mx, accum_out=sm))

        def normalise(h):
            z = h % 2
            t = recip(st[:, z, 4:8], st[:, z, 4:8], probs[h][3])
            return [ts(PB[z][m], PB[z][m], st[:, z, 4 + m:5 + m], None, MUL, None, t)
                    for m in range(4)]

        def conv_out(c):
            tt(CO[:, c, :], CO[:, c, :], rs, MUL, t_cr)
            t = ts(CO[:, c, :], CO[:, c, :], vec("conv_ln_g_2")[:, c:c + 1], vec("conv_ln_b_2")[:, c:c + 1], MUL, ADD)
            ta = act(nrm[:, c % 2, :], CO[:, c, :], ACT.Sigmoid, [t, t_cs])
            return tt(CO[:, c, :], CO[:, c, :], nrm[:, c % 2, :], MUL, ta, "pool")

        scores(0)
        soften(0)
        for m in range(4):
            i, b, f = take()
            r = [(u[:, 0, k, 512:1024], u[:, 1, k, 512:1024]) for k in range(2)]
            t = mm(mm3(b, [(x[:, 128 * m:128 * m + 128], y[:, 128 * m:128 * m + 128]) for x, y in kvp], r), [f])
            t_v2 = cp(V2[:, m, :], b, t, "act")
            give(i, t_v2)
        used(zkv, t)
        im, bm, f = take()
        t_mean = mm([(bm, ones, CO[:, c, :], c == 0, c == 3) for c in range(4)], [t_co, f])
        t_pv = t_cs = None
        for h in range(8):
            z = h % 2
            t_p = normalise(h)
            if h < 7:
                scores(h + 1)
            for kb in range(4):
                i, b, f = take()
                t_pt[z] = tr([(b[:, 128 * m:128 * m + 128], PB[z][m][:, 128 * kb:128 * kb + 128], ident) for m in range(4)],
                             [t_p, f])
                t = cp(PT[kb], b, [t_pt[z], t_pv], "act")
                give(i, t)
            if h < 7:
                soften(h + 1)
            if h % 2 == 0:
                ia, ba, fa = take()
            o = ba[64 * (h % 2):64 * (h % 2) + 64, :]
            t_pv = mm([(o, V2[:, kb, 64 * h:64 * h + 64], PT[kb], kb == 0, kb == 3) for kb in range(4)], [t, t_v2, fa])
            if h % 2:
                t = act(ath[:, h // 2, :], ba, ACT.Copy, t_pv)
                t_as.append(tt(atl[:, h // 2, :], ba, ath[:, h // 2, :].bitcast(F32), SUB, t))
                give(ia, t_as[-1])
            if h == 0:
                for c in range(4):
                    t = stt(CO[:, c, :], bm, -1.0 / 512, CO[:, c, :], MUL, ADD, t_mean)
                give(im, t)
                t_sq = [act(nrm[:, c, :], CO[:, c, :], ACT.Square, t) for c in range(4)]
            elif h == 1:
                i, b, f = take()
                t = mm([(b, ones, nrm[:, c, :], c == 0, c == 3) for c in range(4)], [t_sq, f])
                t_cr = root(i, b, rs, t, 512)
            elif h < 6:
                t_cs = conv_out(h - 2)
        drop(*lat[3], KH, V2, *PB[0], *PB[1], *PT)
        cvh, cvl = al(4, 512, dt=F32R, by=("act",)), al(4, 512, dt=F32R, by=("dve",))
        t_cv = split_all(4, lambda k: t_cs, *halves_of(cvh, cvl, CO), eng=("dve",))
        mh, ml = al(8, 512, dt=F32R, by=("act",)), high_low(GA)
        for i in range(2):
            linear("oa", i, lambda j, b, t: tt(GA[:, j, :], b, GA[:, j, :], MUL, [t, t_ga]), pairs(ath, atl, n=4), t_as, 4)
        t_mx = []

        def e_yc(j, b, t):
            t1 = tt(GC[:, j, :], b, GC[:, j, :], MUL, [t, t_ga])
            t = tt(GA[:, j, :], GA[:, j, :], GC[:, j, :], ADD)
            t_mx.append(split((mh[:, j, :], ml[:, j, :]), GA[:, j, :], t))
            return t1

        for i in range(2):
            linear("oc", i, e_yc, pairs(cvh, cvl, n=4), t_cv, 4)

        def e_res(j, b, t):
            t = stt(X[:, j, :], b, ada[2][:, j:j + 1], X[:, j, :], MUL, ADD, t)
            sum_squares(nrm[:, 2, :], X[:, j, :], nrm[:, j % 2, :], j == 0, t)
            return t

        for i in range(4):
            linear("wo2", i, e_res, pairs(mh, ml), t_mx)
        t_rs = over_partitions(nrm[:, 2, :], rs, [now("dve"), now("act")], 1024)
        drop(QH, cvh, cvl, mh, GA, GC, CA, MKf)

        HB = al(8, 512, by=("dve", "act"))
        RW = al(8, 36, by=("sp",))
        MCT = al(MC, by=("sp",))
        t_rw = [ld(RW, rw), ld(MCT, mcst)]
        t_hbs = []
        for k in range(8):
            t = modulate(HB[:, k, :], k, g2, t_rs)
            t_hbs.append(act(HB[:, k, :], HB[:, k, :], ACT.Identity, t, bias=ada[3][:, k:k + 1]))
        t_hb = t_hbs[7]
        i, b, f = take()
        t = mm([(b[0:36, :], RW[:, k, :], HB[:, k, :], k == 0, k == 7, t_hbs[k]) for k in range(8)], [t_rw, f])
        LT = al(512, by=("dve",))
        t_l = cp(LT[0:36, :], b[0:36, :], t)
        give(i, t_l)
        i, b, f = take()
        t = tr([(b[:, 36 * m:36 * m + 36], LT[0:36, 128 * m:128 * m + 128], ident[0:36, 0:36]) for m in range(4)], [t_l, f])
        L = al(4, 36, by=("dve",))
        rbv = vec("rb").unsqueeze(1).to_broadcast([128, 4, 36])
        t = tt(L, b[:, 0:144].rearrange("p (m c) -> p m c", m=4), rbv, ADD, t)
        give(i, t)
        HT = al(4, ROW, by=("act", "dve"))

        def turn_tokens(m):
            for hf in range(2):
                i, b, f = take()
                t = tr([(b[:, 128 * k:128 * k + 128], HB[:, 4 * hf + k, 128 * m:128 * m + 128], ident) for k in range(4)],
                       [t_hb, f])
                t = cp(HT[:, m, 512 * hf:512 * hf + 512], b, t, "act")
                give(i, t)
            return t

        turn_tokens(0)
        LG = L[:, :, 0:4]

        def bc_(a, n):
            return a.unsqueeze(2).to_broadcast([128, 4, n])

        def first_max(oh, v, m, n, rev):
            tt(oh, v, bc_(m, n), ALU.is_equal)
            tt(oh, oh, rev.unsqueeze(1).to_broadcast([128, 4, n]), MUL)
            red(km, oh, MAX)
            return tt(oh, oh, bc_(km, n), ALU.is_equal)

        RT = al(640, by=("dve", "act"))
        ro = [0]

        def piece(*dims):
            n = int(np.prod(dims))
            a = RT[:, ro[0]:ro[0] + n]
            ro[0] += n
            if len(dims) == 2:
                a = a.rearrange("p (a b) -> p a b", b=dims[1])
            if len(dims) == 3:
                a = a.rearrange("p (a b c) -> p a b c", b=dims[1], c=dims[2])
            return a

        gm, km, sg_, gv, m1, m2, sw_ = [piece(4) for _ in range(7)]
        og_, eg = piece(4, 4), piece(4, 4)
        es, es2, exx, o1, o2, wn = [piece(4, 8) for _ in range(6)]
        tmp4 = piece(4, 8, 4)
        rk = piece(8, 4)
        nb, s4, s128 = piece(4), piece(4), piece(4)
        bgr, sl = piece(NB), piece(4)
        ixf = piece(NB, 12)
        IX = al(NB * 12 + 4, by=("dve",)).bitcast(I32)
        red(gm, LG, MAX)
        tt(eg, LG, bc_(gm, 4), SUB)
        first_max(og_, LG, gm, 4, con("rev4"))
        i, b, f = take()
        ogf = og_.rearrange("p m g -> p (m g)")
        t = mm([(b[:, 0:16], MCT[:, 0:128], ogf, True, True), (b[:, 16:32], ones, ogf, True, True)], [now("dve"), t_rw, f])
        turn_tokens(1)
        t = cp(rk, b[:, 0:32].rearrange("p (m g) -> p m g", g=4), t)
        give(i, t)
        for m in range(1, 4):
            tt(rk[:, m, :], rk[:, m, :], rk[:, 3 + m, :], ADD)
            tt(rk[:, 4 + m, :], rk[:, 4 + m, :], rk[:, 3 + m, :], ADD)
        ng = rk[:, 7, :]
        ts(nb, ng, 0.0, None, ALU.is_gt)
        for lim in (128.0, 256.0, 384.0):
            stt(nb, ng, lim, nb, ALU.is_gt, ADD)
        step("dve", lambda g: g.memset(s4[:, 0:1], 0.0))
        for q in range(3):
            tt(s4[:, q + 1:q + 2], s4[:, q:q + 1], nb[:, q:q + 1], ADD)
        blk, off, mult = MCT[:, 152:152 + NB], MCT[:, 128:140], MCT[:, 140:152]
        ts(bgr, blk, s4[:, 1:2], None, ALU.is_ge)
        for q in (2, 3):
            stt(bgr, blk, s4[:, q:q + 1], bgr, ALU.is_ge, ADD)
        tt(ixf, bgr.unsqueeze(2).to_broadcast([128, NB, 12]), mult.unsqueeze(1).to_broadcast([128, NB, 12]), MUL)
        tt(ixf, ixf, off.unsqueeze(1).to_broadcast([128, NB, 12]), ADD)
        t_ix = cp(IX[:, 4:4 + NB * 12], ixf.rearrange("p b u -> p (b u)"))
        ts(s128, s4, 128.0, None, MUL)
        tt(rk[:, 0:4, :], rk[:, 0:4, :], s128.unsqueeze(1).to_broadcast([128, 4, 4]), ADD)
        tt(rk[:, 0:4, :], rk[:, 0:4, :], og_, MUL)
        red(sl, rk[:, 0:4, :], ADD)
        cp(IX[:, 0:4], sl)
        LE = L[:, :, 4:36].rearrange("p m (g e) -> p m e g", g=4)
        tt(tmp4, LE, og_.unsqueeze(2).to_broadcast([128, 4, 8, 4]), MUL)
        red(es, tmp4, ADD)
        red(m1, es, MAX)
        t = tt(exx, es, bc_(m1, 8), SUB)
        act(eg, eg, ACT.Exp, t)
        t_e = act(exx, exx, ACT.Exp)
        turn_tokens(2)
        t_ht = turn_tokens(3)
        first_max(o1, es, m1, 8, con("rev8"))
        stt(es2, o1, BIG, es, MUL, ADD)
        red(m2, es2, MAX)
        first_max(o2, es2, m2, 8, con("rev8"))
        tt(o1, o1, o2, ADD)
        tt(wn, exx, o1, MUL, t_e)
        red(sg_, eg, ADD)
        recip(gv, sg_)
        red(sw_, wn, ADD)
        recip(sw_, sw_)
        tt(sw_, sw_, gv, MUL)
        tt(wn, wn, bc_(sw_, 8), MUL)
        t_wn = cp(HT[:, :, 1024:ROW], wn)
        XTK = al(4, 1024, by=("act",))
        ROWS = al(2, 1024, by=("act",))
        dg = al(2, 128, by=("dve",))
        dread = [None, None]

        def spread(o, v):
            for hf in range(2):
                i, b, f = take()
                for j in range(4):
                    t = ts(dg[:, j % 2, :], ident, v[:, 4 * hf + j:4 * hf + j + 1], None, MUL, None, dread[j % 2])
                    dread[j % 2] = t = mm([(b[:, 128 * j:128 * j + 128], ones, dg[:, j % 2, :], True, True)], [t, f])
                t = cp(o[:, 512 * hf:512 * hf + 512], b, t, "act")
                give(i, t)
            return t

        def turn_residual(m):
            for hf in range(2):
                i, b, f = take()
                t = tr([(b[:, 128 * k:128 * k + 128], X[:, 4 * hf + k, 128 * m:128 * m + 128], ident) for k in range(4)], f)
                t = cp(XTK[:, m, 512 * hf:512 * hf + 512], b, t, "act")
                give(i, t)
            return t

        for m in range(4):
            t_xtk = turn_residual(m)
        spread(ROWS[:, 0, :], ada[5])
        t_rows = spread(ROWS[:, 1, :], vec("final_norm_g_2"))
        drop(X, nrm, HB, LT, dg)

        def indexed(c):
            return bass.IndirectOffsetOnAxis(ap=IX[:, c:c + 1].bitcast(U32), axis=0)

        NS, NP = RING + 3, 4
        XS = al(2, ROW, by=("sp",))
        XH, XL = [al(8, 128, dt=F32R, by=("act",)) for _ in range(2)], [al(8, 128, dt=F32R, by=("dve",)) for _ in range(2)]
        w3 = [al(2, 2048, dt=F32R, by=("act", "dve")) for _ in range(NP - 2)]
        YS = al(2, 512, by=("act", "dve"))
        PD = al(2, 512, by=("act", "dve"))
        TH, TL = al(2, 256, dt=F32R, by=("act",)), al(2, 256, dt=F32R, by=("dve",))
        slots = [ringt[:, k, :] for k in range(RING)]
        sfree = ring_read + [None] * (NS - RING)
        parts = [wst[:, 0], wst[:, 1]] + w3
        pfree = wfree + [None] * (NP - 2)
        parted = {}
        NG = NB * 12

        def gather(n, w=None):
            z, (k, kind, i) = n % NS, STREAM[n]
            c = 4 + 12 * k + COLS.index((kind, i))
            emit("pool", lambda g: g.indirect_dma_start(slots[z], None, wmoe, indexed(c)).then_inc(s_gat[z], 16),
                 [t_ix, sfree[z], w], False)

        def part(n):
            z, y = n % NS, n % NP
            t = act(parts[y][:, 0, :], slots[z], ACT.Copy, [(s_gat[z], 16 * (n // NS + 1)), pfree[y]])
            t = tt(parts[y][:, 1, :], slots[z], parts[y][:, 0, :].bitcast(F32), SUB, t)
            sfree[z] = t
            parted[n] = t
            if n + NS < NG:
                gather(n + NS)

        npart = [0]

        def moe_unit(*which):
            n = mpos[0]
            assert STREAM[n] == which
            mpos[0] += 1
            while npart[0] < min(n + NP, NG):
                part(npart[0])
                npart[0] += 1
            return n % NP, parts[n % NP], parted[n]

        mpos = [0]
        for n in range(2):
            gather(n)
        for m in range(4):
            emit("pool", lambda g, m=m: g.indirect_dma_start(xslot, indexed(m), HT[:, m, :], None).then_inc(s_scat, 16),
                 [t_ht, t_wn, (s_clear, 16 * NB)], False)
        slots += [al(2048, by=("pool",)) for _ in range(NS - RING)]
        for n in range(2, NS):
            gather(n, (s_xs[0], 16))
        xread = [None, None]
        tread = [None, None]

        def load_block(n):
            z = n % 2
            emit("sp", lambda g: g.dma_start(XS[:, z, :], xslot[128 * n:128 * n + 128, :]).then_inc(s_xs[z], 16),
                 [(s_scat, 64), xread[z]], False)

        t_xt = {}

        def turn_block(n):
            z = n % 2
            for hf in range(2):
                i, b, f = take()
                t = tr([(b[:, 128 * k:128 * k + 128], XS[:, z, 512 * hf + 128 * k:512 * hf + 128 * k + 128], ident)
                        for k in range(4)], [(s_xs[z], 16 * (n // 2 + 1)), f])
                b = b.rearrange("p (k m) -> p k m", k=4)
                ta = act(XH[z][:, 4 * hf:4 * hf + 4, :], b, ACT.Copy, [t, tread[z]])
                t2 = tt(XL[z][:, 4 * hf:4 * hf + 4, :], b, XH[z][:, 4 * hf:4 * hf + 4, :].bitcast(F32), SUB, ta)
                give(i, t2)
            t_xt[n] = t2

        hfree = [None, None]
        state = {}

        def gate_up(n, p, kh):
            z = n % 2
            y, u, tu = moe_unit(n, "ex", 2 * p + kh)
            u = u.rearrange("p a (k m) -> p a k m", k=4)
            if kh == 0:
                state["g", p] = take()
            i, b, f = state["g", p]
            ls = [(XH[z][:, 4 * kh + k, :], XL[z][:, 4 * kh + k, :]) for k in range(4)]
            t = mm(mm3(b, ls, [(u[:, 0, k, :], u[:, 1, k, :]) for k in range(4)], kh == 0, kh == 1),
                   [tu, t_xt[n], f if kh == 0 else None])
            pfree[y] = t
            tread[z] = t
            if kh:
                gu = b.rearrange("p (e x m) -> p e x m", e=2, x=2)
                d = PD[:, p % 2, :].rearrange("p (x e m) -> p x e m", x=2, e=2)
                ta = act(d[:, 0], gu[:, :, 0, :], ACT.Sigmoid, [t, hfree[p % 2]])
                tt(d[:, 0], d[:, 0], gu[:, :, 0, :], MUL, ta)
                t = tt(d[:, 0], d[:, 0], gu[:, :, 1, :], MUL)
                give(i, t)
                c = XS[:, z, 1024 + 2 * p:1026 + 2 * p].unsqueeze(2).to_broadcast([128, 2, 128])
                state["h", p] = xread[z] = tt(d[:, 0], d[:, 0], c, MUL)

        def turn_hidden(p):
            z = p % 2
            i, b, f = take()
            hfree[z] = t = tr([(b[:, 128 * e:128 * e + 128], PD[:, z, 128 * e:128 * e + 128], ident) for e in range(2)],
                              [state["h", p], f])
            ta = act(TH[:, z, :], b[:, 0:256], ACT.Copy, [t, state.get(("d", p % 2))])
            state["t", p] = tt(TL[:, z, :], b[:, 0:256], TH[:, z, :].bitcast(F32), SUB, ta)
            give(i, state["t", p])

        def down(n, p):
            z = p % 2
            y, u, tu = moe_unit(n, "dn", p)
            u = u.rearrange("p a (e m) -> p a e m", e=2)
            if p == 0:
                state["y"] = [take(), take()]
            for hf, (i, b, f) in enumerate(state["y"]):
                ls = [(TH[:, z, 128 * e:128 * e + 128], TL[:, z, 128 * e:128 * e + 128]) for e in range(2)]
                cols = slice(512 * hf, 512 * hf + 512)
                t = mm(mm3(b, ls, [(u[:, 0, e, cols], u[:, 1, e, cols]) for e in range(2)], p == 0, p == 3),
                       [tu, state["t", p], f if p == 0 else None])
                if p == 3:
                    to = tt(YS[:, hf, :], b, ROWS[:, 0, cols], MUL, [t, t_rows, (s_y, 16 * n)])
                    give(i, to)
                    state["o", hf] = to
            pfree[y] = state["d", z] = t
            if p == 3:
                emit("sp", lambda g: g.dma_start(yslot[128 * n:128 * n + 128, :], YS.rearrange("p a m -> p (a m)"))
                     .then_inc(s_y, 16), [state["o", 0], state["o", 1]], False)

        load_block(0)
        load_block(1)
        turn_block(0)
        for n in range(NB):
            for p in range(4):
                gate_up(n, p, 0)
                if p:
                    turn_hidden(p - 1)
                elif n:
                    turn_hidden(3)
                gate_up(n, p, 1)
                if p:
                    down(n, p - 1)
                elif n:
                    down(n - 1, 3)
                if p == 0 and 0 < n < NB - 1:
                    load_block(n + 1)
                if p == 2 and n < NB - 1:
                    turn_block(n + 1)
        turn_hidden(3)
        down(NB - 1, 3)
        for m in range(4):
            emit("pool", lambda g, m=m: g.indirect_dma_start(HT[:, m, 0:1024], None, yslot, indexed(m)).then_inc(s_back[m], 16),
                 [(s_y, 16 * NB), (s_scat, 64)], False)
        ss = small[:, 32:40]

        def finish(m, w):
            y = HT[:, m, 0:1024]
            r = recip(ss[:, 4 + m:5 + m], ss[:, m:m + 1], w)
            t = stt(y, y, ss[:, 4 + m:5 + m], ROWS[:, 1, :], MUL, MUL, [r, t_rows])
            emit("sp", lambda g: g.dma_start(out[128 * m:128 * m + 128, :], y).then_inc(s_out, 16), t, False)

        for m in range(4):
            y = HT[:, m, 0:1024]
            t = tt(y, y, XTK[:, m, :], ADD, [(s_back[m], 16), t_xtk])
            act(XTK[:, m, :], y, ACT.Square, t, accum_out=ss[:, m:m + 1])
            t = act(ss[:, m:m + 1], ss[:, m:m + 1], ACT.Sqrt, scale=1.0 / 1024, bias=con("eps"))
            if m:
                finish(m - 1, t_sd)
            t_sd = now("act")
        finish(3, t_sd)
        emit("sp", None, [(s_out, 64)], False)
        assert upos[0] == NU

        block = ctx.enter_context(nc.Block())

        def play(e, g):
            seen = {}
            for w, fn, inc in queue[e]:
                for s, v in w:
                    if v > seen.get(s.name, 0):
                        g.wait_ge(s, v)
                        seen[s.name] = v
                if fn is not None:
                    ins = fn(g)
                    if inc:
                        ins.then_inc(sem[e], 1)

        @block.tensor
        def _(g):
            play("pe", g)

        @block.scalar
        def _(g):
            play("act", g)

        @block.vector
        def _(g):
            play("dve", g)

        @block.gpsimd
        def _(g):
            play("pool", g)

        @block.sync
        def _(g):
            play("sp", g)


def lay(w, n):
    K, N = w.shape
    return w.reshape(K // 128, 128, N // n, n).transpose(2, 1, 0, 3).reshape(N // n, 128, K // 128 * n)


def constants():
    c = {}
    c["ident"] = np.eye(128)
    c["ones"] = np.ones((128, 128))
    j, i = np.arange(128)[:, None], np.arange(128)[None, :]
    c["tril"] = (j // 64 == i // 64) & (j <= i)
    t = np.arange(NT)
    c["reset"] = np.broadcast_to(((t != 0) & ((t < 16) | ((t - 16) % 64 != 0))), (128, NT))
    p = np.arange(128)
    freq = np.float32(10000.0) ** (-np.arange(0, 32, 2, dtype=np.float32) / np.float32(32))
    c["freq"] = freq[p % 16][:, None]
    c["sign"] = np.where(p % 32 < 16, -1.0, 1.0)[:, None]
    c["eps"] = np.full((128, 1), EPS)
    c["rev4"] = np.broadcast_to(np.arange(4, 0, -1), (128, 4))
    c["rev8"] = np.broadcast_to(np.arange(8, 0, -1), (128, 8))
    m = np.zeros((128, MC))
    m[:, 0:128] = j < i
    for n, (kind, q) in enumerate(COLS):
        m[:, 128 + n] = (q if kind == "ex" else 32 + q) * 128 + p
        m[:, 140 + n] = 1024 if kind == "ex" else 512
    m[:, 152:] = np.arange(NB)
    return np.concatenate([c[n] for n, _ in CST], axis=1).astype(np.float32), m.astype(np.float32)


def layout(a):
    def col(v):
        v = v.reshape(-1)
        return v.reshape(-1, 128).T

    w = a["w_in"][0]
    parts = {
        "u": lay(w[:, 3088:4112], 256), "k": lay(w[:, 512:1024], 256), "q": lay(w[:, 0:512], 256),
        "v": np.stack([w[512 * kg:512 * kg + 512, 1024 + 512 * hf:1536 + 512 * hf].reshape(4, 128, 512)
                       .transpose(1, 0, 2).reshape(128, 2048) for hf in range(2) for kg in range(2)]),
        "r": lay(w[:, 2048:3072], 256), "zg": lay(w[:, 4112:5136], 256), "zs": lay(w[:, 5136:6160], 256),
        "og": lay(a["w_o_gla"][0], 256),
        "glua": lay(a["w_glu"][0][:, 0:1024], 256), "glub": lay(a["w_glu"][0][:, 1024:2048], 256),
        "wo": lay(a["w_out"][0], 256), "f1": lay(a["w_ff1"][0], 256),
        "f2": a["w_ff2"][0].reshape(2, 2, 8, 128, 4, 256)
        .transpose(0, 4, 1, 3, 2, 5).reshape(16, 128, 2048),
        "ada": a["ada_w_2"][0].reshape(8, 128, 3, 2048).transpose(2, 0, 1, 3).reshape(24, 128, 2048),
    }
    w = a["w_in_2"][0]
    kr = w[:, 640:672]
    ks = np.concatenate([kr[:, 16:32], kr[:, 0:16]], axis=1)
    parts["lat"] = lay(np.concatenate([w[:, 0:640], kr, ks, kr, ks], axis=1), 256)
    parts["cin"] = lay(w[:, 672:1696], 256)
    parts["ga"], parts["gc"] = lay(w[:, 1696:2720], 256), lay(w[:, 2720:3744], 256)
    kv = a["w_ukv_2"][0].reshape(256, 8, 128)
    parts["kv"] = lay(np.concatenate([kv[:, :, 0:64].reshape(256, 512), kv[:, :, 64:128].reshape(256, 512)], axis=1), 1024)
    parts["oa"], parts["oc"] = lay(a["w_o_attn_2"][0], 512), lay(a["w_conv_out_2"][0], 512)
    parts["wo2"] = lay(a["w_out_2"][0], 256)
    e = np.stack([a[n][0].reshape(4, 4, 2, 2, 4, 128, 128) for n in ("expert_w_gate_2", "expert_w_up_2")])
    ex = e.transpose(1, 2, 4, 6, 5, 3, 0, 7).reshape(4096, 2048)
    dn = a["expert_w_down_2"][0].reshape(16, 2, 128, 1024).transpose(0, 2, 1, 3).reshape(2048, 2048)
    q = a["w_uq_2"][0].reshape(384, 8, 96)
    q = lay(np.concatenate([q, q[:, :, 80:96], q[:, :, 64:80]], axis=2).reshape(384, 1024), 512)
    parts["uq"] = np.concatenate([q, np.zeros((2, 128, 512), np.float32)], axis=2)
    W = np.stack([parts[n][i] for n, i in PLAN])

    two = lambda v: v.reshape(32, 128).T
    v = {n: col(a[n]) for n, _ in VEC if n in a and n not in ("a_re", "a_im", "log_step", "conv_w_2")}
    v["conv_w_2"] = a["conv_w_2"][0].reshape(31, 4, 128).transpose(2, 1, 0).reshape(128, 124)
    v["a_re"], v["a_im"] = two(a["a_re"][0]), two(a["a_im"][0])
    v["log_step"] = two(np.broadcast_to(a["log_step"][0][:, None], (64, 64)))
    rb = np.concatenate([a["router_group_b_2"][0], a["router_expert_b_2"][0]])
    v["rb"] = np.broadcast_to(rb, (128, 36))
    vecs = np.concatenate([v[n] for n, _ in VEC], axis=1)
    cst, mcst = constants()
    b3 = lambda t: t.reshape(32, 128, 16).transpose(1, 0, 2).reshape(128, 512)
    c3 = lambda t: b3(t.transpose(0, 2, 1))
    bc = np.stack([b3(a["b_re"][0]), b3(a["b_im"][0]), c3(a["c_re"][0]), c3(a["c_im"][0])], axis=1)
    xT = np.concatenate([a["meta_tokens"], a["x"][0]], axis=0).T.reshape(8, 128, NT).transpose(1, 0, 2)
    rw = np.concatenate([a["router_group_w_2"][0], a["router_expert_w_2"][0]], axis=1)
    pos = a["positions_2"].reshape(512)
    three = lambda w: w.reshape(-1, 128, w.shape[1]).transpose(1, 0, 2)
    return {"W": W, "wmoe": np.concatenate([ex, dn]), "mcst": mcst, "vecs": vecs, "cst": cst, "xT": xT, "wal": three(a["w_in"][0][:, 3072:3088]),
            "wgu": a["w_gate_up"][0], "bc": bc, "rw": three(rw),
            "posr": np.broadcast_to(pos, (128, 512)), "posc": pos.reshape(4, 128).T}


def kernel(**inputs):
    import concourse.bacc as _bacc
    from concourse.bass_utils import run_bass_kernel_spmd as _run

    arrays = {k: np.ascontiguousarray(v) for k, v in layout({k: np.asarray(v) for k, v in inputs.items()}).items()}
    nc = _bacc.Bacc("TRN2", target_bir_lowering=False, num_devices=1)
    args = {k: nc.dram_tensor(f"in_{k}", v.shape, mybir.dt.from_np(v.dtype), kind="ExternalInput").ap()
            for k, v in arrays.items()}
    args["xslot"] = nc.dram_tensor("xslot", (128 * NB, ROW), F32, kind="Internal").ap()
    args["yslot"] = nc.dram_tensor("yslot", (128 * NB, 1024), F32, kind="Internal").ap()
    args["out"] = nc.dram_tensor("out_y", (512, 1024), F32, kind="ExternalOutput").ap()
    program(nc, **args)
    r = _run(nc, [{f"in_{k}": v for k, v in arrays.items()}], core_ids=[0])
    return np.ascontiguousarray(r.results[0]["out_y"].reshape(1, 512, 1024))
```
